# Optimizing a Trainium2 kernel written in Bass

```python
import math
import jax
import jax.numpy as jnp
from jax import lax
import numpy as np

D_MODEL = 1024
BATCH = 1
SEQ = 1024
DEPTH = 2

CHUNK = 64
N_A_LAYERS = DEPTH // 2
N_B_LAYERS = DEPTH - N_A_LAYERS
HEAD_DIM = 64
MEM_TOKENS = 256
MEM_HEADS = 4
MEM_WIDTH = MEM_HEADS * HEAD_DIM
MIX_WIDTH = D_MODEL
LRU_WIDTH = MIX_WIDTH - MEM_WIDTH
RG_BLOCKS = 8
RG_BLOCK_WIDTH = LRU_WIDTH // RG_BLOCKS
CONV_WIDTH = 4
RG_C = 8.0
SWA_HEADS = LRU_WIDTH // HEAD_DIM
SWA_KV_HEADS = 4
SWA_GROUP = SWA_HEADS // SWA_KV_HEADS
SWA_Q_WIDTH = SWA_HEADS * HEAD_DIM
SWA_KV_WIDTH = SWA_KV_HEADS * HEAD_DIM
WINDOW = 128
WINDOW_CHUNKS = WINDOW // CHUNK
BAND = WINDOW_CHUNKS * CHUNK
D_FF = 4 * D_MODEL
N_BUCKETS = 32
MAX_DISTANCE = 128
EPS = 1e-6
NEG_INF = -1e30

kernel_name = 'yoco_rglru_swa_sink_hybrid'

def _rmsnorm(x, g):
    xf = x.astype(jnp.float32)
    y = xf * lax.rsqrt(jnp.mean(jnp.square(xf), axis=-1, keepdims=True) + EPS)
    return (y * g.astype(jnp.float32)).astype(x.dtype)

def _t5_buckets():
    i = np.arange(CHUNK)[:, None]
    j = np.arange(BAND)[None, :]
    rel = j - (WINDOW_CHUNKS - 1) * CHUNK - i
    n = -rel
    half = N_BUCKETS // 2
    ret = (n < 0).astype(np.int32) * half
    n = np.abs(n)
    max_exact = half // 2
    large = max_exact + (np.log(np.maximum(n, 1) / max_exact) / np.log(MAX_DISTANCE / max_exact) * (half - max_exact)).astype(np.int32)
    large = np.minimum(large, half - 1)
    return (ret + np.where(n < max_exact, n, large)).astype(np.int32)

def _rglru_branch(xr, conv_w, conv_b, gx_w, gx_b, ga_w, ga_b, lam):
    B, S, _ = xr.shape
    xc = lax.conv_general_dilated(xr, conv_w[:, None, :].astype(xr.dtype), window_strides=(1,), padding=[(CONV_WIDTH - 1, 0)], dimension_numbers=('NWC', 'WIO', 'NWC'), feature_group_count=LRU_WIDTH) + conv_b
    xb = xc.reshape(B, S, RG_BLOCKS, RG_BLOCK_WIDTH)
    gate_x = jax.nn.sigmoid((jnp.einsum('bsnh,nhk->bsnk', xb, gx_w).reshape(B, S, LRU_WIDTH) + gx_b).astype(jnp.float32))
    gate_a = jax.nn.sigmoid((jnp.einsum('bsnh,nhk->bsnk', xb, ga_w).reshape(B, S, LRU_WIDTH) + ga_b).astype(jnp.float32))
    log_a = -RG_C * gate_a * jax.nn.softplus(-lam.astype(jnp.float32))
    a = jnp.exp(log_a)
    b = jnp.sqrt(-jnp.expm1(2.0 * log_a)) * gate_x * xc.astype(jnp.float32)

    def combine(left, right):
        return (left[0] * right[0], right[0] * left[1] + right[1])

    _, h = lax.associative_scan(combine, (a, b), axis=1)
    return h.astype(xr.dtype)

def _memory_attention(q, mk, mv):
    B, S, _ = q.shape
    q = q.reshape(B, S, MEM_HEADS, HEAD_DIM)
    s = jnp.einsum('bshd,bmhd->bhsm', q, mk).astype(jnp.float32) * (HEAD_DIM ** -0.5)
    p = jax.nn.softmax(s, axis=-1)
    out = jnp.einsum('bhsm,bmhd->bshd', p.astype(mv.dtype), mv)
    return out.reshape(B, S, MEM_WIDTH)

def _sliding_window_attention(q, k, v, sinks, pos_bias):
    B, S, _ = q.shape
    n_chunks = S // CHUNK
    q = q.reshape(B, n_chunks, CHUNK, SWA_KV_HEADS, SWA_GROUP, HEAD_DIM)
    pad = (WINDOW_CHUNKS - 1) * CHUNK

    def band(t):
        tp = jnp.pad(t, ((0, 0), (pad, 0), (0, 0), (0, 0))).reshape(B, n_chunks + WINDOW_CHUNKS - 1, CHUNK, SWA_KV_HEADS, HEAD_DIM)
        return jnp.concatenate([tp[:, w:w + n_chunks] for w in range(WINDOW_CHUNKS)], axis=2)

    kb = band(k)
    vb = band(v)
    s = jnp.einsum('bcikgd,bcjkd->bckgij', q, kb).astype(jnp.float32) * (HEAD_DIM ** -0.5)
    s = s + pos_bias
    key_chunk = jnp.arange(n_chunks)[:, None] - (WINDOW_CHUNKS - 1) + jnp.arange(BAND)[None, :] // CHUNK
    valid = (key_chunk >= 0)[None, :, None, None, None, :]
    s = jnp.where(valid, s, NEG_INF)
    sink = sinks.astype(jnp.float32).reshape(1, 1, SWA_KV_HEADS, SWA_GROUP, 1, 1)
    m = jnp.maximum(jnp.max(s, axis=-1, keepdims=True), sink)
    p = jnp.exp(s - m)
    probs = p / (jnp.sum(p, axis=-1, keepdims=True) + jnp.exp(sink - m))
    out = jnp.einsum('bckgij,bcjkd->bcikgd', probs.astype(vb.dtype), vb)
    return out.reshape(B, S, SWA_Q_WIDTH)

def setup_inputs(seed: int = 0) -> dict:
    key = jax.random.key(seed)
    ks = jax.random.split(key, 24)

    def nrm(k, shape, scale):
        return jax.random.normal(k, shape, jnp.float32) * scale

    u = jax.random.uniform(ks[16], (N_A_LAYERS, LRU_WIDTH), jnp.float32, minval=0.9, maxval=0.999)
    s = u ** (1.0 / RG_C)
    a_lambda = jnp.log(s) - jnp.log1p(-s)
    return {
        'x': nrm(ks[0], (BATCH, SEQ, D_MODEL), 1.0),
        'mem': nrm(ks[1], (BATCH, MEM_TOKENS, D_MODEL), 1.0),
        'mem_norm_g': 1.0 + nrm(ks[2], (D_MODEL,), 0.02),
        'mix_norm_g': 1.0 + nrm(ks[3], (DEPTH, D_MODEL), 0.02),
        'mlp_norm_g': 1.0 + nrm(ks[4], (DEPTH, D_MODEL), 0.02),
        'w_mem_kv': nrm(ks[5], (DEPTH, D_MODEL, 2 * MEM_WIDTH), D_MODEL ** -0.5),
        'w_out': nrm(ks[6], (DEPTH, MIX_WIDTH, D_MODEL), 0.5 * MIX_WIDTH ** -0.5),
        'w1': nrm(ks[7], (DEPTH, D_MODEL, D_FF), D_MODEL ** -0.5),
        'w2': nrm(ks[8], (DEPTH, D_FF, D_MODEL), 0.5 * D_FF ** -0.5),
        'a_w_in': nrm(ks[9], (N_A_LAYERS, D_MODEL, 2 * LRU_WIDTH + MEM_WIDTH), D_MODEL ** -0.5),
        'a_conv_w': nrm(ks[10], (N_A_LAYERS, CONV_WIDTH, LRU_WIDTH), CONV_WIDTH ** -0.5),
        'a_conv_b': nrm(ks[11], (N_A_LAYERS, LRU_WIDTH), 0.02),
        'a_gx_w': nrm(ks[12], (N_A_LAYERS, RG_BLOCKS, RG_BLOCK_WIDTH, RG_BLOCK_WIDTH), RG_BLOCK_WIDTH ** -0.5),
        'a_gx_b': nrm(ks[13], (N_A_LAYERS, LRU_WIDTH), 0.02),
        'a_ga_w': nrm(ks[14], (N_A_LAYERS, RG_BLOCKS, RG_BLOCK_WIDTH, RG_BLOCK_WIDTH), RG_BLOCK_WIDTH ** -0.5),
        'a_ga_b': nrm(ks[15], (N_A_LAYERS, LRU_WIDTH), 0.02),
        'a_lambda': a_lambda,
        'kv_norm_g': 1.0 + nrm(ks[17], (D_MODEL,), 0.02),
        'w_kv_shared': nrm(ks[18], (D_MODEL, 2 * SWA_KV_WIDTH), D_MODEL ** -0.5),
        'b_w_in': nrm(ks[19], (N_B_LAYERS, D_MODEL, SWA_Q_WIDTH + MEM_WIDTH), D_MODEL ** -0.5),
        'b_sinks': nrm(ks[20], (N_B_LAYERS, SWA_HEADS), 0.5),
        'rel_bias': nrm(ks[21], (N_BUCKETS, SWA_HEADS), 0.5),
        'final_norm_g': 1.0 + nrm(ks[22], (D_MODEL,), 0.02),
    }

def reference(x, mem, mem_norm_g, mix_norm_g, mlp_norm_g, w_mem_kv, w_out, w1, w2, a_w_in, a_conv_w, a_conv_b, a_gx_w, a_gx_b, a_ga_w, a_ga_b, a_lambda, kv_norm_g, w_kv_shared, b_w_in, b_sinks, rel_bias, final_norm_g):
    B, S, _ = x.shape
    M = mem.shape[1]
    mem_n = _rmsnorm(mem, mem_norm_g)
    pos_bias = jnp.transpose(rel_bias[_t5_buckets()].astype(jnp.float32), (2, 0, 1)).reshape(SWA_KV_HEADS, SWA_GROUP, CHUNK, BAND)
    shared_k = None
    shared_v = None
    for layer in range(DEPTH):
        h = _rmsnorm(x, mix_norm_g[layer])
        mkv = mem_n @ w_mem_kv[layer]
        mk = mkv[..., :MEM_WIDTH].reshape(B, M, MEM_HEADS, HEAD_DIM)
        mv = mkv[..., MEM_WIDTH:].reshape(B, M, MEM_HEADS, HEAD_DIM)
        if layer < N_A_LAYERS:
            proj = h @ a_w_in[layer]
            gate = proj[..., :LRU_WIDTH]
            xr = proj[..., LRU_WIDTH:2 * LRU_WIDTH]
            qm = proj[..., 2 * LRU_WIDTH:]
            y = jax.nn.gelu(gate) * _rglru_branch(xr, a_conv_w[layer], a_conv_b[layer], a_gx_w[layer], a_gx_b[layer], a_ga_w[layer], a_ga_b[layer], a_lambda[layer])
        else:
            j = layer - N_A_LAYERS
            if layer == N_A_LAYERS:
                kv = _rmsnorm(x, kv_norm_g) @ w_kv_shared
                shared_k = kv[..., :SWA_KV_WIDTH].reshape(B, S, SWA_KV_HEADS, HEAD_DIM)
                shared_v = kv[..., SWA_KV_WIDTH:].reshape(B, S, SWA_KV_HEADS, HEAD_DIM)
            proj = h @ b_w_in[j]
            qs = proj[..., :SWA_Q_WIDTH]
            qm = proj[..., SWA_Q_WIDTH:]
            y = _sliding_window_attention(qs, shared_k, shared_v, b_sinks[j], pos_bias)
        y_mem = _memory_attention(qm, mk, mv)
        x = x + jnp.concatenate([y, y_mem], axis=-1) @ w_out[layer]
        h = _rmsnorm(x, mlp_norm_g[layer])
        x = x + jnp.square(jax.nn.relu(h @ w1[layer])) @ w2[layer]
    return _rmsnorm(x, final_norm_g)


_drawn_inputs = setup_inputs


def setup_inputs(seed=0):
    import zlib

    import numpy as np

    out = dict(_drawn_inputs(seed))
    spreads = {}
    factors = {'mem_norm_g': 8.0,
     'mix_norm_g': 8.0,
     'mlp_norm_g': 3.523,
     'a_gx_b': 8.0,
     'a_ga_b': 8.0,
     'kv_norm_g': 21.599,
     'b_sinks': 200.0,
     'final_norm_g': 22.485,
     'rel_bias': 6.147}
    for name, (base, spread) in spreads.items():
        noise = np.random.default_rng([zlib.crc32(name.encode()), seed]).standard_normal(out[name].shape)
        drawn = base * np.exp(spread * noise) if base else spread * noise
        out[name] = jnp.asarray(drawn.astype(out[name].dtype))
    for name, factor in factors.items():
        out[name] = (out[name] * factor).astype(out[name].dtype)
    return out
```

```python
import numpy as np
import concourse.bass as bass
from concourse import mybir
from concourse.alu_op_type import AluOpType as ALU
from contextlib import ExitStack

D, S, P, HALF = 1024, 1024, 128, 512
KT = D // P
HEAD, MEM, CHUNK = 64, 256, 64
LRU, LT = 768, 6
GB = 96
FF, GF = 4096, 4
GROUPS = FF // P // GF
EPS = 1e-6
NEG = -1e30
SCALE = HEAD ** -0.5
GELU_A, GELU_C = 0.044715, float(np.sqrt(2.0 / np.pi))
PAIRS = [(0, 3), (1, 4), (2, 5), (6, 9), (7, 10), (8, 11)]
GATE_K = [(0, 1), (0, 1, 2), (1, 2)]
REL = 2 * CHUNK + CHUNK - 1

A_ORDER = ([("mem", i) for i in range(4)] + [("xr", 0), ("xr", 1), ("xr", 2), ("qm", 0), ("G", 0), ("qm", 1), ("G", 1),
           ("xr", 3), ("G", 2), ("xr", 4), ("xr", 5), ("G", 3), ("gate", 0), ("G", 4), ("gate", 1), ("G", 5)]
           + [("gate", j) for j in range(2, 6)])
B_ORDER = ([("q", i) for i in range(6)] + [("qm", 0), ("qm", 1)] + [("mem", i) for i in range(4)]
           + [("K", 0), ("K", 1), ("V", 0), ("V", 1)])
MLP_ORDER = [x for g in range(GROUPS) for x in [("w1", 4 * g + i) for i in range(4)] + [("w2", 4 * g + i) for i in range(4)]]
ORDER = ([(0, *x) for x in A_ORDER] + [(0, "wout", n) for n in range(8)] + [(0, *x) for x in MLP_ORDER]
         + [(1, *x) for x in B_ORDER] + [(1, "wout", n) for n in range(8)] + [(1, *x) for x in MLP_ORDER])
NBANKS = {"mem": 1, "G": 4, "w2": 4}
UNIT, BANK, LAST = {}, {}, []
_b = 0
for _u, _key in enumerate(ORDER):
    UNIT[_key], BANK[_key] = _u, _b
    _b += NBANKS.get(_key[1], 2)
    LAST.append(_b)
NU, NB = len(ORDER), _b
for (_l, _k, _i), _u in UNIT.items():
    if _k == "V" and _i == 0 or _k == "mem" and _i == 2:
        LAST[_u] = LAST[_u + 1]
EMPTIED = []
_n = [0, 0]
for _key in ORDER:
    for _ in range(NBANKS.get(_key[1], 2)):
        _a = int(_key[1] == "G")
        _n[_a] += 1
        EMPTIED.append((_a, _n[_a]))


def trunk(nc, xT, memT, gains, cols, sinkc, relb, onehot, wst, rep, outT):
    f32, f32r = mybir.dt.float32, mybir.dt.float32r
    ACT, AX = mybir.ActivationFunctionType, mybir.AxisListType
    V, A, T, G = nc.vector, nc.scalar, nc.tensor, nc.gpsimd
    ctx = ExitStack()
    with ctx:
        def sb(name, shape, dt=f32):
            return ctx.enter_context(nc.sbuf_tensor(name, shape, dt))

        def sem(name):
            return ctx.enter_context(nc.semaphore(name))

        X = sb("X", [P, KT, S])
        Hh, Hl = sb("Hh", [P, KT * S], f32r), sb("Hl", [P, KT * S], f32r)
        raw = sb("raw", [P, 2, 1024])
        wh, wl = sb("wh", [P, 2, 1024], f32r), sb("wl", [P, 2, 1024], f32r)
        Rh, Rl = sb("Rh", [P, 4 * S], f32r), sb("Rl", [P, 4 * S], f32r)
        Q = sb("Q", [P, 8, S])
        XR = sb("XR", [P, 3 + S])
        mkh, mkl = sb("mkh", [P, 2, 512], f32r), sb("mkl", [P, 2, 512], f32r)
        mvh, mvl = sb("mvh", [P, 2, 256], f32r), sb("mvl", [P, 2, 256], f32r)
        rstd = sb("rstd", [P, S])
        tmp = sb("tmp", [P, 3, 1024])
        ident, ones = sb("ident", [P, P]), sb("ones", [P, P])
        gain = sb("gain", [P, 7, KT])
        col = sb("col", [P, 8, LT])
        sink = sb("sink", [P, 6])
        nrm = sb("nrm", [P, 5, 10])
        sp = sb("sp", [P, 8, LT])
        stat = sb("stat", [P, 2, 5, 4])
        zero = sb("zero", [P, 1])
        relsb = sb("relsb", [32, 12])
        onesb = Q[0:32, 0, 0:REL]
        toep = Q[0:12, 1, 0:REL]
        rx = XR[:, 3:3 + S].rearrange("p (a t) -> p a t", a=2)
        memraw = tmp[:, 0:2, :].rearrange("p a t -> p (a t)")
        bias = XR[:, 0:768].rearrange("p (a j) -> p a j", a=6)

        bank = [ctx.enter_context(nc.psum_tensor(f"bank{i}", [P, HALF], f32)) for i in range(8)]
        pS, pT, pO = bank[4:6], bank[6], bank[7]

        consts_loaded, mem_loaded, x_loaded, out_written = sem("consts_loaded"), sem("mem_loaded"), sem("x_loaded"), sem("out_written")
        consts_made, zeros_made = sem("consts_made"), sem("zeros_made")
        raw_loaded = [sem("raw_loaded0"), sem("raw_loaded1")]
        unit_hi, unit_split = sem("unit_hi"), sem("unit_split")
        bank_done = sem("bank_done")
        emptied = [sem("emptied_vector"), sem("emptied_scalar")]
        dve_own, act_own = sem("dve_own"), sem("act_own")
        ssq_mem, colsum_done, var_ready, std_ready, diag_ready, bcast_done = (
            sem(n) for n in ("ssq_mem", "colsum_done", "var_ready", "std_ready", "diag_ready", "bcast_done"))
        x_squared, sq_added = sem("x_squared"), sem("sq_added")
        h_hi, h_ready = sem("h_hi"), sem("h_ready")
        mem_normed, mem_hi, mem_ready = sem("mem_normed"), sem("mem_hi"), sem("mem_ready")
        mkv_hi = sem("mkv_hi")
        lam_exp, conv_seeded, conv_ready, conv_hi, conv_split = (
            sem(n) for n in ("lam_exp", "conv_seeded", "conv_ready", "conv_hi", "conv_split"))
        sp_ready = sem("sp_ready")
        decay_tanh, decay_half, decay_sqrt, lru_done = sem("decay_tanh"), sem("decay_half"), sem("decay_sqrt"), sem("lru_done")
        gate_squared, gate_inner, gate_tanh, y_done = (
            sem(n) for n in ("gate_squared", "gate_inner", "gate_tanh", "y_done"))
        toep_done, toep_copied, toep_written, bias_loaded = (sem(n) for n in ("toep_done", "toep_copied", "toep_written", "bias_loaded"))
        kv_hi, kv_split, v2_made = sem("kv_hi"), sem("kv_split"), sem("v2_made")
        q_hi, q_split, score_done, max_ready, exp_done, prob_ready, turned, turned_hi, turned_split, pv_done, att_out = (
            sem(n) for n in ("q_hi", "q_split", "score_done", "max_ready", "exp_done", "prob_ready", "turned",
                             "turned_hi", "turned_split", "pv_done", "att_out"))
        relu_squared, hid_hi, hid_split = sem("relu_squared"), sem("hid_hi"), sem("hid_split")
        final_ready = sem("final_ready")
        block = ctx.enter_context(nc.Block())

        def hb(k, lo, n):
            return slice(k * S + lo, k * S + lo + n)

        TOK, MEMC = slice(0, 8), slice(8, 10)

        def raw32(ap):
            return ap.bitcast(f32)

        V2 = 0
        QS = 2048
        PT = 4096
        QB = 5120
        NMEM, NSWA = 16, 24
        STEP0 = [0, NMEM]
        def steps(layer):
            out = [("mem", i // 8, i % 8) for i in range(NMEM)]
            if layer:
                out += [("swa", i // 4, i % 4) for i in range(NSWA)]
            return out
        N_MEM0, N_MIX0, N_MLP0, N_MIX1, N_MEM1, N_MLP1, N_FINAL = range(7)
        VERSION_OF = {N_MIX0: 0, N_MLP0: 1, N_MIX1: 2, N_MLP1: 3, N_FINAL: 4}
        UPDATES = {1: BANK[0, "wout", 0], 2: BANK[0, "w2", 28], 3: BANK[1, "wout", 0], 4: BANK[1, "w2", 28]}
        H_MIX0, H_Y0, H_MLP0, H_MIX1, H_KV, H_Y1, H_MLP1 = range(7)
        GAIN_OF = {H_MIX0: 1, H_MLP0: 3, H_MIX1: 2, H_KV: 5, H_MLP1: 4}
        H_FREE = {H_Y0: BANK[0, "wout", 0], H_MLP0: BANK[0, "w1", 0], H_MIX1: BANK[0, "w2", 28],
                  H_KV: BANK[1, "mem", 0], H_Y1: BANK[1, "wout", 0], H_MLP1: BANK[1, "w1", 0]}

        @block.sync
        def _(sync):
            sync.dma_start(memraw, memT).then_inc(mem_loaded, 16)
            for u in range(2):
                sync.dma_start(raw[:, u, :], wst[u]).then_inc(raw_loaded[u], 16)
            with sync.Fori(1, NU // 2) as i:
                for s in range(2):
                    sync.wait_ge(unit_split, 2 * i + s - 1)
                    sync.dma_start(raw[:, s, :], wst[2 * i + s]).then_inc(raw_loaded[s], 16)
            for n in range(KT):
                sync.wait_ge(final_ready, n + 1)
                sync.dma_start(outT[:, n, :], X[:, n, :]).then_inc(out_written, 16)
            sync.wait_ge(out_written, 16 * KT)

        @block.gpsimd
        def _(pool):
            G.memset(ident[:, :], 0.0).then_inc(consts_made, 1)
            G.memset(ones[:, :], 1.0).then_inc(consts_made, 1)
            G.memset(XR[:, 0:3], 0.0).then_inc(consts_made, 1)
            G.memset(raw32(mkh[:, :, :]), 0.0).then_inc(consts_made, 1)
            G.memset(raw32(mkl[:, :, :]), 0.0).then_inc(consts_made, 1)
            G.memset(zero[:, :], 0.0).then_inc(consts_made, 1)
            pool.wait_ge(consts_made, 6)
            G.affine_select(out=ident[:, :], in_=ident[:, :], compare_op=ALU.not_equal, fill=1.0, base=0,
                            pattern=[[-1, P]], channel_multiplier=1).then_inc(consts_made, 1)

            def split(s, loaded, n, used):
                pool.wait_ge(raw_loaded[s], loaded)
                if used is not None:
                    pool.wait_ge(bank_done, used)
                G.tensor_tensor(wh[:, s, :], raw[:, s, :], zero[:, :].to_broadcast([P, 1024]), ALU.add).then_inc(unit_hi, 1)
                pool.wait_ge(unit_hi, n)
                G.tensor_tensor(wl[:, s, :], raw[:, s, :], raw32(wh[:, s, :]), ALU.subtract).then_inc(unit_split, 1)

            def split_static(u0, u1):
                for u in range(u0, u1):
                    split(u % 2, 16 * (u // 2 + 1), u + 1, LAST[u - 2] if u >= 2 else None)

            done = 0
            for layer in range(2):
                u0, b0 = UNIT[layer, "w1", 0], BANK[layer, "w1", 0]
                if layer == 1:
                    split_static(done, UNIT[1, "wout", 0])
                    done = UNIT[1, "wout", 0]
                    pool.wait_ge(bank_done, H_FREE[H_Y1])
                    G.memset(raw32(Hh[:, QB:QB + 2048]), 0.0).then_inc(zeros_made, 1)
                    G.memset(raw32(Hl[:, QB:QB + 2048]), 0.0).then_inc(zeros_made, 1)
                split_static(done, u0 + 8)
                with pool.Fori(1, GROUPS) as g:
                    for i in range(8):
                        used = 24 * g + b0 + ([-4, 0, 2, 4, 6, 8, 12, 16][i])
                        split(i % 2, 64 * g + 16 * ((u0 + i) // 2 + 1), 8 * g + (u0 + i + 1), used)
                done = u0 + 8 * GROUPS

        @block.tensor
        def _(pe):
            def passes(out, lh, ll, rh, rl, first, last):
                T.matmul(out, lh, rh, start=first, stop=False)
                T.matmul(out, lh, rl, start=False, stop=False)
                return T.matmul(out, ll, rh, start=False, stop=last)

            def bank_free(b):
                if b >= 4:
                    a, n = EMPTIED[b - 4]
                    pe.wait_ge(emptied[a], n)

            def norm_sums(n, cols):
                if n in VERSION_OF:
                    pe.wait_ge(sq_added, 16 * VERSION_OF[n] + 16)
                else:
                    pe.wait_ge(ssq_mem, (N_MEM0, N_MEM1).index(n) + 1)
                for j in range(cols):
                    last = T.matmul(bank[4][:, j:j + 1], tmp[:, 2, j * P:(j + 1) * P], ones[:, 0:1], start=True, stop=True)
                last.then_inc(colsum_done, 1)

            def norm_spread(n, cols):
                pe.wait_ge(diag_ready, n + 1)
                for h in range(max(1, cols * P // HALF)):
                    w = min(HALF, cols * P)
                    last = T.matmul(bank[5 + h][:, 0:w], ones[:, :], tmp[:, 2, h * HALF:h * HALF + w], start=True, stop=True)
                last.then_inc(bcast_done, 1)

            def unit_from_h(slot, b, h_version, k_major, emptied_of=None):
                order = [(k, h) for k in range(KT) for h in range(2)] if k_major else [(k, h) for h in range(2) for k in range(KT)]
                for k, h in order:
                    if k == 0 and emptied_of is not None:
                        emptied_of(h)
                    if h_version is not None and h == 0:
                        pe.wait_ge(h_ready, 8 * h_version + k + 1)
                    ls = slice(k * P, k * P + P)
                    last = passes(bank[(b + h) % 4][:, :], wh[:, slot, ls], wl[:, slot, ls],
                                  Hh[:, hb(k, h * HALF, HALF)], Hl[:, hb(k, h * HALF, HALF)], k == 0, k == KT - 1)
                    if k == KT - 1:
                        last.then_inc(bank_done, 1)

            def unit_static(layer, kind, i, h_version=None):
                u, b = UNIT[layer, kind, i], BANK[layer, kind, i]
                pe.wait_ge(unit_split, u + 1)
                unit_from_h(u % 2, b, h_version, h_version is not None, lambda h: bank_free(b + h))

            def units_loop(layer, kind, i0, n):
                u, b = UNIT[layer, kind, i0], BANK[layer, kind, i0]
                e = EMPTIED[b - 4][1]
                assert not EMPTIED[b - 4][0] and b % 4 == 0 and u % 2 == 0
                with pe.Fori(0, n // 2) as i:
                    for s in range(2):
                        pe.wait_ge(unit_split, 2 * i + (u + s + 1))
                        unit_from_h(s, b + 2 * s, None, False, lambda h, s=s: pe.wait_ge(emptied[0], 4 * i + (e + 2 * s + h)))

            def memory_kv(layer):
                pe.wait_ge(mem_ready, layer + 1)
                for i in range(2):
                    u, b = UNIT[layer, "mem", i], BANK[layer, "mem", i]
                    pe.wait_ge(unit_split, u + 1)
                    bank_free(b)
                    for k in range(KT):
                        ls, rs = slice(k * P, k * P + P), slice(k * MEM, k * MEM + MEM)
                        last = passes(bank[b % 4][:, 0:MEM], wh[:, u % 2, ls], wl[:, u % 2, ls], Rh[:, rs], Rl[:, rs], k == 0, k == KT - 1)
                    last.then_inc(bank_done, 1)
                pe.wait_ge(unit_split, UNIT[layer, "mem", 3] + 1)
                for m in range(2):
                    b = BANK[layer, "mem", 2 + m]
                    bank_free(b)
                    for k in range(KT):
                        ls, rs = slice(k * MEM + m * P, k * MEM + m * P + P), slice(k % 4 * 256, k % 4 * 256 + 256)
                        last = passes(bank[b % 4][:, 0:256], Rh[:, ls], Rl[:, ls], wh[:, k // 4, rs], wl[:, k // 4, rs], k == 0, k == KT - 1)
                    last.then_inc(bank_done, 1)

            def shared_v(layer):
                pe.wait_ge(unit_split, UNIT[layer, "V", 1] + 1)
                for t in range(KT):
                    b = BANK[layer, "V", 0] + t // 2
                    if t % 2 == 0:
                        bank_free(b)
                    for k in range(KT):
                        ls, rs = hb(k, t * P, P), slice(k % 4 * 256, k % 4 * 256 + 256)
                        last = passes(bank[b % 4][:, t % 2 * 256:t % 2 * 256 + 256], Hh[:, ls], Hl[:, ls],
                                      wh[:, k // 4, rs], wl[:, k // 4, rs], k == 0, k == KT - 1)
                    if t % 2:
                        last.then_inc(bank_done, 1)

            def gates(j):
                u, b, ks = UNIT[0, "G", j], BANK[0, "G", j], GATE_K[j % 3]
                pe.wait_ge(unit_split, u + 1)
                pe.wait_ge(conv_split, 2 * (j - j % 3 + ks[-1]) + 2)
                for h in range(2):
                    for which in range(2):
                        bb = b + 2 * h + which
                        bank_free(bb)
                        for n, k in enumerate(ks):
                            ls, rs = slice((which * len(ks) + n) * P, (which * len(ks) + n + 1) * P), hb(k, h * HALF, HALF)
                            last = passes(bank[bb % 4][:, :], wh[:, u % 2, ls], wl[:, u % 2, ls], Rh[:, rs], Rl[:, rs],
                                          n == 0, n == len(ks) - 1)
                        last.then_inc(bank_done, 1)

            def attention(layer):
                todo = steps(layer)
                s0 = STEP0[layer]

                def scores(i):
                    kind, t, c = todo[i]
                    n = s0 + i
                    pe.wait_ge(q_split, n + 1)
                    if i >= 2:
                        pe.wait_ge(exp_done, n - 1)
                    qs = (QS if kind == "mem" else QB) + i % 4 * 512
                    out = pS[i % 2]
                    if kind == "mem":
                        last = passes(out[:, :], Hh[:, qs:qs + P], Hl[:, qs:qs + P], mkh[:, t, :], mkl[:, t, :], True, True)
                    else:
                        for j in range(4):
                            first_key = max(4 * c + j - 1, 0) * CHUNK
                            rs = slice(t // 3 * S + first_key, t // 3 * S + first_key + P)
                            ls = slice(qs + j * P, qs + j * P + P)
                            last = passes(out[:, j * P:j * P + P], Hh[:, ls], Hl[:, ls], Rh[:, rs], Rl[:, rs], True, True)
                    last.then_inc(score_done, 1)

                def turn(i):
                    kind, t, c = todo[i]
                    n = s0 + i
                    pe.wait_ge(prob_ready, n + 1)
                    if i >= 1:
                        pe.wait_ge(turned_split, n)
                    for j in range(4):
                        o = (j % 2 * 2 + j // 2 if kind == "mem" else j) * P
                        last = T.transpose(pT[:, o:o + P], tmp[:, i % 2, j * P:j * P + P], ident[:, :])
                    last.then_inc(turned, 1)

                def values(i):
                    kind, t, c = todo[i]
                    n = s0 + i
                    pe.wait_ge(turned_split, n + 1)
                    if i >= 1:
                        pe.wait_ge(att_out, n)
                    pt = PT + i % 2 * 512
                    if kind == "mem":
                        for m in range(2):
                            ls, rs = slice(t * P, t * P + P), slice(pt + m * 256, pt + m * 256 + 256)
                            last = passes(pO[:, 0:256], mvh[:, m, ls], mvl[:, m, ls], Hh[:, rs], Hl[:, rs], m == 0, m == 1)
                    else:
                        for j in range(4):
                            q, gp = 4 * c + j, t // 3
                            rs = slice(pt + j * P, pt + j * P + P)
                            if q % 2 or q == 0:
                                vs = slice(2 * S + q // 2 * 256 + gp * P, 2 * S + q // 2 * 256 + gp * P + P)
                                vh, vl = Rh[:, vs], Rl[:, vs]
                            else:
                                vs = slice(V2 + (q // 2 - 1) * 256 + gp * P, V2 + (q // 2 - 1) * 256 + gp * P + P)
                                vh, vl = Hh[:, vs], Hl[:, vs]
                            last = passes(pO[:, j * P:j * P + P], vh, vl, Hh[:, rs], Hl[:, rs], True, True)
                    last.then_inc(pv_done, 1)

                pe.wait_ge(emptied[0], EMPTIED[BANK[layer, "mem", 3]][1])
                scores(0)
                for i in range(len(todo)):
                    if i + 1 < len(todo):
                        if todo[i + 1][0] == "swa" and todo[i][0] == "mem":
                            pe.wait_ge(kv_split, 8)
                            pe.wait_ge(v2_made, 4)
                        scores(i + 1)
                    turn(i)
                    if i >= 1:
                        values(i - 1)
                values(len(todo) - 1)

            def mlp(layer):
                u0, b0 = UNIT[layer, "w1", 0], BANK[layer, "w1", 0]
                e0 = EMPTIED[b0 - 4][1]

                def group(g, first):
                    for f in range(GF):
                        pe.wait_ge(unit_split, 8 * g + (u0 + f + 1))
                        unit_from_h(f % 2, b0 + 2 * f, (H_MLP0, H_MLP1)[layer] if first and f == 0 else None, first and f == 0,
                                    lambda h, f=f: pe.wait_ge(emptied[0], 24 * g + (e0 + 2 * f + h)))
                        if first and f == 0:
                            norm_spread((N_MLP0, N_MLP1)[layer], KT)
                    for v in range(4):
                        pe.wait_ge(unit_split, 8 * g + (u0 + 4 + v + 1))
                        for n in range(2):
                            for h in range(2):
                                c = 8 + 4 * v + 2 * n + h
                                pe.wait_ge(emptied[0], 24 * g + (e0 + c))
                                for f in range(GF):
                                    if v == 0 and n == 0:
                                        pe.wait_ge(hid_split, 8 * g + (64 * layer + 2 * f + h + 1))
                                    ls, rs = slice((n * GF + f) * P, (n * GF + f + 1) * P), slice(f * S + h * HALF, f * S + h * HALF + HALF)
                                    last = passes(bank[(b0 + c) % 4][:, :], wh[:, v % 2, ls], wl[:, v % 2, ls],
                                                  Rh[:, rs], Rl[:, rs], f == 0, f == GF - 1)
                                last.then_inc(bank_done, 1)
                group(0, True)
                with pe.Fori(1, GROUPS) as g:
                    group(g, False)

            pe.wait_ge(consts_loaded, 16 * 5)
            pe.wait_ge(consts_made, 7)
            T.matmul(pO[0:12, 0:REL], relsb[:, :], onesb, start=True, stop=True).then_inc(toep_done, 1)
            norm_sums(N_MEM0, 2)
            norm_spread(N_MEM0, 2)
            memory_kv(0)
            norm_sums(N_MIX0, KT)
            for n, (kind, i) in enumerate(A_ORDER[4:]):
                if kind == "G":
                    gates(i)
                else:
                    unit_static(0, kind, i, H_MIX0 if n == 0 else None)
                if n == 0:
                    norm_spread(N_MIX0, KT)
            attention(0)
            unit_static(0, "wout", 0, H_Y0)
            unit_static(0, "wout", 1)
            units_loop(0, "wout", 2, 6)
            norm_sums(N_MLP0, KT)
            mlp(0)
            norm_sums(N_MIX1, KT)
            unit_static(1, "q", 0, H_MIX1)
            norm_spread(N_MIX1, KT)
            unit_static(1, "q", 1)
            units_loop(1, "q", 2, 4)
            norm_sums(N_MEM1, 2)
            unit_static(1, "qm", 0)
            norm_spread(N_MEM1, 2)
            unit_static(1, "qm", 1)
            memory_kv(1)
            unit_static(1, "K", 0, H_KV)
            unit_static(1, "K", 1)
            shared_v(1)
            attention(1)
            unit_static(1, "wout", 0, H_Y1)
            unit_static(1, "wout", 1)
            units_loop(1, "wout", 2, 6)
            norm_sums(N_MLP1, KT)
            mlp(1)
            norm_sums(N_FINAL, KT)
            norm_spread(N_FINAL, KT)

        @block.scalar
        def _(act):
            own = [0]

            def link(ins):
                own[0] += 1
                ins.then_inc(act_own, 1)
                act.wait_ge(act_own, own[0])

            for dst, src in ((gain[:, :, :], gains), (col[:, :, :], cols), (sink[:, :], sinkc), (relsb[:, :], relb), (onesb, onehot)):
                act.dma_start(dst, src).then_inc(consts_loaded, 16)
            for k in range(KT):
                act.dma_start(X[:, k, :], xT[:, k, :]).then_inc(x_loaded, 16)

            def norm_std(n, c):
                act.wait_ge(var_ready, n + 1)
                A.activation(nrm[:, 1, c], nrm[:, 0, c], ACT.Sqrt).then_inc(std_ready, 1)

            def memory_hi(layer):
                act.wait_ge(mem_normed, layer + 1)
                A.activation(Rh[:, 0:2 * S], memraw, ACT.Copy).then_inc(mem_hi, 1)

            def squares(version):
                for i in range(16):
                    n = 16 * version + i
                    if version:
                        act.wait_ge(emptied[0], EMPTIED[UPDATES[version] + i][1])
                    if n >= 2:
                        act.wait_ge(sq_added, n - 1)
                    A.activation(tmp[:, 1, i % 2 * HALF:i % 2 * HALF + HALF], X[:, i // 2, i % 2 * HALF:i % 2 * HALF + HALF],
                                 ACT.Square).then_inc(x_squared, 1)

            def h_hi_tiles(v, ks):
                for k in ks:
                    A.activation(Hh[:, hb(k, 0, S)], X[:, k, :], ACT.Copy, scale=gain[:, GAIN_OF[v], k:k + 1]).then_inc(h_hi, 1)

            def h_version(v, norm):
                if v in H_FREE:
                    act.wait_ge(bank_done, H_FREE[v])
                h_hi_tiles(v, range(4))
                if norm is not None:
                    norm_std(norm, TOK)
                h_hi_tiles(v, range(4, KT))

            def y_version(v):
                act.wait_ge(bank_done, H_FREE[v])
                act.wait_ge(pv_done, (NMEM, 2 * NMEM + NSWA)[v == H_Y1])
                act.wait_ge(att_out, (NMEM, 2 * NMEM + NSWA)[v == H_Y1])
                if v == H_Y0:
                    act.wait_ge(y_done, 2 * LT)
                for k in range(KT):
                    A.activation(Hh[:, hb(k, 0, S)], Q[:, k, :], ACT.Copy).then_inc(h_hi, 1)

            def memory_kv_hi(layer):
                for i in range(4):
                    b = BANK[layer, "mem", i]
                    act.wait_ge(bank_done, b + 1)
                    if i < 2:
                        for a in range(2):
                            ps = slice(64 * a, 64 * a + 64)
                            last = A.activation(mkh[ps, i, 256 * a:256 * a + 256], bank[b % 4][ps, 0:MEM], ACT.Copy)
                    else:
                        last = A.activation(mvh[:, i - 2, :], bank[b % 4][:, 0:256], ACT.Copy)
                    last.then_inc(mkv_hi, 1)

            def attention(layer):
                todo, s0 = steps(layer), STEP0[layer]

                def query_hi(i):
                    kind, t, c = todo[i]
                    if i >= 4:
                        act.wait_ge(score_done, s0 + i - 3)
                    qs = (QS if kind == "mem" else QB) + i % 4 * 512
                    if kind == "mem":
                        last = A.activation(Hh[:, qs:qs + P], Q[:, 6 + t, c * P:c * P + P], ACT.Copy)
                    else:
                        for a in range(2):
                            ps = slice(64 * a, 64 * a + 64)
                            dst = Hh[ps, qs:qs + 512].rearrange("p (j b t) -> p j b t", j=4, b=2)[:, :, a, :]
                            last = A.activation(dst, Q[ps, t, c * 256:c * 256 + 256].rearrange("p (j t) -> p j t", j=4), ACT.Copy)
                    last.then_inc(q_hi, 1)

                def exps(i):
                    kind, t, c = todo[i]
                    n = s0 + i
                    act.wait_ge(max_ready, n + 1)
                    if i >= 2:
                        act.wait_ge(turned, n - 1)
                    st = stat[:, i % 2]
                    if kind == "mem":
                        for j in range(2):
                            last = A.activation(tmp[:, i % 2, j * 256:j * 256 + 256], pS[i % 2][:, j * 256:j * 256 + 256], ACT.Exp,
                                                scale=SCALE, bias=st[:, 1, j:j + 1], accum_out=st[:, 2, j:j + 1])
                    else:
                        for j in range(4):
                            A.activation(tmp[:, i % 2, j * P:j * P + P], tmp[:, i % 2, HALF + j * P:HALF + j * P + P], ACT.Exp,
                                         bias=st[:, 1, j:j + 1], accum_out=st[:, 2, j:j + 1])
                        last = A.activation(st[:, 3, :], st[:, 1, :], ACT.Exp, bias=sink[:, t:t + 1])
                    last.then_inc(exp_done, 1)

                def turned_hi_part(i):
                    act.wait_ge(turned, s0 + i + 1)
                    if i >= 2:
                        act.wait_ge(pv_done, s0 + i - 1)
                    A.activation(Hh[:, PT + i % 2 * 512:PT + i % 2 * 512 + 512], pT[:, :], ACT.Copy).then_inc(turned_hi, 1)

                act.wait_ge(bank_done, H_FREE[(H_Y0, H_Y1)[layer]])
                act.wait_ge(emptied[0], EMPTIED[BANK[layer, "qm", 1] + 1][1])
                if layer:
                    act.wait_ge(kv_split, 8)
                    for a in range(2):
                        src = slice(2 * S + a * 256, 2 * S + a * 256 + 7 * 256)
                        A.activation(Hh[64 * a:64 * a + 64, V2:V2 + 7 * 256], raw32(Rh[64 - 64 * a:128 - 64 * a, src]), ACT.Copy).then_inc(v2_made, 1)
                query_hi(0)
                query_hi(1)
                exps(0)
                for i in range(len(todo)):
                    if i + 2 < len(todo):
                        if todo[i + 2][0] == "swa" and todo[i + 1][0] == "mem":
                            act.wait_ge(zeros_made, 2)
                        query_hi(i + 2)
                    turned_hi_part(i)
                    if i + 1 < len(todo):
                        exps(i + 1)

            def mlp(layer):
                b0 = BANK[layer, "w1", 0]
                e0 = EMPTIED[b0 - 1][1]

                def group(g):
                    for i in range(2 * GF):
                        s = slice(i % 2 * HALF, i % 2 * HALF + HALF)
                        act.wait_ge(emptied[0], 24 * g + (e0 + i + 1))
                        if i < 2:
                            act.wait_ge(bank_done, 24 * g + b0)
                        else:
                            act.wait_ge(hid_split, 8 * g + (64 * layer + i - 1))
                        A.activation(tmp[:, 1, s], tmp[:, 0, s], ACT.Square).then_inc(relu_squared, 1)
                        act.wait_ge(relu_squared, 8 * g + (64 * layer + i + 1))
                        A.activation(Rh[:, (i // 2) * S + i % 2 * HALF:(i // 2) * S + i % 2 * HALF + HALF], tmp[:, 1, s],
                                     ACT.Copy).then_inc(hid_hi, 1)
                with act.Fori(0, GROUPS) as g:
                    group(g)

            act.wait_ge(consts_loaded, 16 * 5)
            link(A.activation(sp[:, 0, :], col[:, 7, :], ACT.Abs))
            A.activation(sp[:, 1, :], sp[:, 0, :], ACT.Exp, scale=-1.0).then_inc(lam_exp, 1)
            act.wait_ge(toep_copied, 1)
            act.dma_start(rep.rearrange("(h i r) -> h i r", h=12, i=CHUNK), toep.unsqueeze(1).to_broadcast([12, CHUNK, REL])).then_inc(toep_written, 16)
            norm_std(N_MEM0, MEMC)
            memory_hi(0)
            memory_kv_hi(0)
            act.wait_ge(x_loaded, 16 * KT)
            act.wait_ge(mem_ready, 1)
            squares(0)
            h_version(H_MIX0, N_MIX0)

            def decay_root(j):
                act.wait_ge(decay_half, j + 1)
                A.activation(tmp[:, 1, :], tmp[:, 1, :], ACT.Sqrt).then_inc(decay_sqrt, 1)

            pending = None
            for kind, j in A_ORDER[4:]:
                if kind == "xr":
                    for h in range(2):
                        s = slice(h * HALF, h * HALF + HALF)
                        act.wait_ge(emptied[0], EMPTIED[BANK[0, "xr", j] + h][1])
                        A.activation(Q[:, j, s], XR[:, 3 + h * HALF:3 + h * HALF + HALF], ACT.Identity,
                                     scale=col[:, 3, j:j + 1], bias=col[:, 4, j:j + 1]).then_inc(conv_seeded, 1)
                        act.wait_ge(conv_ready, 2 * j + h + 1)
                        if j >= 3 and h == 0:
                            act.wait_ge(bank_done, LAST[UNIT[0, "G", 2 if j > 3 else 1]])
                        A.activation(Rh[:, (j % 3) * S + h * HALF:(j % 3) * S + h * HALF + HALF], Q[:, j, s], ACT.Copy).then_inc(conv_hi, 1)
                elif kind == "gate":
                    for h in range(2):
                        n, s = 2 * j + h, slice(h * HALF, h * HALF + HALF)
                        act.wait_ge(emptied[0], EMPTIED[BANK[0, "gate", j] + h][1])
                        A.activation(rx[:, 1, :], rx[:, 0, :], ACT.Square).then_inc(gate_squared, 1)
                        act.wait_ge(gate_inner, n + 1)
                        A.activation(rx[:, 1, :], rx[:, 1, :], ACT.Tanh, scale=GELU_C * GELU_A).then_inc(gate_tanh, 1)
                if pending is not None:
                    decay_root(pending)
                    pending = None
                if kind == "G":
                    if j >= 1:
                        act.wait_ge(lru_done, j)
                    if j == 0:
                        act.wait_ge(sp_ready, 1)
                    for h in range(2):
                        for which in range(2):
                            b = BANK[0, "G", j] + 2 * h + which
                            act.wait_ge(bank_done, b + 1)
                            A.activation(tmp[:, 2 * which, h * HALF:h * HALF + HALF], bank[b % 4][:, :], ACT.Tanh, scale=0.5,
                                         bias=col[:, 5 + which, j:j + 1]).then_inc(emptied[1], 1)
                    act.wait_ge(emptied[1], EMPTIED[b][1])
                    A.activation(tmp[:, 1, :], tmp[:, 2, :], ACT.Tanh, scale=sp[:, 4, j:j + 1], bias=sp[:, 4, j:j + 1]).then_inc(decay_tanh, 1)
                    act.wait_ge(decay_tanh, 2 * j + 1)
                    A.activation(tmp[:, 2, :], tmp[:, 2, :], ACT.Exp, scale=sp[:, 5, j:j + 1], bias=sp[:, 5, j:j + 1]).then_inc(decay_tanh, 1)
                    pending = j
            attention(0)
            y_version(H_Y0)
            squares(1)
            h_version(H_MLP0, N_MLP0)
            mlp(0)
            squares(2)
            h_version(H_MIX1, N_MIX1)
            act.wait_ge(bcast_done, N_MIX1 + 1)
            act.dma_start(memraw, memT).then_inc(mem_loaded, 16)
            norm_std(N_MEM1, MEMC)
            memory_hi(1)
            act.wait_ge(toep_written, 16)
            for p, pair in enumerate(PAIRS):
                for a, head in enumerate(pair):
                    o = head * CHUNK * REL + CHUNK - 1
                    act.dma_start(bias[64 * a:64 * a + 64, p, :], rep[o:o + CHUNK * (REL - 1)].rearrange(
                        "(i r) -> i r", r=REL - 1)[:, 0:2 * CHUNK]).then_inc(bias_loaded, 16)
            memory_kv_hi(1)
            h_version(H_KV, None)
            for i in range(8):
                s = slice(i * HALF, i * HALF + HALF)
                act.wait_ge(emptied[0], EMPTIED[BANK[1, "K", 0] + i][1])
                A.activation(Rh[:, s], tmp[:, 0, i % 2 * HALF:i % 2 * HALF + HALF], ACT.Copy).then_inc(kv_hi, 1)
            attention(1)
            y_version(H_Y1)
            squares(3)
            h_version(H_MLP1, N_MLP1)
            mlp(1)
            squares(4)
            norm_std(N_FINAL, TOK)

        @block.vector
        def _(dve):
            own = [0]

            def link(ins):
                own[0] += 1
                ins.then_inc(dve_own, 1)
                dve.wait_ge(dve_own, own[0])

            def norm_var(n, c):
                dve.wait_ge(colsum_done, n + 1)
                V.tensor_scalar(nrm[:, 0, c], bank[4][:, 0:c.stop - c.start], 1.0 / D, EPS, ALU.mult, ALU.add).then_inc(var_ready, 1)

            def norm_diag(n, c):
                w = c.stop - c.start
                dve.wait_ge(std_ready, n + 1)
                link(V.reciprocal(nrm[:, 2, c], nrm[:, 1, c]))
                link(V.tensor_tensor(nrm[:, 3, c], nrm[:, 2, c], nrm[:, 2, c], ALU.mult))
                link(V.tensor_tensor(nrm[:, 3, c], nrm[:, 3, c], nrm[:, 0, c], ALU.mult))
                link(V.tensor_scalar(nrm[:, 3, c], nrm[:, 3, c], -0.5, 1.5, ALU.mult, ALU.add))
                link(V.tensor_tensor(nrm[:, 4, c], nrm[:, 2, c], nrm[:, 3, c], ALU.mult))
                V.tensor_tensor(tmp[:, 2, 0:w * P].rearrange("p (j t) -> p j t", t=P),
                                ident[:, :].unsqueeze(1).to_broadcast([P, w, P]),
                                nrm[:, 4, c].unsqueeze(2).to_broadcast([P, w, P]), ALU.mult).then_inc(diag_ready, 1)

            def norm_rstd(n):
                dve.wait_ge(bcast_done, n + 1)
                for h in range(2):
                    link(V.tensor_copy(rstd[:, h * HALF:h * HALF + HALF], bank[5 + h][:, :]))

            def memory_stats(layer):
                dve.wait_ge(mem_loaded, 16 * layer + 16)
                sq = XR[:, 3:3 + S]
                for part in range(2):
                    half = memraw[:, part * S:part * S + S]
                    link(V.tensor_tensor(sq, half, half, ALU.mult))
                    link(V.tensor_reduce(tmp[:, 2, part * MEM:part * MEM + MEM], sq.rearrange("p (k m) -> p m k", m=MEM), AX.X, ALU.add))
                V.tensor_tensor(tmp[:, 2, 0:MEM], tmp[:, 2, 0:MEM], tmp[:, 2, MEM:2 * MEM], ALU.add).then_inc(ssq_mem, 1)
                n = (N_MEM0, N_MEM1)[layer]
                norm_var(n, MEMC)
                norm_diag(n, MEMC)

            def memory_scale(layer):
                dve.wait_ge(bcast_done, (N_MEM0, N_MEM1)[layer] + 1)
                for k in range(KT):
                    ks = slice(k * MEM, k * MEM + MEM)
                    last = V.scalar_tensor_tensor(memraw[:, ks], memraw[:, ks], gain[:, 0, k:k + 1], bank[5][:, 0:MEM], ALU.mult, ALU.mult)
                last.then_inc(mem_normed, 1)

            def memory_lo(layer):
                dve.wait_ge(mem_hi, layer + 1)
                V.tensor_tensor(Rl[:, 0:2 * S], memraw, raw32(Rh[:, 0:2 * S]), ALU.subtract).then_inc(mem_ready, 1)

            def add_square(version, i):
                n = 16 * version + i
                h = i % 2
                dst, sq = tmp[:, 2, h * HALF:h * HALF + HALF], tmp[:, 1, h * HALF:h * HALF + HALF]
                dve.wait_ge(x_squared, n + 1)
                if i < 2:
                    ins = V.tensor_copy(dst, sq)
                else:
                    dve.wait_ge(sq_added, n - 1)
                    ins = V.tensor_tensor(dst, dst, sq, ALU.add)
                ins.then_inc(sq_added, 1)

            def h_lo_tiles(v, ks):
                for k in ks:
                    dve.wait_ge(h_hi, 8 * v + k + 1)
                    V.scalar_tensor_tensor(Hl[:, hb(k, 0, S)], X[:, k, :], gain[:, GAIN_OF[v], k:k + 1], raw32(Hh[:, hb(k, 0, S)]),
                                           ALU.mult, ALU.subtract).then_inc(h_ready, 1)

            def h_version(v, norm):
                if norm is None:
                    return h_lo_tiles(v, range(KT))
                h_lo_tiles(v, range(2))
                norm_var(norm, TOK)
                h_lo_tiles(v, range(2, 4))
                norm_diag(norm, TOK)
                h_lo_tiles(v, range(4, KT))
                norm_rstd(norm)

            def y_version(v):
                for k in range(KT):
                    dve.wait_ge(h_hi, 8 * v + k + 1)
                    V.tensor_tensor(Hl[:, hb(k, 0, S)], Q[:, k, :], raw32(Hh[:, hb(k, 0, S)]), ALU.subtract).then_inc(h_ready, 1)

            def memory_kv_lo(layer):
                for i in range(4):
                    b = BANK[layer, "mem", i]
                    dve.wait_ge(mkv_hi, 4 * layer + i + 1)
                    if i < 2:
                        for a in range(2):
                            ps, cs = slice(64 * a, 64 * a + 64), slice(256 * a, 256 * a + 256)
                            last = V.tensor_tensor(mkl[ps, i, cs], bank[b % 4][ps, 0:MEM], raw32(mkh[ps, i, cs]), ALU.subtract)
                    else:
                        last = V.tensor_tensor(mvl[:, i - 2, :], bank[b % 4][:, 0:256], raw32(mvh[:, i - 2, :]), ALU.subtract)
                    last.then_inc(emptied[0], 1)

            def evict(layer, kind, i, h):
                b = BANK[layer, kind, i] + h
                dve.wait_ge(bank_done, b + 1)
                return bank[b % 4]

            def wout(layer):
                version = (1, 3)[layer]
                for i in range(16):
                    n, h = i // 2, i % 2
                    s = slice(h * HALF, h * HALF + HALF)
                    pb = evict(layer, "wout", n, h)
                    V.tensor_tensor(X[:, n, s], X[:, n, s], pb[:, :], ALU.add).then_inc(emptied[0], 1)
                    if i >= 1:
                        add_square(version, i - 1)
                add_square(version, 15)

            def mlp(layer):
                b0 = BANK[layer, "w1", 0]
                version = (2, 4)[layer]

                def hidden_lo(g, i):
                    s = slice((i // 2) * S + i % 2 * HALF, (i // 2) * S + i % 2 * HALF + HALF)
                    dve.wait_ge(hid_hi, 8 * g + (64 * layer + i + 1))
                    V.tensor_tensor(Rl[:, s], tmp[:, 1, i % 2 * HALF:i % 2 * HALF + HALF], raw32(Rh[:, s]), ALU.subtract).then_inc(hid_split, 1)

                def group(g, last_group):
                    for i in range(2 * GF):
                        s = slice(i % 2 * HALF, i % 2 * HALF + HALF)
                        dve.wait_ge(bank_done, 24 * g + (b0 + i + 1))
                        if i >= 2:
                            dve.wait_ge(relu_squared, 8 * g + (64 * layer + i - 1))
                        V.scalar_tensor_tensor(tmp[:, 0, s], bank[(b0 + i) % 4][:, :], 0.0, rstd[:, s], ALU.max, ALU.mult).then_inc(emptied[0], 1)
                        if i >= 1:
                            hidden_lo(g, i - 1)
                    hidden_lo(g, 2 * GF - 1)
                    for i in range(16):
                        s = slice(i % 2 * HALF, i % 2 * HALF + HALF)
                        dve.wait_ge(bank_done, 24 * g + (b0 + 8 + i + 1))
                        V.tensor_tensor(X[:, i // 2, s], X[:, i // 2, s], bank[(b0 + i) % 4][:, :], ALU.add).then_inc(emptied[0], 1)
                        if last_group and i >= 1:
                            add_square(version, i - 1)
                with dve.Fori(0, GROUPS - 1) as g:
                    group(g, False)
                group(GROUPS - 1, True)
                add_square(version, 15)

            def attention(layer):
                todo, s0 = steps(layer), STEP0[layer]

                def query_lo(i):
                    kind, t, c = todo[i]
                    dve.wait_ge(q_hi, s0 + i + 1)
                    qs = (QS if kind == "mem" else QB) + i % 4 * 512
                    if kind == "mem":
                        last = V.tensor_tensor(Hl[:, qs:qs + P], Q[:, 6 + t, c * P:c * P + P], raw32(Hh[:, qs:qs + P]), ALU.subtract)
                    else:
                        for a in range(2):
                            ps = slice(64 * a, 64 * a + 64)
                            hi = Hh[ps, qs:qs + 512].rearrange("p (j b t) -> p j b t", j=4, b=2)[:, :, a, :]
                            lo = Hl[ps, qs:qs + 512].rearrange("p (j b t) -> p j b t", j=4, b=2)[:, :, a, :]
                            last = V.tensor_tensor(lo, Q[ps, t, c * 256:c * 256 + 256].rearrange("p (j t) -> p j t", j=4), raw32(hi), ALU.subtract)
                    last.then_inc(q_split, 1)

                def maxima(i):
                    kind, t, c = todo[i]
                    n = s0 + i
                    dve.wait_ge(score_done, n + 1)
                    st = stat[:, i % 2]
                    if kind == "mem":
                        link(V.tensor_reduce(st[:, 0, 0:2], pS[i % 2][:, :].rearrange("p (a m) -> p a m", a=2), AX.X, ALU.max))
                        V.tensor_scalar(st[:, 1, 0:2], st[:, 0, 0:2], -SCALE, None, ALU.mult).then_inc(max_ready, 1)
                    else:
                        s = tmp[:, i % 2, HALF:2 * HALF].rearrange("p (j m) -> p j m", j=4)
                        ps = pS[i % 2][:, :].rearrange("p (j m) -> p j m", j=4)
                        j0 = 0
                        if c == 0:
                            V.scalar_tensor_tensor(s[:, 0, 0:CHUNK], ps[:, 0, 0:CHUNK], SCALE, bias[:, t, CHUNK:2 * CHUNK], ALU.mult, ALU.add)
                            V.memset(s[:, 0, CHUNK:2 * CHUNK], NEG)
                            j0 = 1
                        link(V.scalar_tensor_tensor(s[:, j0:4, :], ps[:, j0:4, :], SCALE,
                                                    bias[:, t, :].unsqueeze(1).to_broadcast([P, 4 - j0, P]), ALU.mult, ALU.add))
                        link(V.tensor_reduce(st[:, 0, :], s, AX.X, ALU.max))
                        V.tensor_scalar(st[:, 1, :], st[:, 0, :], sink[:, t:t + 1], -1.0, ALU.max, ALU.mult).then_inc(max_ready, 1)

                def normalise(i):
                    kind, t, c = todo[i]
                    n = s0 + i
                    st = stat[:, i % 2]
                    g = 2 if kind == "mem" else 4
                    dve.wait_ge(exp_done, n + 1)
                    if kind == "swa":
                        link(V.tensor_tensor(st[:, 2, :], st[:, 2, :], st[:, 3, :], ALU.add))
                    link(V.reciprocal(st[:, 4, 0:g], st[:, 2, 0:g]))
                    pr = tmp[:, i % 2, 0:HALF].rearrange("p (j m) -> p j m", j=g)
                    V.tensor_tensor(pr, pr, st[:, 4, 0:g].unsqueeze(2).to_broadcast([P, g, HALF // g]), ALU.mult).then_inc(prob_ready, 1)

                def turned_lo_part(i):
                    dve.wait_ge(turned_hi, s0 + i + 1)
                    s = slice(PT + i % 2 * 512, PT + i % 2 * 512 + 512)
                    V.tensor_tensor(Hl[:, s], pT[:, :], raw32(Hh[:, s]), ALU.subtract).then_inc(turned_split, 1)

                def take_out(i):
                    kind, t, c = todo[i]
                    dve.wait_ge(pv_done, s0 + i + 1)
                    for a in range(2):
                        ps = slice(64 * a, 64 * a + 64)
                        if kind == "mem":
                            last = V.tensor_copy(Q[ps, 6 + t, c * P:c * P + P], pO[ps, a * P:a * P + P])
                        else:
                            last = V.tensor_copy(Q[ps, t, c * 256:c * 256 + 256].rearrange("p (j t) -> p j t", j=4),
                                                 pO[ps, :].rearrange("p (j b t) -> p j b t", j=4, b=2)[:, :, a, :])
                    last.then_inc(att_out, 1)

                if layer:
                    dve.wait_ge(bank_done, H_FREE[H_Y1])
                    dve.wait_ge(kv_split, 8)
                    for a in range(2):
                        src = slice(2 * S + a * 256, 2 * S + a * 256 + 7 * 256)
                        V.tensor_copy(Hl[64 * a:64 * a + 64, V2:V2 + 7 * 256], raw32(Rl[64 - 64 * a:128 - 64 * a, src])).then_inc(v2_made, 1)
                    dve.wait_ge(bias_loaded, 16 * 12)
                query_lo(0)
                query_lo(1)
                maxima(0)
                for i in range(len(todo)):
                    normalise(i)
                    if i + 2 < len(todo):
                        query_lo(i + 2)
                    if i + 1 < len(todo):
                        maxima(i + 1)
                    turned_lo_part(i)
                    if i >= 1:
                        take_out(i - 1)
                take_out(len(todo) - 1)

            dve.wait_ge(toep_done, 1)
            V.tensor_copy(toep, pO[0:12, 0:REL]).then_inc(toep_copied, 1)
            dve.wait_ge(lam_exp, 1)
            link(V.tensor_scalar(sp[:, 0, :], sp[:, 1, :], 2.0, None, ALU.add))
            link(V.reciprocal(sp[:, 0, :], sp[:, 0, :]))
            link(V.tensor_tensor(sp[:, 2, :], sp[:, 1, :], sp[:, 0, :], ALU.mult))
            link(V.tensor_tensor(sp[:, 3, :], sp[:, 2, :], sp[:, 2, :], ALU.mult))
            link(V.memset(sp[:, 4, :], 1.0 / 17.0))
            for d in (15, 13, 11, 9, 7, 5, 3, 1):
                link(V.tensor_tensor(sp[:, 4, :], sp[:, 4, :], sp[:, 3, :], ALU.mult))
                link(V.tensor_scalar(sp[:, 4, :], sp[:, 4, :], 1.0 / d, None, ALU.add))
            link(V.tensor_tensor(sp[:, 4, :], sp[:, 4, :], sp[:, 2, :], ALU.mult))
            link(V.tensor_scalar(sp[:, 5, :], col[:, 7, :], -1.0, 0.0, ALU.mult, ALU.max))
            link(V.scalar_tensor_tensor(sp[:, 6, :], sp[:, 4, :], 2.0, sp[:, 5, :], ALU.mult, ALU.add))
            link(V.tensor_scalar(sp[:, 4, :], sp[:, 6, :], 2.0, None, ALU.mult))
            link(V.tensor_scalar(sp[:, 5, :], sp[:, 6, :], -4.0, None, ALU.mult))
            V.tensor_scalar(col[:, 5:7, :], col[:, 5:7, :], 0.5, None, ALU.mult).then_inc(sp_ready, 1)
            memory_stats(0)
            memory_scale(0)
            memory_lo(0)
            memory_kv_lo(0)
            for i in range(16):
                add_square(0, i)
            h_version(H_MIX0, N_MIX0)
            dve.wait_ge(toep_written, 16)

            def decay_chain(j):
                th_x, root, a = tmp[:, 0, :], tmp[:, 1, :], tmp[:, 2, :]
                dve.wait_ge(decay_tanh, 2 * j + 2)
                link(V.scalar_tensor_tensor(a, a, 1.0, root, ALU.add, ALU.mult))
                V.tensor_scalar(a, a, -1.0, 1.0, ALU.mult, ALU.add).then_inc(decay_half, 1)
                link(V.scalar_tensor_tensor(th_x, th_x, 1.0, Q[:, j, :], ALU.add, ALU.mult))
                dve.wait_ge(decay_sqrt, j + 1)
                link(V.scalar_tensor_tensor(root, a, 1.0, root, ALU.add, ALU.mult))
                link(V.scalar_tensor_tensor(th_x, root, 0.5, th_x, ALU.mult, ALU.mult))
                V.tensor_tensor_scan(Q[:, j, :], a, th_x, 0.0, ALU.mult, ALU.add).then_inc(lru_done, 1)

            pending = None
            for kind, j in A_ORDER[4:]:
                for h in range(2):
                    s = slice(h * HALF, h * HALF + HALF)
                    if kind == "G":
                        continue
                    pb = evict(0, kind, j, h)
                    if kind == "qm":
                        V.tensor_tensor(Q[:, 6 + j, s], pb[:, :], rstd[:, s], ALU.mult).then_inc(emptied[0], 1)
                    elif kind == "xr":
                        V.tensor_tensor(XR[:, 3 + h * HALF:3 + h * HALF + HALF], pb[:, :], rstd[:, s], ALU.mult).then_inc(emptied[0], 1)
                        dve.wait_ge(conv_seeded, 2 * j + h + 1)
                        for tap in range(3):
                            xs = XR[:, tap + h * HALF:tap + h * HALF + HALF]
                            ins = V.scalar_tensor_tensor(Q[:, j, s], xs, col[:, tap, j:j + 1], Q[:, j, s], ALU.mult, ALU.add)
                            if tap < 2:
                                link(ins)
                        ins.then_inc(conv_ready, 1)
                        dve.wait_ge(conv_hi, 2 * j + h + 1)
                        rs = slice((j % 3) * S + h * HALF, (j % 3) * S + h * HALF + HALF)
                        V.tensor_tensor(Rl[:, rs], Q[:, j, s], raw32(Rh[:, rs]), ALU.subtract).then_inc(conv_split, 1)
                    else:
                        n = 2 * j + h
                        g, t = rx[:, 0, :], rx[:, 1, :]
                        V.tensor_tensor(g, pb[:, :], rstd[:, s], ALU.mult).then_inc(emptied[0], 1)
                        dve.wait_ge(gate_squared, n + 1)
                        V.scalar_tensor_tensor(t, t, 1.0 / GELU_A, g, ALU.add, ALU.mult).then_inc(gate_inner, 1)
                        dve.wait_ge(gate_tanh, n + 1)
                        link(V.scalar_tensor_tensor(t, t, 1.0, g, ALU.add, ALU.mult))
                        dve.wait_ge(lru_done, j + 1)
                        V.scalar_tensor_tensor(Q[:, j, s], t, 0.5, Q[:, j, s], ALU.mult, ALU.mult).then_inc(y_done, 1)
                        dve.wait_ge(y_done, n + 1)
                if pending is not None:
                    decay_chain(pending)
                    pending = None
                if kind == "G":
                    pending = j
            attention(0)
            y_version(H_Y0)
            wout(0)
            h_version(H_MLP0, N_MLP0)
            mlp(0)
            h_version(H_MIX1, N_MIX1)

            def queries(kind, i, tile):
                for h in range(2):
                    s = slice(h * HALF, h * HALF + HALF)
                    pb = evict(1, kind, i, h)
                    V.tensor_tensor(Q[:, tile, s], pb[:, :], rstd[:, s], ALU.mult).then_inc(emptied[0], 1)
            for i in range(6):
                queries("q", i, i)
            memory_stats(1)
            queries("qm", 0, 6)
            memory_scale(1)
            queries("qm", 1, 7)
            memory_lo(1)
            memory_kv_lo(1)
            h_version(H_KV, None)
            for i in range(9):
                if i < 8:
                    b = BANK[1, "K", 0] + i
                    t = tmp[:, 0, i % 2 * HALF:i % 2 * HALF + HALF]
                    dve.wait_ge(bank_done, b + 1)
                    if i >= 2:
                        dve.wait_ge(kv_split, i - 1)
                    if i < 4:
                        V.tensor_tensor(t, bank[b % 4][:, :], rstd[:, i % 2 * HALF:i % 2 * HALF + HALF], ALU.mult).then_inc(emptied[0], 1)
                    else:
                        V.tensor_tensor(t.rearrange("p (a d) -> p a d", a=2), bank[b % 4][:, :].rearrange("p (a d) -> p a d", a=2),
                                        nrm[:, 4, 2 * i - 8:2 * i - 6].unsqueeze(2).to_broadcast([P, 2, 256]), ALU.mult).then_inc(emptied[0], 1)
                if i >= 1:
                    s = slice((i - 1) * HALF, i * HALF)
                    dve.wait_ge(kv_hi, i)
                    V.tensor_tensor(Rl[:, s], tmp[:, 0, (i - 1) % 2 * HALF:(i - 1) % 2 * HALF + HALF], raw32(Rh[:, s]), ALU.subtract).then_inc(kv_split, 1)
            attention(1)
            y_version(H_Y1)
            wout(1)
            h_version(H_MLP1, N_MLP1)
            mlp(1)
            norm_var(N_FINAL, TOK)
            norm_diag(N_FINAL, TOK)
            norm_rstd(N_FINAL)
            for n in range(KT):
                V.scalar_tensor_tensor(X[:, n, :], X[:, n, :], gain[:, 6, n:n + 1], rstd[:, :], ALU.mult, ALU.mult).then_inc(final_ready, 1)


def _buckets():
    n = -(np.arange(REL) - (2 * CHUNK - 1))
    half, exact = 16, 8
    out = (n < 0).astype(np.int32) * half
    n = np.abs(n)
    large = exact + (np.log(np.maximum(n, 1) / exact) / np.log(128 / exact) * (half - exact)).astype(np.int32)
    return out + np.where(n < exact, n, np.minimum(large, half - 1))


def _columns(w, tiles=None):
    k, n = w.shape
    return np.ascontiguousarray(w.reshape(k // P, P, n // P, P).transpose(2, 1, 0, 3)).reshape(n // P, P, k)


def _units(x):
    parts = {}
    heads = np.concatenate([np.arange(h * HEAD, h * HEAD + HEAD) for pair in PAIRS for h in pair])
    out_rows = np.concatenate([heads, np.arange(LRU, D)])
    a_in = _columns(x["a_w_in"][0])
    b_in = _columns(np.concatenate([x["b_w_in"][0][:, heads], x["b_w_in"][0][:, LRU:]], axis=1))

    def rows(w):
        return w.reshape(2, 4, P, 256).transpose(0, 2, 1, 3).reshape(2, P, 1024)
    for i in range(6):
        parts[0, "gate", i], parts[0, "xr", i], parts[1, "q", i] = a_in[i], a_in[6 + i], b_in[i]
        unit = np.zeros((P, 8, P), np.float32)
        ks = GATE_K[i % 3]
        for which, name in enumerate(("a_gx_w", "a_ga_w")):
            for n, k in enumerate(ks):
                r0, c0 = (i - i % 3 + k) * P, i * P
                for blk in range(8):
                    lo, hi = blk * GB, blk * GB + GB
                    ra, rb, ca, cb = max(lo, r0), min(hi, r0 + P), max(lo, c0), min(hi, c0 + P)
                    if ra < rb and ca < cb:
                        unit[ra - r0:rb - r0, which * len(ks) + n, ca - c0:cb - c0] = x[name][0, blk, ra - lo:rb - lo, ca - lo:cb - lo]
        parts[0, "G", i] = unit.reshape(P, 1024)
    for i in range(2):
        parts[0, "qm", i], parts[1, "qm", i] = a_in[12 + i], b_in[6 + i]
    kv = x["w_kv_shared"]
    k_units, v_units = _columns(kv[:, :256]), rows(kv[:, 256:])
    for i in range(2):
        parts[1, "K", i], parts[1, "V", i] = k_units[i], v_units[i]
    for layer in range(2):
        m = x["w_mem_kv"][layer]
        mk, mv = _columns(m[:, :256]), rows(m[:, 256:])
        wo = _columns(x["w_out"][layer][out_rows] if layer else x["w_out"][layer])
        w1 = _columns(x["w1"][layer])
        w2 = x["w2"][layer].reshape(GROUPS, GF, P, 4, 2, P).transpose(0, 3, 2, 4, 1, 5).reshape(4 * GROUPS, P, 1024)
        for i in range(2):
            parts[layer, "mem", i], parts[layer, "mem", 2 + i] = mk[i], mv[i]
        for i in range(8):
            parts[layer, "wout", i] = wo[i]
        for i in range(32):
            parts[layer, "w1", i], parts[layer, "w2", i] = w1[i], w2[i]
    return np.stack([parts[key] for key in ORDER])


def _tiles(v, n):
    return v.reshape(n, P).T


def kernel(**inputs):
    import concourse.bacc as bacc
    from concourse.bass_utils import run_bass_kernel_spmd

    x = {k: np.asarray(v) for k, v in inputs.items()}
    gains = [x["mem_norm_g"], x["mix_norm_g"][0], x["mix_norm_g"][1], x["mlp_norm_g"][0], x["mlp_norm_g"][1], x["kv_norm_g"], x["final_norm_g"]]
    cols = [*x["a_conv_w"][0], x["a_conv_b"][0], x["a_gx_b"][0], x["a_ga_b"][0], x["a_lambda"][0]]
    onehot = (_buckets()[None, :] == np.arange(32)[:, None]).astype(np.float32)
    arrays = {
        "xT": x["x"][0].T.reshape(KT, P, S).transpose(1, 0, 2),
        "memT": x["mem"][0].T.reshape(KT, P, MEM).transpose(1, 0, 2).reshape(P, KT * MEM),
        "gains": np.stack([_tiles(g, KT) for g in gains], axis=1),
        "cols": np.stack([_tiles(c, LT) for c in cols], axis=1),
        "sinkc": np.repeat(x["b_sinks"][0][np.array(PAIRS)].T, CHUNK, axis=0),
        "relb": x["rel_bias"],
        "onehot": onehot,
        "wst": _units(x),
    }
    nc = bacc.Bacc("TRN2", target_bir_lowering=False, num_devices=1, dynamic_dma_scratch_size=1024)
    f32 = mybir.dt.float32
    arrays = {k: np.ascontiguousarray(v) for k, v in arrays.items()}
    aps = {k: nc.dram_tensor(k, v.shape, f32, kind="ExternalInput").ap() for k, v in arrays.items()}
    rep = nc.dram_tensor("rep", (12 * CHUNK * REL,), f32).ap()
    outT = nc.dram_tensor("outT", (P, KT, S), f32, kind="ExternalOutput").ap()
    trunk(nc, rep=rep, outT=outT, **aps)
    r = run_bass_kernel_spmd(nc, [arrays], core_ids=[0])
    return np.ascontiguousarray(r.results[0]["outT"].transpose(1, 0, 2).reshape(D, S).T)[None]
```

```python
import numpy as np
import concourse.bass as bass
from concourse import mybir
from concourse.alu_op_type import AluOpType as ALU
from contextlib import ExitStack

D, S, P, HALF = 1024, 1024, 128, 512
KT = D // P
HEAD, MEM, CHUNK = 64, 256, 64
LRU, LT = 768, 6
GB = 96
FF, GF = 4096, 4
GROUPS = FF // P // GF
EPS = 1e-6
NEG = -1e30
SCALE = HEAD ** -0.5
GELU_A, GELU_C = 0.044715, float(np.sqrt(2.0 / np.pi))
PAIRS = [(0, 3), (1, 4), (2, 5), (6, 9), (7, 10), (8, 11)]
GATE_K = [(0, 1), (0, 1, 2), (1, 2)]
REL = 2 * CHUNK + CHUNK - 1

A_ORDER = ([("xr", 0), ("xr", 1)] + [("mem", i) for i in range(4)] + [("xr", 2), ("qm", 0), ("G", 0), ("qm", 1), ("G", 1),
           ("xr", 3), ("G", 2), ("xr", 4), ("xr", 5), ("G", 3), ("gate", 0), ("G", 4), ("gate", 1), ("G", 5)]
           + [("gate", j) for j in range(2, 6)])
B_ORDER = ([("q", 0), ("q", 1), ("q", 2), ("q", 3), ("mem", 0), ("q", 4), ("mem", 1), ("q", 5), ("mem", 2), ("mem", 3), ("qm", 0), ("qm", 1)]
           + [("K", 0), ("K", 1), ("V", 0), ("V", 1)])
MLP_ORDER = [x for g in range(GROUPS) for x in [("w1", 4 * g + i) for i in range(4)] + [("w2", 4 * g + i) for i in range(4)]]
ORDER = ([(0, *x) for x in A_ORDER] + [(0, "wout", n) for n in range(8)] + [(0, *x) for x in MLP_ORDER]
         + [(1, *x) for x in B_ORDER] + [(1, "wout", n) for n in range(8)] + [(1, *x) for x in MLP_ORDER])
NBANKS = {"mem": 1, "G": 4, "w2": 4}
UNIT, BANK, LAST = {}, {}, []
_b = 0
for _u, _key in enumerate(ORDER):
    UNIT[_key], BANK[_key] = _u, _b
    _b += NBANKS.get(_key[1], 2)
    LAST.append(_b)
NU, NB = len(ORDER), _b
for (_l, _k, _i), _u in UNIT.items():
    if _k == "V" and _i == 0 or _k == "mem" and _i == 2:
        LAST[_u] = LAST[_u + 1]
EMPTIED = []
_n = [0, 0]
for _key in ORDER:
    for _ in range(NBANKS.get(_key[1], 2)):
        _a = int(_key[1] == "G")
        _n[_a] += 1
        EMPTIED.append((_a, _n[_a]))


def trunk(nc, xT, memT, gains, cols, sinkc, relb, onehot, wst, rep, outT):
    f32, f32r = mybir.dt.float32, mybir.dt.float32r
    ACT, AX = mybir.ActivationFunctionType, mybir.AxisListType
    V, A, T, G = nc.vector, nc.scalar, nc.tensor, nc.gpsimd
    ctx = ExitStack()
    with ctx:
        def sb(name, shape, dt=f32):
            return ctx.enter_context(nc.sbuf_tensor(name, shape, dt))

        def sem(name):
            return ctx.enter_context(nc.semaphore(name))

        X = sb("X", [P, KT, S])
        Hh, Hl = sb("Hh", [P, KT * S], f32r), sb("Hl", [P, KT * S], f32r)
        raw = sb("raw", [P, 2, 1024])
        wh, wl = sb("wh", [P, 2, 1024], f32r), sb("wl", [P, 2, 1024], f32r)
        Rh, Rl = sb("Rh", [P, 4 * S], f32r), sb("Rl", [P, 4 * S], f32r)
        Q = sb("Q", [P, 8, S])
        XR = sb("XR", [P, 3 + S])
        mkh, mkl = sb("mkh", [P, 2, 512], f32r), sb("mkl", [P, 2, 512], f32r)
        mvh, mvl = sb("mvh", [P, 2, 256], f32r), sb("mvl", [P, 2, 256], f32r)
        rstd = sb("rstd", [P, S])
        tmp = sb("tmp", [P, 3, 1024])
        ident, ones = sb("ident", [P, P]), sb("ones", [P, P])
        gain = sb("gain", [P, 7, KT])
        col = sb("col", [P, 8, LT])
        sink = sb("sink", [P, 6])
        nrm = sb("nrm", [P, 5, 10])
        sp = sb("sp", [P, 8, LT])
        stat = sb("stat", [P, 4, 5, 4])
        zero = sb("zero", [P, 1])
        relsb = sb("relsb", [32, 12])
        onesb = Q[0:32, 0, 0:REL]
        toep = Q[0:12, 1, 0:REL]
        rx = XR[:, 3:3 + S].rearrange("p (a t) -> p a t", a=2)
        memraw = [Q[:, 6:8, :].rearrange("p a t -> p (a t)"), tmp[:, 0:2, :].rearrange("p a t -> p (a t)")]
        MEMR = [2 * S, 0]
        memsq = [(tmp[:, 0, :], XR[:, 3:3 + S]), (XR[:, 3:3 + S], tmp[:, 2, :])]
        bias = XR[:, 0:768].rearrange("p (a j) -> p a j", a=6)

        bank = [ctx.enter_context(nc.psum_tensor(f"bank{i}", [P, HALF], f32)) for i in range(8)]
        pS, pT, pO = [bank[i] for i in (4, 5, 0, 1)], [bank[6], bank[2]], [bank[7], bank[3]]

        consts_loaded, mem_loaded, out_written = sem("consts_loaded"), sem("mem_loaded"), sem("out_written")
        x_loaded = [sem(f"x_loaded{k}") for k in range(KT)]
        consts_made, zeros_made = sem("consts_made"), sem("zeros_made")
        raw_loaded = [sem("raw_loaded0"), sem("raw_loaded1")]
        unit_hi, unit_split = sem("unit_hi"), sem("unit_split")
        bank_done = sem("bank_done")
        emptied = [sem("emptied_vector"), sem("emptied_scalar")]
        dve_own, act_own = sem("dve_own"), sem("act_own")
        colsum_done, var_ready, std_ready, diag_ready, bcast_done = (
            sem(n) for n in ("colsum_done", "var_ready", "std_ready", "diag_ready", "bcast_done"))
        mem_sq, mem_ssq, mem_colsum, mem_var, mem_std, mem_diag, mem_bcast = (
            sem(n) for n in ("mem_sq", "mem_ssq", "mem_colsum", "mem_var", "mem_std", "mem_diag", "mem_bcast"))
        x_squared, sq_added = sem("x_squared"), sem("sq_added")
        h_hi, h_ready = sem("h_hi"), sem("h_ready")
        mem_normed, mem_hi, mem_ready = sem("mem_normed"), sem("mem_hi"), sem("mem_ready")
        mkv_hi = sem("mkv_hi")
        lam_exp, conv_seeded, conv_ready, conv_hi, conv_split = (
            sem(n) for n in ("lam_exp", "conv_seeded", "conv_ready", "conv_hi", "conv_split"))
        sp_ready = sem("sp_ready")
        decay_tanh, decay_half, decay_sqrt, lru_done = sem("decay_tanh"), sem("decay_half"), sem("decay_sqrt"), sem("lru_done")
        gate_squared, gate_inner, gate_tanh, y_done = (
            sem(n) for n in ("gate_squared", "gate_inner", "gate_tanh", "y_done"))
        toep_done, toep_copied, toep_written, bias_loaded = (sem(n) for n in ("toep_done", "toep_copied", "toep_written", "bias_loaded"))
        kv_hi, kv_split, v2_made = sem("kv_hi"), sem("kv_split"), sem("v2_made")
        q_hi, q_split, score_done, max_ready, exp_done, denom_ready, prob_ready, turned, turned_hi, turned_split, pv_done, att_out = (
            sem(n) for n in ("q_hi", "q_split", "score_done", "max_ready", "exp_done", "denom_ready", "prob_ready", "turned",
                             "turned_hi", "turned_split", "pv_done", "att_out"))
        relu_squared, hid_hi, hid_split = sem("relu_squared"), sem("hid_hi"), sem("hid_split")
        final_ready = sem("final_ready")
        block = ctx.enter_context(nc.Block())

        def hb(k, lo, n):
            return slice(k * S + lo, k * S + lo + n)

        TOK, MEMC = slice(0, 8), slice(8, 10)

        def raw32(ap):
            return ap.bitcast(f32)

        V2 = 0
        QS = 1792
        QB = 2304
        PT = 4352

        def query_at(kind, i):
            return QS + i % 4 * P if kind == "mem" else QB + i % 4 * 512

        NMEM, NSWA = 16, 24
        STEP0 = [0, NMEM]
        def steps(layer):
            out = [("mem", i // 8, i % 8) for i in range(NMEM)]
            if layer:
                out += [("swa", i // 4, i % 4) for i in range(NSWA)]
            return out
        MIX0, MLP0, MIX1, MLP1, FINAL = range(5)
        UPDATES = {MLP0: BANK[0, "wout", 0], MIX1: BANK[0, "w2", 28], MLP1: BANK[1, "wout", 0], FINAL: BANK[1, "w2", 28]}
        H_MIX0, H_Y0, H_MLP0, H_MIX1, H_KV, H_Y1, H_MLP1 = range(7)
        GAIN_OF = {H_MIX0: 1, H_MLP0: 3, H_MIX1: 2, H_KV: 5, H_MLP1: 4}
        H_FREE = {H_Y0: BANK[0, "wout", 0], H_MLP0: BANK[0, "w1", 0], H_MIX1: BANK[0, "w2", 28],
                  H_KV: BANK[1, "K", 0], H_Y1: BANK[1, "wout", 0], H_MLP1: BANK[1, "w1", 0]}

        @block.sync
        def _(sync):
            for u in range(2):
                sync.dma_start(raw[:, u, :], wst[u]).then_inc(raw_loaded[u], 16)
            sync.dma_start(memraw[0], memT).then_inc(mem_loaded, 16)
            with sync.Fori(1, NU // 2) as i:
                for s in range(2):
                    sync.wait_ge(unit_split, 2 * i + s - 1)
                    sync.dma_start(raw[:, s, :], wst[2 * i + s]).then_inc(raw_loaded[s], 16)
            for n in range(KT):
                sync.wait_ge(final_ready, n + 1)
                sync.dma_start(outT[:, n, :], X[:, n, :]).then_inc(out_written, 16)
            sync.wait_ge(out_written, 16 * KT)

        @block.gpsimd
        def _(pool):
            G.memset(ident[:, :], 0.0).then_inc(consts_made, 1)
            G.memset(ones[:, :], 1.0).then_inc(consts_made, 1)
            G.memset(XR[:, 0:3], 0.0).then_inc(consts_made, 1)
            G.memset(raw32(mkh[:, :, :]), 0.0).then_inc(consts_made, 1)
            G.memset(raw32(mkl[:, :, :]), 0.0).then_inc(consts_made, 1)
            G.memset(zero[:, :], 0.0).then_inc(consts_made, 1)
            pool.wait_ge(consts_made, 6)
            G.affine_select(out=ident[:, :], in_=ident[:, :], compare_op=ALU.not_equal, fill=1.0, base=0,
                            pattern=[[-1, P]], channel_multiplier=1).then_inc(consts_made, 1)

            def split(s, loaded, n, used):
                pool.wait_ge(raw_loaded[s], loaded)
                if used is not None:
                    pool.wait_ge(bank_done, used)
                G.tensor_tensor(wh[:, s, :], raw[:, s, :], zero[:, :].to_broadcast([P, 1024]), ALU.add).then_inc(unit_hi, 1)
                pool.wait_ge(unit_hi, n)
                G.tensor_tensor(wl[:, s, :], raw[:, s, :], raw32(wh[:, s, :]), ALU.subtract).then_inc(unit_split, 1)

            def memory_squares(layer):
                (one, two), mem, n = memsq[layer], memraw[layer], 4 * layer
                pool.wait_ge(mem_loaded, 16 * layer + 16)
                if layer:
                    pool.wait_ge(bcast_done, MIX1 + 1)
                G.tensor_tensor(one, mem[:, 0:S], mem[:, 0:S], ALU.mult).then_inc(mem_sq, 1)
                G.tensor_tensor(two, mem[:, S:2 * S], mem[:, S:2 * S], ALU.mult).then_inc(mem_sq, 1)
                pool.wait_ge(mem_sq, n + 2)
                G.tensor_tensor(one, one, two, ALU.add).then_inc(mem_sq, 1)
                pool.wait_ge(mem_sq, n + 3)
                G.tensor_tensor(one[:, 0:512], one[:, 0:512], one[:, 512:1024], ALU.add).then_inc(mem_sq, 1)
                pool.wait_ge(mem_sq, n + 4)
                G.tensor_tensor(one[:, 0:256], one[:, 0:256], one[:, 256:512], ALU.add).then_inc(mem_ssq, 1)

            def attention(layer):
                todo, s0 = steps(layer), STEP0[layer]

                def query_lo(i):
                    kind, t, c = todo[i]
                    pool.wait_ge(q_hi, s0 + i + 1)
                    qs = query_at(kind, i)
                    if kind == "mem":
                        last = G.tensor_tensor(Hl[:, qs:qs + P], Q[:, 6 + t, c * P:c * P + P], raw32(Hh[:, qs:qs + P]), ALU.subtract)
                    else:
                        for a in range(2):
                            ps = slice(64 * a, 64 * a + 64)
                            hi = Hh[ps, qs:qs + 512].rearrange("p (j b t) -> p j b t", j=4, b=2)[:, :, a, :]
                            lo = Hl[ps, qs:qs + 512].rearrange("p (j b t) -> p j b t", j=4, b=2)[:, :, a, :]
                            last = G.tensor_tensor(lo, Q[ps, t, c * 256:c * 256 + 256].rearrange("p (j t) -> p j t", j=4), raw32(hi), ALU.subtract)
                    last.then_inc(q_split, 1)

                def normalise(i):
                    g = 2 if todo[i][0] == "mem" else 4
                    pool.wait_ge(denom_ready, s0 + i + 1)
                    pr = tmp[:, i % 3, 0:HALF].rearrange("p (j m) -> p j m", j=g)
                    G.tensor_tensor(pr, pr, stat[:, i % 4, 4, 0:g].unsqueeze(2).to_broadcast([P, g, HALF // g]), ALU.mult).then_inc(prob_ready, 1)

                for i in range(4):
                    query_lo(i)
                for i in range(len(todo)):
                    normalise(i)
                    if i + 4 < len(todo):
                        if todo[i + 4][0] == "swa":
                            pool.wait_ge(prob_ready, s0 + i + 1)
                        query_lo(i + 4)
                        if todo[i + 4][0] == "swa":
                            pool.wait_ge(q_split, s0 + i + 5)

            def split_static(u0, u1):
                for u in range(u0, u1):
                    split(u % 2, 16 * (u // 2 + 1), u + 1, LAST[u - 2] if u >= 2 else None)

            done = 0
            for layer in range(2):
                u0, b0 = UNIT[layer, "w1", 0], BANK[layer, "w1", 0]
                uw = UNIT[layer, "wout", 0]
                split_static(done, UNIT[layer, A_ORDER[0][0] if layer == 0 else "q", 0] + 2)
                memory_squares(layer)
                split_static(UNIT[layer, A_ORDER[0][0] if layer == 0 else "q", 0] + 2, uw + (2 if layer == 0 else 0))
                if layer == 1:
                    pool.wait_ge(bank_done, H_FREE[H_Y1])
                    G.memset(raw32(Hh[:, QB:QB + 2048]), 0.0).then_inc(zeros_made, 1)
                    G.memset(raw32(Hl[:, QB:QB + 2048]), 0.0).then_inc(zeros_made, 1)
                    split_static(uw, uw + 2)
                attention(layer)
                split_static(uw + 2, u0 + 8)
                with pool.Fori(1, GROUPS) as g:
                    for i in range(8):
                        used = 24 * g + b0 + ([-4, 0, 2, 4, 6, 8, 12, 16][i])
                        split(i % 2, 64 * g + 16 * ((u0 + i) // 2 + 1), 8 * g + (u0 + i + 1), used)
                done = u0 + 8 * GROUPS

        @block.tensor
        def _(pe):
            def passes(out, lh, ll, rh, rl, first, last):
                T.matmul(out, lh, rh, start=first, stop=False)
                T.matmul(out, lh, rl, start=False, stop=False)
                return T.matmul(out, ll, rh, start=False, stop=last)

            def bank_free(b):
                if b >= 4:
                    a, n = EMPTIED[b - 4]
                    pe.wait_ge(emptied[a], n)

            def norm_sums(n):
                pe.wait_ge(sq_added, 16 * n + 16)
                for j in range(KT):
                    last = T.matmul(bank[4][:, j:j + 1], tmp[:, 2, j * P:(j + 1) * P], ones[:, 0:1], start=True, stop=True)
                last.then_inc(colsum_done, 1)

            def norm_spread(n):
                pe.wait_ge(diag_ready, n + 1)
                for h in range(2):
                    last = T.matmul(bank[5 + h][:, :], ones[:, :], tmp[:, 2, h * HALF:h * HALF + HALF], start=True, stop=True)
                last.then_inc(bcast_done, 1)

            def memory_sums(layer):
                pe.wait_ge(mem_ssq, layer + 1)
                for j in range(2):
                    last = T.matmul(bank[7][:, j:j + 1], memsq[layer][0][:, j * P:(j + 1) * P], ones[:, 0:1], start=True, stop=True)
                last.then_inc(mem_colsum, 1)

            def memory_spread(layer):
                pe.wait_ge(mem_diag, layer + 1)
                T.matmul(bank[7][:, 0:MEM], ones[:, :], memsq[layer][1][:, 0:MEM], start=True, stop=True).then_inc(mem_bcast, 1)

            def unit_from_h(slot, b, h_version, k_major, emptied_of, between=None):
                order = [(k, h) for k in range(KT) for h in range(2)] if k_major else [(k, h) for h in range(2) for k in range(KT)]
                for k, h in order:
                    if k == 0:
                        if h == 1 and between is not None:
                            between()
                        emptied_of(h)
                    if h_version is not None and h == 0:
                        pe.wait_ge(h_ready, 8 * h_version + k + 1)
                    ls = slice(k * P, k * P + P)
                    last = passes(bank[(b + h) % 4][:, :], wh[:, slot, ls], wl[:, slot, ls],
                                  Hh[:, hb(k, h * HALF, HALF)], Hl[:, hb(k, h * HALF, HALF)], k == 0, k == KT - 1)
                    if k == KT - 1:
                        last.then_inc(bank_done, 1)

            def unit_static(layer, kind, i, h_version=None, between=None):
                u, b = UNIT[layer, kind, i], BANK[layer, kind, i]
                pe.wait_ge(unit_split, u + 1)
                unit_from_h(u % 2, b, h_version, h_version is not None, lambda h: bank_free(b + h), between)

            def units_loop(layer, kind, i0, n):
                u, b = UNIT[layer, kind, i0], BANK[layer, kind, i0]
                e = EMPTIED[b - 4][1]
                assert not EMPTIED[b - 4][0] and b % 4 == 0 and u % 2 == 0
                with pe.Fori(0, n // 2) as i:
                    for s in range(2):
                        pe.wait_ge(unit_split, 2 * i + (u + s + 1))
                        unit_from_h(s, b + 2 * s, None, False, lambda h, s=s: pe.wait_ge(emptied[0], 4 * i + (e + 2 * s + h)))

            def memory_k(layer, i):
                pe.wait_ge(mem_ready, layer + 1)
                u, b = UNIT[layer, "mem", i], BANK[layer, "mem", i]
                pe.wait_ge(unit_split, u + 1)
                bank_free(b)
                for k in range(KT):
                    ls, rs = slice(k * P, k * P + P), slice(MEMR[layer] + k * MEM, MEMR[layer] + k * MEM + MEM)
                    last = passes(bank[b % 4][:, 0:MEM], wh[:, u % 2, ls], wl[:, u % 2, ls], Rh[:, rs], Rl[:, rs], k == 0, k == KT - 1)
                last.then_inc(bank_done, 1)

            def memory_v(layer):
                pe.wait_ge(unit_split, UNIT[layer, "mem", 3] + 1)
                for m in range(2):
                    b = BANK[layer, "mem", 2 + m]
                    bank_free(b)
                    for k in range(KT):
                        ls, rs = slice(MEMR[layer] + k * MEM + m * P, MEMR[layer] + k * MEM + m * P + P), slice(k % 4 * 256, k % 4 * 256 + 256)
                        last = passes(bank[b % 4][:, 0:256], Rh[:, ls], Rl[:, ls], wh[:, k // 4, rs], wl[:, k // 4, rs], k == 0, k == KT - 1)
                    last.then_inc(bank_done, 1)

            def shared_v(layer):
                pe.wait_ge(unit_split, UNIT[layer, "V", 1] + 1)
                for t in range(KT):
                    b = BANK[layer, "V", 0] + t // 2
                    if t % 2 == 0:
                        bank_free(b)
                    for k in range(KT):
                        ls, rs = hb(k, t * P, P), slice(k % 4 * 256, k % 4 * 256 + 256)
                        last = passes(bank[b % 4][:, t % 2 * 256:t % 2 * 256 + 256], Hh[:, ls], Hl[:, ls],
                                      wh[:, k // 4, rs], wl[:, k // 4, rs], k == 0, k == KT - 1)
                    if t % 2:
                        last.then_inc(bank_done, 1)

            def gates(j):
                u, b, ks = UNIT[0, "G", j], BANK[0, "G", j], GATE_K[j % 3]
                pe.wait_ge(unit_split, u + 1)
                pe.wait_ge(conv_split, 2 * (j - j % 3 + ks[-1]) + 2)
                for h in range(2):
                    for which in range(2):
                        bb = b + 2 * h + which
                        bank_free(bb)
                        for n, k in enumerate(ks):
                            ls, rs = slice((which * len(ks) + n) * P, (which * len(ks) + n + 1) * P), hb(k, h * HALF, HALF)
                            last = passes(bank[bb % 4][:, :], wh[:, u % 2, ls], wl[:, u % 2, ls], Rh[:, rs], Rl[:, rs],
                                          n == 0, n == len(ks) - 1)
                        last.then_inc(bank_done, 1)

            def attention(layer):
                todo = steps(layer)
                s0 = STEP0[layer]

                def scores(i):
                    kind, t, c = todo[i]
                    n = s0 + i
                    pe.wait_ge(q_split, n + 1)
                    if i >= 4:
                        pe.wait_ge(exp_done, n - 3)
                    if i == 2:
                        pe.wait_ge(emptied[0], EMPTIED[BANK[layer, "wout", 0] - 1][1])
                    if kind == "swa" and todo[i - 1][0] == "mem":
                        pe.wait_ge(v2_made, 4)
                    qs = query_at(kind, i)
                    out = pS[i % 4]
                    if kind == "mem":
                        last = passes(out[:, :], Hh[:, qs:qs + P], Hl[:, qs:qs + P], mkh[:, t, :], mkl[:, t, :], True, True)
                    else:
                        for j in range(4):
                            first_key = max(4 * c + j - 1, 0) * CHUNK
                            rs = slice(t // 3 * S + first_key, t // 3 * S + first_key + P)
                            ls = slice(qs + j * P, qs + j * P + P)
                            last = passes(out[:, j * P:j * P + P], Hh[:, ls], Hl[:, ls], Rh[:, rs], Rl[:, rs], True, True)
                    last.then_inc(score_done, 1)

                def turn(i):
                    kind, t, c = todo[i]
                    n = s0 + i
                    pe.wait_ge(prob_ready, n + 1)
                    if i >= 2:
                        pe.wait_ge(turned_split, n - 1)
                    for j in range(4):
                        o = (j % 2 * 2 + j // 2 if kind == "mem" else j) * P
                        last = T.transpose(pT[i % 2][:, o:o + P], tmp[:, i % 3, j * P:j * P + P], ident[:, :])
                    last.then_inc(turned, 1)

                def values(i):
                    kind, t, c = todo[i]
                    n = s0 + i
                    pe.wait_ge(turned_split, n + 1)
                    if i >= 2:
                        pe.wait_ge(att_out, n - 1)
                    pt, out = PT + i % 3 * 512, pO[i % 2]
                    if kind == "mem":
                        for m in range(2):
                            ls, rs = slice(t * P, t * P + P), slice(pt + m * 256, pt + m * 256 + 256)
                            last = passes(out[:, 0:256], mvh[:, m, ls], mvl[:, m, ls], Hh[:, rs], Hl[:, rs], m == 0, m == 1)
                    else:
                        for j in range(4):
                            q, gp = 4 * c + j, t // 3
                            rs = slice(pt + j * P, pt + j * P + P)
                            if q % 2 or q == 0:
                                vs = slice(2 * S + q // 2 * 256 + gp * P, 2 * S + q // 2 * 256 + gp * P + P)
                                vh, vl = Rh[:, vs], Rl[:, vs]
                            else:
                                vs = slice(V2 + (q // 2 - 1) * 256 + gp * P, V2 + (q // 2 - 1) * 256 + gp * P + P)
                                vh, vl = Hh[:, vs], Hl[:, vs]
                            last = passes(out[:, j * P:j * P + P], vh, vl, Hh[:, rs], Hl[:, rs], True, True)
                    last.then_inc(pv_done, 1)

                pe.wait_ge(emptied[0], EMPTIED[BANK[layer, "mem", 3]][1])
                for i in range(3):
                    scores(i)
                for i in range(len(todo)):
                    if i + 3 < len(todo):
                        scores(i + 3)
                    turn(i)
                    if i >= 1:
                        values(i - 1)
                values(len(todo) - 1)

            def mlp(layer):
                u0, b0 = UNIT[layer, "w1", 0], BANK[layer, "w1", 0]
                e0 = EMPTIED[b0 - 4][1]

                def group(g, first):
                    for f in range(GF):
                        pe.wait_ge(unit_split, 8 * g + (u0 + f + 1))
                        unit_from_h(f % 2, b0 + 2 * f, (H_MLP0, H_MLP1)[layer] if first and f == 0 else None, first and f == 0,
                                    lambda h, f=f: pe.wait_ge(emptied[0], 24 * g + (e0 + 2 * f + h)),
                                    (lambda: norm_spread((MLP0, MLP1)[layer])) if first and f == 1 else None)
                        if first and f == 0:
                            norm_sums((MLP0, MLP1)[layer])
                    for v in range(4):
                        pe.wait_ge(unit_split, 8 * g + (u0 + 4 + v + 1))
                        for n in range(2):
                            for h in range(2):
                                c = 8 + 4 * v + 2 * n + h
                                pe.wait_ge(emptied[0], 24 * g + (e0 + c))
                                for f in range(GF):
                                    if v == 0 and n == 0:
                                        pe.wait_ge(hid_split, 8 * g + (64 * layer + 2 * f + h + 1))
                                    ls, rs = slice((n * GF + f) * P, (n * GF + f + 1) * P), slice(f * S + h * HALF, f * S + h * HALF + HALF)
                                    last = passes(bank[(b0 + c) % 4][:, :], wh[:, v % 2, ls], wl[:, v % 2, ls],
                                                  Rh[:, rs], Rl[:, rs], f == 0, f == GF - 1)
                                last.then_inc(bank_done, 1)
                group(0, True)
                with pe.Fori(1, GROUPS) as g:
                    group(g, False)

            pe.wait_ge(consts_loaded, 16 * 5)
            pe.wait_ge(consts_made, 7)
            T.matmul(bank[7][0:12, 0:REL], relsb[:, :], onesb, start=True, stop=True).then_inc(toep_done, 1)
            unit_static(0, "xr", 0, H_MIX0)
            norm_sums(MIX0)
            pe.wait_ge(toep_copied, 1)
            memory_sums(0)

            def spreads():
                norm_spread(MIX0)
                memory_spread(0)
            unit_static(0, "xr", 1, between=spreads)
            memory_k(0, 0)
            memory_k(0, 1)
            memory_v(0)
            for kind, i in A_ORDER[6:]:
                if kind == "G":
                    gates(i)
                else:
                    unit_static(0, kind, i)
            attention(0)
            unit_static(0, "wout", 0, H_Y0)
            unit_static(0, "wout", 1)
            units_loop(0, "wout", 2, 6)
            mlp(0)
            unit_static(1, "q", 0, H_MIX1)
            norm_sums(MIX1)
            unit_static(1, "q", 1, between=lambda: norm_spread(MIX1))
            unit_static(1, "q", 2)
            memory_sums(1)
            unit_static(1, "q", 3, between=lambda: memory_spread(1))
            memory_k(1, 0)
            unit_static(1, "q", 4)
            memory_k(1, 1)
            unit_static(1, "q", 5)
            memory_v(1)
            unit_static(1, "qm", 0)
            unit_static(1, "qm", 1)
            unit_static(1, "K", 0, H_KV)
            unit_static(1, "K", 1)
            shared_v(1)
            attention(1)
            unit_static(1, "wout", 0, H_Y1)
            unit_static(1, "wout", 1)
            units_loop(1, "wout", 2, 6)
            mlp(1)
            norm_sums(FINAL)
            norm_spread(FINAL)

        @block.scalar
        def _(act):
            own = [0]

            def link(ins):
                own[0] += 1
                ins.then_inc(act_own, 1)
                act.wait_ge(act_own, own[0])

            for dst, src in ((gain[:, :, :], gains), (col[:, :, :], cols), (sink[:, :], sinkc), (relsb[:, :], relb), (onesb, onehot)):
                act.dma_start(dst, src).then_inc(consts_loaded, 16)
            for k in range(KT):
                act.dma_start(X[:, k, :], xT[:, k, :]).then_inc(x_loaded[k], 16)

            def norm_std(n):
                act.wait_ge(var_ready, n + 1)
                A.activation(nrm[:, 1, TOK], nrm[:, 0, TOK], ACT.Sqrt).then_inc(std_ready, 1)

            def memory_std(layer):
                act.wait_ge(mem_var, layer + 1)
                A.activation(nrm[:, 1, MEMC], nrm[:, 0, MEMC], ACT.Sqrt).then_inc(mem_std, 1)

            def memory_hi(layer):
                act.wait_ge(mem_normed, layer + 1)
                A.activation(Rh[:, MEMR[layer]:MEMR[layer] + 2 * S], memraw[layer], ACT.Copy).then_inc(mem_hi, 1)

            def squares(version, which):
                for i in which:
                    n = 16 * version + i
                    if version == MIX0:
                        act.wait_ge(x_loaded[i // 2], 16)
                    else:
                        act.wait_ge(emptied[0], EMPTIED[UPDATES[version] + i][1])
                    if n >= 2:
                        act.wait_ge(sq_added, n - 1)
                    A.activation(tmp[:, 1, i % 2 * HALF:i % 2 * HALF + HALF], X[:, i // 2, i % 2 * HALF:i % 2 * HALF + HALF],
                                 ACT.Square).then_inc(x_squared, 1)

            def h_hi_tiles(v, ks):
                for k in ks:
                    A.activation(Hh[:, hb(k, 0, S)], X[:, k, :], ACT.Copy, scale=gain[:, GAIN_OF[v], k:k + 1]).then_inc(h_hi, 1)

            def h_version(v, norm):
                if v in H_FREE:
                    act.wait_ge(bank_done, H_FREE[v])
                if norm == MIX0:
                    for k in range(KT):
                        squares(MIX0, (2 * k, 2 * k + 1))
                        h_hi_tiles(v, (k,))
                else:
                    h_hi_tiles(v, range(2))
                    if norm is not None:
                        squares(norm, (14, 15))
                    h_hi_tiles(v, range(2, KT))
                if norm is not None:
                    norm_std(norm)

            def y_version(v):
                act.wait_ge(bank_done, H_FREE[v])
                act.wait_ge(pv_done, (NMEM, 2 * NMEM + NSWA)[v == H_Y1])
                act.wait_ge(att_out, (NMEM, 2 * NMEM + NSWA)[v == H_Y1])
                if v == H_Y0:
                    act.wait_ge(y_done, 2 * LT)
                for k in range(KT):
                    A.activation(Hh[:, hb(k, 0, S)], Q[:, k, :], ACT.Copy).then_inc(h_hi, 1)

            def memory_kv_hi(layer, which=range(4)):
                for i in which:
                    b = BANK[layer, "mem", i]
                    act.wait_ge(bank_done, b + 1)
                    if i < 2:
                        for a in range(2):
                            ps = slice(64 * a, 64 * a + 64)
                            last = A.activation(mkh[ps, i, 256 * a:256 * a + 256], bank[b % 4][ps, 0:MEM], ACT.Copy)
                    else:
                        last = A.activation(mvh[:, i - 2, :], bank[b % 4][:, 0:256], ACT.Copy)
                    last.then_inc(mkv_hi, 1)

            def attention(layer):
                todo, s0 = steps(layer), STEP0[layer]

                def query_hi(i):
                    kind, t, c = todo[i]
                    if i >= 4:
                        act.wait_ge(score_done, s0 + i - 3)
                    if kind == "swa" and todo[i - 1][0] == "mem":
                        act.wait_ge(zeros_made, 2)
                    qs = query_at(kind, i)
                    if kind == "mem":
                        last = A.activation(Hh[:, qs:qs + P], Q[:, 6 + t, c * P:c * P + P], ACT.Copy)
                    else:
                        for a in range(2):
                            ps = slice(64 * a, 64 * a + 64)
                            dst = Hh[ps, qs:qs + 512].rearrange("p (j b t) -> p j b t", j=4, b=2)[:, :, a, :]
                            last = A.activation(dst, Q[ps, t, c * 256:c * 256 + 256].rearrange("p (j t) -> p j t", j=4), ACT.Copy)
                    last.then_inc(q_hi, 1)

                def exps(i):
                    kind, t, c = todo[i]
                    n = s0 + i
                    act.wait_ge(max_ready, n + 1)
                    if i >= 3:
                        act.wait_ge(turned, n - 2)
                    st = stat[:, i % 4]
                    if kind == "mem":
                        for j in range(2):
                            last = A.activation(tmp[:, i % 3, j * 256:j * 256 + 256], pS[i % 4][:, j * 256:j * 256 + 256], ACT.Exp,
                                                scale=SCALE, bias=st[:, 1, j:j + 1], accum_out=st[:, 2, j:j + 1])
                    else:
                        for j in range(4):
                            A.activation(tmp[:, i % 3, j * P:j * P + P], tmp[:, i % 3, HALF + j * P:HALF + j * P + P], ACT.Exp,
                                         bias=st[:, 1, j:j + 1], accum_out=st[:, 2, j:j + 1])
                        last = A.activation(st[:, 3, :], st[:, 1, :], ACT.Exp, bias=sink[:, t:t + 1])
                    last.then_inc(exp_done, 1)

                def turned_hi_part(i):
                    act.wait_ge(turned, s0 + i + 1)
                    if i >= 3:
                        act.wait_ge(pv_done, s0 + i - 2)
                    A.activation(Hh[:, PT + i % 3 * 512:PT + i % 3 * 512 + 512], pT[i % 2][:, :], ACT.Copy).then_inc(turned_hi, 1)

                act.wait_ge(bank_done, H_FREE[(H_Y0, H_Y1)[layer]])
                act.wait_ge(emptied[0], EMPTIED[BANK[layer, "qm", 1] + 1][1])
                for i in range(4):
                    query_hi(i)
                exps(0)
                for i in range(len(todo)):
                    if i + 1 < len(todo):
                        exps(i + 1)
                    if i + 4 < len(todo):
                        query_hi(i + 4)
                    turned_hi_part(i)
                    if layer and i in (4, 5):
                        a = i - 4
                        act.wait_ge(kv_split, 8)
                        src = slice(2 * S + a * 256, 2 * S + a * 256 + 7 * 256)
                        A.activation(Hh[64 * a:64 * a + 64, V2:V2 + 7 * 256], raw32(Rh[64 - 64 * a:128 - 64 * a, src]), ACT.Copy).then_inc(v2_made, 1)

            def mlp(layer):
                b0 = BANK[layer, "w1", 0]
                e0 = EMPTIED[b0 - 1][1]

                def group(g):
                    for i in range(2 * GF):
                        s = slice(i % 2 * HALF, i % 2 * HALF + HALF)
                        act.wait_ge(emptied[0], 24 * g + (e0 + i + 1))
                        if i < 2:
                            act.wait_ge(bank_done, 24 * g + b0)
                        else:
                            act.wait_ge(hid_split, 8 * g + (64 * layer + i - 1))
                        A.activation(tmp[:, 1, s], tmp[:, 0, s], ACT.Square).then_inc(relu_squared, 1)
                        act.wait_ge(relu_squared, 8 * g + (64 * layer + i + 1))
                        A.activation(Rh[:, (i // 2) * S + i % 2 * HALF:(i // 2) * S + i % 2 * HALF + HALF], tmp[:, 1, s],
                                     ACT.Copy).then_inc(hid_hi, 1)
                with act.Fori(0, GROUPS) as g:
                    group(g)

            act.wait_ge(consts_loaded, 16 * 5)
            link(A.activation(sp[:, 0, :], col[:, 7, :], ACT.Abs))
            A.activation(sp[:, 1, :], sp[:, 0, :], ACT.Exp, scale=-1.0).then_inc(lam_exp, 1)
            act.wait_ge(toep_copied, 1)
            act.dma_start(rep.rearrange("(h i r) -> h i r", h=12, i=CHUNK), toep.unsqueeze(1).to_broadcast([12, CHUNK, REL])).then_inc(toep_written, 16)
            h_version(H_MIX0, MIX0)
            memory_std(0)
            memory_hi(0)

            def decay_root(j):
                act.wait_ge(decay_half, j + 1)
                A.activation(tmp[:, 1, :], tmp[:, 1, :], ACT.Sqrt).then_inc(decay_sqrt, 1)

            pending = None
            for kind, j in A_ORDER:
                if kind == "mem":
                    memory_kv_hi(0, (j,))
                if kind == "xr":
                    for h in range(2):
                        s = slice(h * HALF, h * HALF + HALF)
                        act.wait_ge(emptied[0], EMPTIED[BANK[0, "xr", j] + h][1])
                        A.activation(Q[:, j, s], XR[:, 3 + h * HALF:3 + h * HALF + HALF], ACT.Identity,
                                     scale=col[:, 3, j:j + 1], bias=col[:, 4, j:j + 1]).then_inc(conv_seeded, 1)
                        act.wait_ge(conv_ready, 2 * j + h + 1)
                        if j == 2 and h == 0:
                            act.wait_ge(bank_done, LAST[UNIT[0, "mem", 3]])
                        if j >= 3 and h == 0:
                            act.wait_ge(bank_done, LAST[UNIT[0, "G", 2 if j > 3 else 1]])
                        A.activation(Rh[:, (j % 3) * S + h * HALF:(j % 3) * S + h * HALF + HALF], Q[:, j, s], ACT.Copy).then_inc(conv_hi, 1)
                elif kind == "gate":
                    for h in range(2):
                        n, s = 2 * j + h, slice(h * HALF, h * HALF + HALF)
                        act.wait_ge(emptied[0], EMPTIED[BANK[0, "gate", j] + h][1])
                        A.activation(rx[:, 1, :], rx[:, 0, :], ACT.Square).then_inc(gate_squared, 1)
                        act.wait_ge(gate_inner, n + 1)
                        A.activation(rx[:, 1, :], rx[:, 1, :], ACT.Tanh, scale=GELU_C * GELU_A).then_inc(gate_tanh, 1)
                if pending is not None:
                    decay_root(pending)
                    pending = None
                if kind == "G":
                    if j >= 1:
                        act.wait_ge(lru_done, j)
                    if j == 0:
                        act.wait_ge(sp_ready, 1)
                    for h in range(2):
                        for which in range(2):
                            b = BANK[0, "G", j] + 2 * h + which
                            act.wait_ge(bank_done, b + 1)
                            A.activation(tmp[:, 2 * which, h * HALF:h * HALF + HALF], bank[b % 4][:, :], ACT.Tanh, scale=0.5,
                                         bias=col[:, 5 + which, j:j + 1]).then_inc(emptied[1], 1)
                    act.wait_ge(emptied[1], EMPTIED[b][1])
                    A.activation(tmp[:, 1, :], tmp[:, 2, :], ACT.Tanh, scale=sp[:, 4, j:j + 1], bias=sp[:, 4, j:j + 1]).then_inc(decay_tanh, 1)
                    act.wait_ge(decay_tanh, 2 * j + 1)
                    A.activation(tmp[:, 2, :], tmp[:, 2, :], ACT.Exp, scale=sp[:, 5, j:j + 1], bias=sp[:, 5, j:j + 1]).then_inc(decay_tanh, 1)
                    pending = j
            attention(0)
            y_version(H_Y0)
            squares(MLP0, range(14))
            h_version(H_MLP0, MLP0)
            mlp(0)
            squares(MIX1, range(14))
            h_version(H_MIX1, MIX1)
            act.dma_start(memraw[1], memT).then_inc(mem_loaded, 16)
            memory_std(1)
            memory_hi(1)
            act.wait_ge(toep_written, 16)
            for p, pair in enumerate(PAIRS):
                for a, head in enumerate(pair):
                    o = head * CHUNK * REL + CHUNK - 1
                    act.dma_start(bias[64 * a:64 * a + 64, p, :], rep[o:o + CHUNK * (REL - 1)].rearrange(
                        "(i r) -> i r", r=REL - 1)[:, 0:2 * CHUNK]).then_inc(bias_loaded, 16)
            memory_kv_hi(1)
            h_version(H_KV, None)
            for i in range(8):
                s = slice(i * HALF, i * HALF + HALF)
                act.wait_ge(emptied[0], EMPTIED[BANK[1, "K", 0] + i][1])
                A.activation(Rh[:, s], tmp[:, 0, i % 2 * HALF:i % 2 * HALF + HALF], ACT.Copy).then_inc(kv_hi, 1)
            attention(1)
            y_version(H_Y1)
            squares(MLP1, range(14))
            h_version(H_MLP1, MLP1)
            mlp(1)
            squares(FINAL, range(16))
            norm_std(FINAL)

        @block.vector
        def _(dve):
            own = [0]

            def link(ins):
                own[0] += 1
                ins.then_inc(dve_own, 1)
                dve.wait_ge(dve_own, own[0])

            def newton(c):
                link(V.reciprocal(nrm[:, 2, c], nrm[:, 1, c]))
                link(V.tensor_tensor(nrm[:, 3, c], nrm[:, 2, c], nrm[:, 2, c], ALU.mult))
                link(V.tensor_tensor(nrm[:, 3, c], nrm[:, 3, c], nrm[:, 0, c], ALU.mult))
                link(V.tensor_scalar(nrm[:, 3, c], nrm[:, 3, c], -0.5, 1.5, ALU.mult, ALU.add))
                link(V.tensor_tensor(nrm[:, 4, c], nrm[:, 2, c], nrm[:, 3, c], ALU.mult))

            def diagonal(dst, c):
                w = c.stop - c.start
                return V.tensor_tensor(dst.rearrange("p (j t) -> p j t", t=P), ident[:, :].unsqueeze(1).to_broadcast([P, w, P]),
                                       nrm[:, 4, c].unsqueeze(2).to_broadcast([P, w, P]), ALU.mult)

            def norm_finish(n):
                dve.wait_ge(colsum_done, n + 1)
                V.tensor_scalar(nrm[:, 0, TOK], bank[4][:, 0:8], 1.0 / D, EPS, ALU.mult, ALU.add).then_inc(var_ready, 1)
                dve.wait_ge(std_ready, n + 1)
                newton(TOK)
                diagonal(tmp[:, 2, :], TOK).then_inc(diag_ready, 1)
                dve.wait_ge(bcast_done, n + 1)
                for h in range(2):
                    link(V.tensor_copy(rstd[:, h * HALF:h * HALF + HALF], bank[5 + h][:, :]))

            def memory_stats(layer):
                dve.wait_ge(mem_colsum, layer + 1)
                V.tensor_scalar(nrm[:, 0, MEMC], bank[7][:, 0:2], 1.0 / D, EPS, ALU.mult, ALU.add).then_inc(mem_var, 1)
                dve.wait_ge(mem_std, layer + 1)
                newton(MEMC)
                diagonal(memsq[layer][1][:, 0:MEM], MEMC).then_inc(mem_diag, 1)

            def memory_scale(layer):
                mem = memraw[layer]
                dve.wait_ge(mem_bcast, layer + 1)
                for k in range(KT):
                    ks = slice(k * MEM, k * MEM + MEM)
                    last = V.scalar_tensor_tensor(mem[:, ks], mem[:, ks], gain[:, 0, k:k + 1], bank[7][:, 0:MEM], ALU.mult, ALU.mult)
                last.then_inc(mem_normed, 1)

            def memory_lo(layer):
                dve.wait_ge(mem_hi, layer + 1)
                rs = slice(MEMR[layer], MEMR[layer] + 2 * S)
                V.tensor_tensor(Rl[:, rs], memraw[layer], raw32(Rh[:, rs]), ALU.subtract).then_inc(mem_ready, 1)

            def add_square(version, i):
                n = 16 * version + i
                h = i % 2
                dst, sq = tmp[:, 2, h * HALF:h * HALF + HALF], tmp[:, 1, h * HALF:h * HALF + HALF]
                dve.wait_ge(x_squared, n + 1)
                if i < 2:
                    ins = V.tensor_copy(dst, sq)
                else:
                    dve.wait_ge(sq_added, n - 1)
                    ins = V.tensor_tensor(dst, dst, sq, ALU.add)
                ins.then_inc(sq_added, 1)

            def h_lo_tiles(v, ks):
                for k in ks:
                    dve.wait_ge(h_hi, 8 * v + k + 1)
                    V.scalar_tensor_tensor(Hl[:, hb(k, 0, S)], X[:, k, :], gain[:, GAIN_OF[v], k:k + 1], raw32(Hh[:, hb(k, 0, S)]),
                                           ALU.mult, ALU.subtract).then_inc(h_ready, 1)

            def h_version(v, norm):
                if norm == MIX0:
                    for k in range(KT):
                        add_square(MIX0, 2 * k)
                        add_square(MIX0, 2 * k + 1)
                        h_lo_tiles(v, (k,))
                elif norm is not None:
                    h_lo_tiles(v, range(2))
                    add_square(norm, 14)
                    add_square(norm, 15)
                    h_lo_tiles(v, range(2, KT))
                else:
                    h_lo_tiles(v, range(KT))

            def y_version(v):
                for k in range(KT):
                    dve.wait_ge(h_hi, 8 * v + k + 1)
                    V.tensor_tensor(Hl[:, hb(k, 0, S)], Q[:, k, :], raw32(Hh[:, hb(k, 0, S)]), ALU.subtract).then_inc(h_ready, 1)

            def memory_kv_lo(layer, which):
                for i in which:
                    b = BANK[layer, "mem", i]
                    dve.wait_ge(mkv_hi, 4 * layer + i + 1)
                    if i < 2:
                        for a in range(2):
                            ps, cs = slice(64 * a, 64 * a + 64), slice(256 * a, 256 * a + 256)
                            last = V.tensor_tensor(mkl[ps, i, cs], bank[b % 4][ps, 0:MEM], raw32(mkh[ps, i, cs]), ALU.subtract)
                    else:
                        last = V.tensor_tensor(mvl[:, i - 2, :], bank[b % 4][:, 0:256], raw32(mvh[:, i - 2, :]), ALU.subtract)
                    last.then_inc(emptied[0], 1)

            def evict(layer, kind, i, h):
                b = BANK[layer, kind, i] + h
                dve.wait_ge(bank_done, b + 1)
                return bank[b % 4]

            def wout(layer):
                version = (MLP0, MLP1)[layer]
                for i in range(16):
                    n, h = i // 2, i % 2
                    s = slice(h * HALF, h * HALF + HALF)
                    pb = evict(layer, "wout", n, h)
                    V.tensor_tensor(X[:, n, s], X[:, n, s], pb[:, :], ALU.add).then_inc(emptied[0], 1)
                    if 1 <= i < 15:
                        add_square(version, i - 1)

            def mlp(layer):
                b0 = BANK[layer, "w1", 0]
                version = (MIX1, FINAL)[layer]

                def hidden_lo(g, i):
                    s = slice((i // 2) * S + i % 2 * HALF, (i // 2) * S + i % 2 * HALF + HALF)
                    dve.wait_ge(hid_hi, 8 * g + (64 * layer + i + 1))
                    V.tensor_tensor(Rl[:, s], tmp[:, 1, i % 2 * HALF:i % 2 * HALF + HALF], raw32(Rh[:, s]), ALU.subtract).then_inc(hid_split, 1)

                def group(g, last_group):
                    for i in range(2 * GF):
                        s = slice(i % 2 * HALF, i % 2 * HALF + HALF)
                        dve.wait_ge(bank_done, 24 * g + (b0 + i + 1))
                        if i >= 2:
                            dve.wait_ge(relu_squared, 8 * g + (64 * layer + i - 1))
                        V.scalar_tensor_tensor(tmp[:, 0, s], bank[(b0 + i) % 4][:, :], 0.0, rstd[:, s], ALU.max, ALU.mult).then_inc(emptied[0], 1)
                        if i >= 1:
                            hidden_lo(g, i - 1)
                    hidden_lo(g, 2 * GF - 1)
                    for i in range(16):
                        s = slice(i % 2 * HALF, i % 2 * HALF + HALF)
                        dve.wait_ge(bank_done, 24 * g + (b0 + 8 + i + 1))
                        V.tensor_tensor(X[:, i // 2, s], X[:, i // 2, s], bank[(b0 + i) % 4][:, :], ALU.add).then_inc(emptied[0], 1)
                        if last_group and 1 <= i < 15:
                            add_square(version, i - 1)
                with dve.Fori(0, GROUPS - 1) as g:
                    group(g, False)
                group(GROUPS - 1, True)

            def attention(layer):
                todo, s0 = steps(layer), STEP0[layer]

                def maxima(i):
                    kind, t, c = todo[i]
                    n = s0 + i
                    dve.wait_ge(score_done, n + 1)
                    st = stat[:, i % 4]
                    if kind == "mem":
                        link(V.tensor_reduce(st[:, 0, 0:2], pS[i % 4][:, :].rearrange("p (a m) -> p a m", a=2), AX.X, ALU.max))
                        V.tensor_scalar(st[:, 1, 0:2], st[:, 0, 0:2], -SCALE, None, ALU.mult).then_inc(max_ready, 1)
                    else:
                        if todo[i - 1][0] == "mem":
                            dve.wait_ge(bias_loaded, 16 * 12)
                        s = tmp[:, i % 3, HALF:2 * HALF].rearrange("p (j m) -> p j m", j=4)
                        ps = pS[i % 4][:, :].rearrange("p (j m) -> p j m", j=4)
                        j0 = 0
                        if c == 0:
                            V.scalar_tensor_tensor(s[:, 0, 0:CHUNK], ps[:, 0, 0:CHUNK], SCALE, bias[:, t, CHUNK:2 * CHUNK], ALU.mult, ALU.add)
                            V.memset(s[:, 0, CHUNK:2 * CHUNK], NEG)
                            j0 = 1
                        link(V.scalar_tensor_tensor(s[:, j0:4, :], ps[:, j0:4, :], SCALE,
                                                    bias[:, t, :].unsqueeze(1).to_broadcast([P, 4 - j0, P]), ALU.mult, ALU.add))
                        link(V.tensor_reduce(st[:, 0, :], s, AX.X, ALU.max))
                        V.tensor_scalar(st[:, 1, :], st[:, 0, :], sink[:, t:t + 1], -1.0, ALU.max, ALU.mult).then_inc(max_ready, 1)

                def denominators(i):
                    kind, t, c = todo[i]
                    st, g = stat[:, i % 4], 2 if kind == "mem" else 4
                    dve.wait_ge(exp_done, s0 + i + 1)
                    if kind == "swa":
                        link(V.tensor_tensor(st[:, 2, :], st[:, 2, :], st[:, 3, :], ALU.add))
                    V.reciprocal(st[:, 4, 0:g], st[:, 2, 0:g]).then_inc(denom_ready, 1)

                def turned_lo_part(i):
                    dve.wait_ge(turned_hi, s0 + i + 1)
                    s = slice(PT + i % 3 * 512, PT + i % 3 * 512 + 512)
                    V.tensor_tensor(Hl[:, s], pT[i % 2][:, :], raw32(Hh[:, s]), ALU.subtract).then_inc(turned_split, 1)

                def take_out(i):
                    kind, t, c = todo[i]
                    dve.wait_ge(pv_done, s0 + i + 1)
                    for a in range(2):
                        ps = slice(64 * a, 64 * a + 64)
                        if kind == "mem":
                            last = V.tensor_copy(Q[ps, 6 + t, c * P:c * P + P], pO[i % 2][ps, a * P:a * P + P])
                        else:
                            last = V.tensor_copy(Q[ps, t, c * 256:c * 256 + 256].rearrange("p (j t) -> p j t", j=4),
                                                 pO[i % 2][ps, :].rearrange("p (j b t) -> p j b t", j=4, b=2)[:, :, a, :])
                    last.then_inc(att_out, 1)

                maxima(0)
                maxima(1)
                for i in range(len(todo)):
                    denominators(i)
                    if i + 2 < len(todo):
                        maxima(i + 2)
                    if i >= 1:
                        turned_lo_part(i - 1)
                    if i >= 2:
                        take_out(i - 2)
                    if layer and i in (4, 5):
                        a = i - 4
                        dve.wait_ge(kv_split, 8)
                        src = slice(2 * S + a * 256, 2 * S + a * 256 + 7 * 256)
                        V.tensor_copy(Hl[64 * a:64 * a + 64, V2:V2 + 7 * 256], raw32(Rl[64 - 64 * a:128 - 64 * a, src])).then_inc(v2_made, 1)
                turned_lo_part(len(todo) - 1)
                take_out(len(todo) - 2)
                take_out(len(todo) - 1)

            dve.wait_ge(toep_done, 1)
            V.tensor_copy(toep, bank[7][0:12, 0:REL]).then_inc(toep_copied, 1)
            dve.wait_ge(lam_exp, 1)
            link(V.tensor_scalar(sp[:, 0, :], sp[:, 1, :], 2.0, None, ALU.add))
            link(V.reciprocal(sp[:, 0, :], sp[:, 0, :]))
            link(V.tensor_tensor(sp[:, 2, :], sp[:, 1, :], sp[:, 0, :], ALU.mult))
            link(V.tensor_tensor(sp[:, 3, :], sp[:, 2, :], sp[:, 2, :], ALU.mult))
            link(V.memset(sp[:, 4, :], 1.0 / 17.0))
            for d in (15, 13, 11, 9, 7, 5, 3, 1):
                link(V.tensor_tensor(sp[:, 4, :], sp[:, 4, :], sp[:, 3, :], ALU.mult))
                link(V.tensor_scalar(sp[:, 4, :], sp[:, 4, :], 1.0 / d, None, ALU.add))
            link(V.tensor_tensor(sp[:, 4, :], sp[:, 4, :], sp[:, 2, :], ALU.mult))
            link(V.tensor_scalar(sp[:, 5, :], col[:, 7, :], -1.0, 0.0, ALU.mult, ALU.max))
            link(V.scalar_tensor_tensor(sp[:, 6, :], sp[:, 4, :], 2.0, sp[:, 5, :], ALU.mult, ALU.add))
            link(V.tensor_scalar(sp[:, 4, :], sp[:, 6, :], 2.0, None, ALU.mult))
            link(V.tensor_scalar(sp[:, 5, :], sp[:, 6, :], -4.0, None, ALU.mult))
            V.tensor_scalar(col[:, 5:7, :], col[:, 5:7, :], 0.5, None, ALU.mult).then_inc(sp_ready, 1)
            h_version(H_MIX0, MIX0)
            norm_finish(MIX0)
            memory_stats(0)
            memory_scale(0)
            dve.wait_ge(toep_written, 16)

            def decay_chain(j):
                th_x, root, a = tmp[:, 0, :], tmp[:, 1, :], tmp[:, 2, :]
                dve.wait_ge(decay_tanh, 2 * j + 2)
                link(V.scalar_tensor_tensor(a, a, 1.0, root, ALU.add, ALU.mult))
                V.tensor_scalar(a, a, -1.0, 1.0, ALU.mult, ALU.add).then_inc(decay_half, 1)
                link(V.scalar_tensor_tensor(th_x, th_x, 1.0, Q[:, j, :], ALU.add, ALU.mult))
                dve.wait_ge(decay_sqrt, j + 1)
                link(V.scalar_tensor_tensor(root, a, 1.0, root, ALU.add, ALU.mult))
                link(V.scalar_tensor_tensor(th_x, root, 0.5, th_x, ALU.mult, ALU.mult))
                V.tensor_tensor_scan(Q[:, j, :], a, th_x, 0.0, ALU.mult, ALU.add).then_inc(lru_done, 1)

            pending = None
            for kind, j in A_ORDER:
                if kind == "mem":
                    if j == 0:
                        memory_lo(0)
                    memory_kv_lo(0, (j,))
                for h in range(2):
                    s = slice(h * HALF, h * HALF + HALF)
                    if kind in ("G", "mem"):
                        continue
                    pb = evict(0, kind, j, h)
                    if kind == "qm":
                        V.tensor_tensor(Q[:, 6 + j, s], pb[:, :], rstd[:, s], ALU.mult).then_inc(emptied[0], 1)
                    elif kind == "xr":
                        V.tensor_tensor(XR[:, 3 + h * HALF:3 + h * HALF + HALF], pb[:, :], rstd[:, s], ALU.mult).then_inc(emptied[0], 1)
                        dve.wait_ge(conv_seeded, 2 * j + h + 1)
                        for tap in range(3):
                            xs = XR[:, tap + h * HALF:tap + h * HALF + HALF]
                            ins = V.scalar_tensor_tensor(Q[:, j, s], xs, col[:, tap, j:j + 1], Q[:, j, s], ALU.mult, ALU.add)
                            if tap < 2:
                                link(ins)
                        ins.then_inc(conv_ready, 1)
                        dve.wait_ge(conv_hi, 2 * j + h + 1)
                        rs = slice((j % 3) * S + h * HALF, (j % 3) * S + h * HALF + HALF)
                        V.tensor_tensor(Rl[:, rs], Q[:, j, s], raw32(Rh[:, rs]), ALU.subtract).then_inc(conv_split, 1)
                    else:
                        n = 2 * j + h
                        g, t = rx[:, 0, :], rx[:, 1, :]
                        V.tensor_tensor(g, pb[:, :], rstd[:, s], ALU.mult).then_inc(emptied[0], 1)
                        dve.wait_ge(gate_squared, n + 1)
                        V.scalar_tensor_tensor(t, t, 1.0 / GELU_A, g, ALU.add, ALU.mult).then_inc(gate_inner, 1)
                        dve.wait_ge(gate_tanh, n + 1)
                        link(V.scalar_tensor_tensor(t, t, 1.0, g, ALU.add, ALU.mult))
                        dve.wait_ge(lru_done, j + 1)
                        V.scalar_tensor_tensor(Q[:, j, s], t, 0.5, Q[:, j, s], ALU.mult, ALU.mult).then_inc(y_done, 1)
                        dve.wait_ge(y_done, n + 1)
                if pending is not None:
                    decay_chain(pending)
                    pending = None
                if kind == "G":
                    pending = j
            attention(0)
            y_version(H_Y0)
            wout(0)
            h_version(H_MLP0, MLP0)
            norm_finish(MLP0)
            mlp(0)
            h_version(H_MIX1, MIX1)
            norm_finish(MIX1)

            def queries(kind, i, tile):
                for h in range(2):
                    s = slice(h * HALF, h * HALF + HALF)
                    pb = evict(1, kind, i, h)
                    V.tensor_tensor(Q[:, tile, s], pb[:, :], rstd[:, s], ALU.mult).then_inc(emptied[0], 1)
            for kind, i in B_ORDER[:12]:
                if kind == "mem":
                    memory_kv_lo(1, (i,))
                else:
                    queries(kind, i, i if kind == "q" else 6 + i)
                if (kind, i) == ("q", 2):
                    memory_stats(1)
                    memory_scale(1)
                if (kind, i) == ("q", 3):
                    memory_lo(1)
            h_version(H_KV, None)
            for i in range(9):
                if i < 8:
                    b = BANK[1, "K", 0] + i
                    t = tmp[:, 0, i % 2 * HALF:i % 2 * HALF + HALF]
                    dve.wait_ge(bank_done, b + 1)
                    if i >= 2:
                        dve.wait_ge(kv_split, i - 1)
                    if i < 4:
                        V.tensor_tensor(t, bank[b % 4][:, :], rstd[:, i % 2 * HALF:i % 2 * HALF + HALF], ALU.mult).then_inc(emptied[0], 1)
                    else:
                        V.tensor_tensor(t.rearrange("p (a d) -> p a d", a=2), bank[b % 4][:, :].rearrange("p (a d) -> p a d", a=2),
                                        nrm[:, 4, 2 * i - 8:2 * i - 6].unsqueeze(2).to_broadcast([P, 2, 256]), ALU.mult).then_inc(emptied[0], 1)
                if i >= 1:
                    s = slice((i - 1) * HALF, i * HALF)
                    dve.wait_ge(kv_hi, i)
                    V.tensor_tensor(Rl[:, s], tmp[:, 0, (i - 1) % 2 * HALF:(i - 1) % 2 * HALF + HALF], raw32(Rh[:, s]), ALU.subtract).then_inc(kv_split, 1)
            attention(1)
            y_version(H_Y1)
            wout(1)
            h_version(H_MLP1, MLP1)
            norm_finish(MLP1)
            mlp(1)
            add_square(FINAL, 14)
            add_square(FINAL, 15)
            norm_finish(FINAL)
            for n in range(KT):
                V.scalar_tensor_tensor(X[:, n, :], X[:, n, :], gain[:, 6, n:n + 1], rstd[:, :], ALU.mult, ALU.mult).then_inc(final_ready, 1)


def _buckets():
    n = -(np.arange(REL) - (2 * CHUNK - 1))
    half, exact = 16, 8
    out = (n < 0).astype(np.int32) * half
    n = np.abs(n)
    large = exact + (np.log(np.maximum(n, 1) / exact) / np.log(128 / exact) * (half - exact)).astype(np.int32)
    return out + np.where(n < exact, n, np.minimum(large, half - 1))


def _columns(w, tiles=None):
    k, n = w.shape
    return np.ascontiguousarray(w.reshape(k // P, P, n // P, P).transpose(2, 1, 0, 3)).reshape(n // P, P, k)


def _units(x):
    parts = {}
    heads = np.concatenate([np.arange(h * HEAD, h * HEAD + HEAD) for pair in PAIRS for h in pair])
    out_rows = np.concatenate([heads, np.arange(LRU, D)])
    a_in = _columns(x["a_w_in"][0])
    b_in = _columns(np.concatenate([x["b_w_in"][0][:, heads], x["b_w_in"][0][:, LRU:]], axis=1))

    def rows(w):
        return w.reshape(2, 4, P, 256).transpose(0, 2, 1, 3).reshape(2, P, 1024)
    for i in range(6):
        parts[0, "gate", i], parts[0, "xr", i], parts[1, "q", i] = a_in[i], a_in[6 + i], b_in[i]
        unit = np.zeros((P, 8, P), np.float32)
        ks = GATE_K[i % 3]
        for which, name in enumerate(("a_gx_w", "a_ga_w")):
            for n, k in enumerate(ks):
                r0, c0 = (i - i % 3 + k) * P, i * P
                for blk in range(8):
                    lo, hi = blk * GB, blk * GB + GB
                    ra, rb, ca, cb = max(lo, r0), min(hi, r0 + P), max(lo, c0), min(hi, c0 + P)
                    if ra < rb and ca < cb:
                        unit[ra - r0:rb - r0, which * len(ks) + n, ca - c0:cb - c0] = x[name][0, blk, ra - lo:rb - lo, ca - lo:cb - lo]
        parts[0, "G", i] = unit.reshape(P, 1024)
    for i in range(2):
        parts[0, "qm", i], parts[1, "qm", i] = a_in[12 + i], b_in[6 + i]
    kv = x["w_kv_shared"]
    k_units, v_units = _columns(kv[:, :256]), rows(kv[:, 256:])
    for i in range(2):
        parts[1, "K", i], parts[1, "V", i] = k_units[i], v_units[i]
    for layer in range(2):
        m = x["w_mem_kv"][layer]
        mk, mv = _columns(m[:, :256]), rows(m[:, 256:])
        wo = _columns(x["w_out"][layer][out_rows] if layer else x["w_out"][layer])
        w1 = _columns(x["w1"][layer])
        w2 = x["w2"][layer].reshape(GROUPS, GF, P, 4, 2, P).transpose(0, 3, 2, 4, 1, 5).reshape(4 * GROUPS, P, 1024)
        for i in range(2):
            parts[layer, "mem", i], parts[layer, "mem", 2 + i] = mk[i], mv[i]
        for i in range(8):
            parts[layer, "wout", i] = wo[i]
        for i in range(32):
            parts[layer, "w1", i], parts[layer, "w2", i] = w1[i], w2[i]
    return np.stack([parts[key] for key in ORDER])


def _tiles(v, n):
    return v.reshape(n, P).T


def kernel(**inputs):
    import concourse.bacc as bacc
    from concourse.bass_utils import run_bass_kernel_spmd

    x = {k: np.asarray(v) for k, v in inputs.items()}
    gains = [x["mem_norm_g"], x["mix_norm_g"][0], x["mix_norm_g"][1], x["mlp_norm_g"][0], x["mlp_norm_g"][1], x["kv_norm_g"], x["final_norm_g"]]
    cols = [*x["a_conv_w"][0], x["a_conv_b"][0], x["a_gx_b"][0], x["a_ga_b"][0], x["a_lambda"][0]]
    onehot = (_buckets()[None, :] == np.arange(32)[:, None]).astype(np.float32)
    arrays = {
        "xT": x["x"][0].T.reshape(KT, P, S).transpose(1, 0, 2),
        "memT": x["mem"][0].T.reshape(KT, P, MEM).transpose(1, 0, 2).reshape(P, KT * MEM),
        "gains": np.stack([_tiles(g, KT) for g in gains], axis=1),
        "cols": np.stack([_tiles(c, LT) for c in cols], axis=1),
        "sinkc": np.repeat(x["b_sinks"][0][np.array(PAIRS)].T, CHUNK, axis=0),
        "relb": x["rel_bias"],
        "onehot": onehot,
        "wst": _units(x),
    }
    nc = bacc.Bacc("TRN2", target_bir_lowering=False, num_devices=1, dynamic_dma_scratch_size=1024)
    f32 = mybir.dt.float32
    arrays = {k: np.ascontiguousarray(v) for k, v in arrays.items()}
    aps = {k: nc.dram_tensor(k, v.shape, f32, kind="ExternalInput").ap() for k, v in arrays.items()}
    rep = nc.dram_tensor("rep", (12 * CHUNK * REL,), f32).ap()
    outT = nc.dram_tensor("outT", (P, KT, S), f32, kind="ExternalOutput").ap()
    trunk(nc, rep=rep, outT=outT, **aps)
    r = run_bass_kernel_spmd(nc, [arrays], core_ids=[0])
    return np.ascontiguousarray(r.results[0]["outT"].transpose(1, 0, 2).reshape(D, S).T)[None]
```

```python
import numpy as np
import concourse.bass as bass
from concourse import mybir
from concourse.alu_op_type import AluOpType as ALU
from contextlib import ExitStack

D, S, P, HALF = 1024, 1024, 128, 512
KT = D // P
HEAD, MEM, CHUNK = 64, 256, 64
LRU, LT = 768, 6
GB = 96
FF, GF = 4096, 4
GROUPS = FF // P // GF
EPS = 1e-6
SCALE = HEAD ** -0.5
GELU_A, GELU_C = 0.044715, float(np.sqrt(2.0 / np.pi))
PAIRS = [(0, 3), (1, 4), (2, 5), (6, 9), (7, 10), (8, 11)]
GATE_K = [(0, 1), (0, 1, 2), (1, 2)]
REL = 2 * CHUNK + CHUNK - 1

A_ORDER = ([("xr", 0), ("xr", 1), ("qm", 0), ("mem", 0), ("mem", 1), ("xr", 2), ("mem", 2), ("mem", 3), ("G", 0), ("qm", 1), ("G", 1),
            ("xr", 3), ("G", 2), ("xr", 4), ("xr", 5), ("G", 3), ("gate", 0), ("G", 4), ("gate", 1), ("G", 5)]
           + [("gate", j) for j in range(2, 6)])
B_ORDER = [("q", 0), ("q", 1), ("mem", 0), ("q", 2), ("mem", 1), ("q", 3), ("mem", 2), ("mem", 3), ("q", 4), ("q", 5),
           ("qm", 0), ("qm", 1), ("K", 0), ("K", 1), ("V", 0), ("V", 1)]
MLP_ORDER = [x for g in range(GROUPS) for x in [("w1", 4 * g + i) for i in range(4)] + [("w2", 4 * g + i) for i in range(4)]]
ORDER = ([(0, *x) for x in A_ORDER] + [(0, "wout", n) for n in range(8)] + [(0, *x) for x in MLP_ORDER]
         + [(1, *x) for x in B_ORDER] + [(1, "wout", n) for n in range(8)] + [(1, *x) for x in MLP_ORDER])
NBANKS = {"mem": 1, "G": 4, "w2": 4}
UNIT, BANK, LAST = {}, {}, []
_b = 0
for _u, _key in enumerate(ORDER):
    UNIT[_key], BANK[_key] = _u, _b
    _b += NBANKS.get(_key[1], 2)
    LAST.append(_b)
NU, NB = len(ORDER), _b
LAST[UNIT[1, "V", 0]] = LAST[UNIT[1, "V", 1]]
EMPTIED = []
_n = [0, 0]
for _key in ORDER:
    for _ in range(NBANKS.get(_key[1], 2)):
        _a = int(_key[1] == "G")
        _n[_a] += 1
        EMPTIED.append((_a, _n[_a]))


def trunk(nc, xT, memT, gains, cols, sinkc, relb, onehot, wst, rep, memn, outT):
    f32, f32r = mybir.dt.float32, mybir.dt.float32r
    ACT, AX = mybir.ActivationFunctionType, mybir.AxisListType
    V, A, T, G = nc.vector, nc.scalar, nc.tensor, nc.gpsimd
    ctx = ExitStack()
    with ctx:
        def sb(name, shape, dt=f32):
            return ctx.enter_context(nc.sbuf_tensor(name, shape, dt))

        def sem(name):
            return ctx.enter_context(nc.semaphore(name))

        X = sb("X", [P, KT, S])
        Hh, Hl = sb("Hh", [P, KT * S], f32r), sb("Hl", [P, KT * S], f32r)
        raw = sb("raw", [P, 2, 1024])
        wh, wl = sb("wh", [P, 2, 1024], f32r), sb("wl", [P, 2, 1024], f32r)
        Rh, Rl = sb("Rh", [P, 4 * S], f32r), sb("Rl", [P, 4 * S], f32r)
        Q = sb("Q", [P, 8, S])
        XR = sb("XR", [P, 3 + S])
        mkh, mkl = sb("mkh", [P, 2, 512], f32r), sb("mkl", [P, 2, 512], f32r)
        mvh, mvl = sb("mvh", [P, 2, 256], f32r), sb("mvl", [P, 2, 256], f32r)
        mqh, mql = sb("mqh", [P, 2, P], f32r), sb("mql", [P, 2, P], f32r)
        rstd = sb("rstd", [P, S])
        tmp = sb("tmp", [P, 3, 1024])
        ident, ones = sb("ident", [P, P]), sb("ones", [P, P])
        gain = sb("gain", [P, 7, KT])
        col = sb("col", [P, 8, LT])
        sink = sb("sink", [P, 6])
        nrm = sb("nrm", [P, 5, 10])
        sp = sb("sp", [P, 8, LT])
        stat = sb("stat", [P, 4, 5, 4])
        zero = sb("zero", [P, 1])
        relsb = sb("relsb", [32, 12])
        onesb = Q[0:32, 0, 0:REL]
        toep = Q[0:12, 1, 0:REL]
        rx = XR[:, 3:3 + S].rearrange("p (a t) -> p a t", a=2)
        memraw = [Q[:, 6:8, :].rearrange("p a t -> p (a t)"), tmp[:, 0:2, :].rearrange("p a t -> p (a t)")]
        MEMR = [2 * S, 0]
        memsq, memdiag = tmp[:, 0, :], XR[:, 3:3 + S]
        bias = XR[:, 0:6 * P].rearrange("p (a j) -> p a j", a=6)

        bank = [ctx.enter_context(nc.psum_tensor(f"bank{i}", [P, HALF], f32)) for i in range(8)]
        pS, pT, pO = [bank[i] for i in (4, 5, 0, 1)], [bank[6], bank[2]], [bank[7], bank[3]]

        gain_loaded, col_loaded = sem("gain_loaded"), sem("col_loaded")
        consts_loaded, mem_loaded, out_written = sem("consts_loaded"), sem("mem_loaded"), sem("out_written")
        x_loaded = [sem(f"x_loaded{k}") for k in range(KT)]
        consts_made, zeros_made = sem("consts_made"), sem("zeros_made")
        raw_loaded = [sem("raw_loaded0"), sem("raw_loaded1")]
        unit_hi, unit_split = sem("unit_hi"), sem("unit_split")
        bank_done = sem("bank_done")
        emptied = [sem("emptied_vector"), sem("emptied_scalar")]
        dve_own, act_own = sem("dve_own"), sem("act_own")
        colsum_done, var_ready, std_ready, diag_ready, bcast_done = (
            sem(n) for n in ("colsum_done", "var_ready", "std_ready", "diag_ready", "bcast_done"))
        mem_written = sem("mem_written")
        mem_sq, mem_ssq, mem_colsum, mem_var, mem_std, mem_diag, mem_bcast = (
            sem(n) for n in ("mem_sq", "mem_ssq", "mem_colsum", "mem_var", "mem_std", "mem_diag", "mem_bcast"))
        x_squared, sq_added = sem("x_squared"), sem("sq_added")
        h_hi, h_ready = sem("h_hi"), sem("h_ready")
        h_used = sem("h_used")
        mem_normed, mem_hi, mem_ready = sem("mem_normed"), sem("mem_hi"), sem("mem_ready")
        mkv_hi, mem_half = sem("mkv_hi"), sem("mem_half")
        lam_exp, conv_seeded, conv_ready, conv_hi, conv_split = (
            sem(n) for n in ("lam_exp", "conv_seeded", "conv_ready", "conv_hi", "conv_split"))
        sp_ready = sem("sp_ready")
        decay_tanh, decay_half, decay_sqrt, lru_done = sem("decay_tanh"), sem("decay_half"), sem("decay_sqrt"), sem("lru_done")
        gate_squared, gate_inner, gate_tanh, y_done = (
            sem(n) for n in ("gate_squared", "gate_inner", "gate_tanh", "y_done"))
        bias_hi, bias_split = sem("bias_hi"), sem("bias_split")
        toep_done, toep_copied, toep_written, bias_loaded = (sem(n) for n in ("toep_done", "toep_copied", "toep_written", "bias_loaded"))
        kv_hi, kv_split, v2_made = sem("kv_hi"), sem("kv_split"), sem("v2_made")
        q_hi, q_split, score_done, max_ready, exp_done, denom_ready, prob_ready, turned, turned_hi, turned_split, pv_done, att_out = (
            sem(n) for n in ("q_hi", "q_split", "score_done", "max_ready", "exp_done", "denom_ready", "prob_ready", "turned",
                             "turned_hi", "turned_split", "pv_done", "att_out"))
        relu_squared, hid_hi, hid_split = sem("relu_squared"), sem("hid_hi"), sem("hid_split")
        rstd_ready, gain_applied = sem("rstd_ready"), sem("gain_applied")
        final_ready = [sem("final_ready_vector"), sem("final_ready_gpsimd")]
        block = ctx.enter_context(nc.Block())

        def hb(k, lo, n):
            return slice(k * S + lo, k * S + lo + n)

        TOK, MEMC = slice(0, 8), slice(8, 10)

        def raw32(ap):
            return ap.bitcast(f32)

        V2 = 0
        QS = 1792
        QB = 2304
        PT = 4352
        BS = 5888
        ID = 6656

        def query_at(kind, i):
            if kind == "mem" and i % 4 < 2:
                return mqh[:, i % 4, :], mql[:, i % 4, :]
            if kind == "mem":
                s = slice(QS + i % 2 * P, QS + i % 2 * P + P)
                return Hh[:, s], Hl[:, s]
            s = slice(QB + i % 4 * 512, QB + i % 4 * 512 + 512)
            return Hh[:, s], Hl[:, s]

        def head_part(q, a):
            return q.rearrange("p (j b t) -> p j b t", j=4, b=2)[:, :, a, :]

        NMEM, NSWA = 16, 24
        STEP0 = [0, NMEM]
        def steps(layer):
            out = [("mem", i // 8, i % 8) for i in range(NMEM)]
            if layer:
                out += [("swa", i // 4, i % 4) for i in range(NSWA)]
            return out
        MIX0, MLP0, MIX1, MLP1, FINAL = range(5)
        UPDATES = {MLP0: BANK[0, "wout", 0], MIX1: BANK[0, "w2", 28], MLP1: BANK[1, "wout", 0], FINAL: BANK[1, "w2", 28]}
        FINAL_V = 5
        H_MIX0, H_Y0, H_MLP0, H_MIX1, H_KV, H_Y1, H_MLP1 = range(7)
        GAIN_OF = {H_MIX0: 1, H_MLP0: 3, H_MIX1: 2, H_KV: 5, H_MLP1: 4}
        H_FREE = {H_Y0: BANK[0, "wout", 0], H_MLP0: BANK[0, "w1", 0], H_MIX1: BANK[0, "w2", 28],
                  H_KV: BANK[1, "K", 0], H_Y1: BANK[1, "wout", 0], H_MLP1: BANK[1, "w1", 0]}
        Y_ORDER = {H_Y0: (0, 2, 3, 1, 4, 5, 6, 7), H_Y1: (7, 6, 3, 0, 1, 2, 4, 5)}
        BEHIND = [H_MLP0, H_KV, H_MLP1]

        @block.sync
        def _(sync):
            sync.dma_start(raw[:, 0, :], wst[0]).then_inc(raw_loaded[0], 16)
            for k in range(KT):
                sync.dma_start(X[:, k, :], xT[:, k, :]).then_inc(x_loaded[k], 16)
                if k == 2:
                    sync.dma_start(raw[:, 1, :], wst[1]).then_inc(raw_loaded[1], 16)
            sync.dma_start(memraw[0], memT).then_inc(mem_loaded, 16)
            with sync.Fori(1, NU // 2) as i:
                for s in range(2):
                    sync.wait_ge(unit_split, 4 * i + 2 * s - 2)
                    sync.dma_start(raw[:, s, :], wst[2 * i + s]).then_inc(raw_loaded[s], 16)
            for h in range(2):
                for n in (0, 5, 1, 2, 6, 3, 7, 4):
                    if n < FINAL_V:
                        sync.wait_ge(final_ready[0], FINAL_V * h + n + 1)
                    else:
                        sync.wait_ge(final_ready[1], (KT - FINAL_V) * h + n - FINAL_V + 1)
                    s = slice(h * HALF, h * HALF + HALF)
                    sync.dma_start(outT[:, n, s], X[:, n, s]).then_inc(out_written, 16)
            sync.wait_ge(out_written, 16 * 2 * KT)

        @block.gpsimd
        def _(pool):
            G.memset(ident[:, :], 0.0).then_inc(consts_made, 1)
            G.memset(ones[:, :], 1.0).then_inc(consts_made, 1)
            G.memset(XR[:, 0:3], 0.0).then_inc(consts_made, 1)
            G.memset(raw32(mkh[:, :, :]), 0.0).then_inc(consts_made, 1)
            G.memset(raw32(mkl[:, :, :]), 0.0).then_inc(consts_made, 1)
            G.memset(zero[:, :], 0.0).then_inc(consts_made, 1)
            pool.wait_ge(consts_made, 6)
            G.affine_select(out=ident[:, :], in_=ident[:, :], compare_op=ALU.not_equal, fill=1.0, base=0,
                            pattern=[[-1, P]], channel_multiplier=1).then_inc(consts_made, 1)

            def split(s, loaded, n, used, of=bank_done):
                pool.wait_ge(raw_loaded[s], loaded)
                if used is not None:
                    pool.wait_ge(of, used)
                for half in range(2):
                    cs = slice(half * HALF, half * HALF + HALF)
                    G.tensor_tensor(wh[:, s, cs], raw[:, s, cs], zero[:, :].to_broadcast([P, HALF]), ALU.add).then_inc(unit_hi, 1)
                    pool.wait_ge(unit_hi, n + (half - 1))
                    G.tensor_tensor(wl[:, s, cs], raw[:, s, cs], raw32(wh[:, s, cs]), ALU.subtract).then_inc(unit_split, 1)

            def memory_squares():
                one, two, mem = memsq, memdiag, memraw[0]
                pool.wait_ge(mem_loaded, 16)
                G.tensor_tensor(one, mem[:, 0:S], mem[:, 0:S], ALU.mult).then_inc(mem_sq, 1)
                G.tensor_tensor(two, mem[:, S:2 * S], mem[:, S:2 * S], ALU.mult).then_inc(mem_sq, 1)
                pool.wait_ge(mem_sq, 2)
                G.tensor_tensor(one, one, two, ALU.add).then_inc(mem_sq, 1)
                pool.wait_ge(mem_sq, 3)
                G.tensor_tensor(one[:, 0:512], one[:, 0:512], one[:, 512:1024], ALU.add).then_inc(mem_sq, 1)
                pool.wait_ge(mem_sq, 4)
                G.tensor_tensor(one[:, 0:256], one[:, 0:256], one[:, 256:512], ALU.add).then_inc(mem_ssq, 1)

            def split_static(u0, u1):
                for u in range(u0, u1):
                    if u >= 2 and ORDER[u - 2][1:] == ("mem", 2):
                        split(u % 2, 16 * (u // 2 + 1), 2 * u + 2, ORDER[u - 2][0] + 1, mem_half)
                    else:
                        split(u % 2, 16 * (u // 2 + 1), 2 * u + 2, LAST[u - 2] if u >= 2 else None)

            def split_quarter(u, q):
                s, cs = u % 2, slice(q % 2 * HALF, q % 2 * HALF + HALF)
                if q == 0:
                    pool.wait_ge(raw_loaded[s], 16 * (u // 2 + 1))
                    pool.wait_ge(bank_done, LAST[u - 2])
                if q == 2:
                    pool.wait_ge(unit_hi, 2 * u + 2)
                if q < 2:
                    ins = G.tensor_tensor(wh[:, s, cs], raw[:, s, cs], zero[:, :].to_broadcast([P, HALF]), ALU.add)
                else:
                    ins = G.tensor_tensor(wl[:, s, cs], raw[:, s, cs], raw32(wh[:, s, cs]), ALU.subtract)
                ins.then_inc((unit_hi, unit_split)[q // 2], 1)

            def attention(layer, part):
                todo, s0, uw = steps(layer), STEP0[layer], UNIT[layer, "wout", 0]

                def query_lo(i):
                    kind, t, c = todo[i]
                    pool.wait_ge(q_hi, s0 + i + 1)
                    hi, lo = query_at(kind, i)
                    if kind == "mem":
                        last = G.tensor_tensor(lo, Q[:, 6 + t, c * P:c * P + P], raw32(hi), ALU.subtract)
                    else:
                        for a in range(2):
                            ps = slice(64 * a, 64 * a + 64)
                            last = G.tensor_tensor(head_part(lo[ps], a), Q[ps, t, c * 256:c * 256 + 256].rearrange("p (j t) -> p j t", j=4),
                                                   raw32(head_part(hi[ps], a)), ALU.subtract)
                    last.then_inc(q_split, 1)

                def normalise(i):
                    g = 2 if todo[i][0] == "mem" else 4
                    pool.wait_ge(denom_ready, s0 + i + 1)
                    pr = tmp[:, i % 3, 0:HALF].rearrange("p (j m) -> p j m", j=g)
                    G.tensor_tensor(pr, pr, stat[:, i % 4, 4, 0:g].unsqueeze(2).to_broadcast([P, g, HALF // g]), ALU.mult).then_inc(prob_ready, 1)

                if part == "start":
                    for i in range(2):
                        query_lo(i)
                    return
                for i in range(len(todo)):
                    normalise(i)
                    if i == 0:
                        query_lo(2)
                        query_lo(3)
                    if i + 4 < len(todo):
                        if todo[i + 4][0] == "swa":
                            pool.wait_ge(prob_ready, s0 + i + 1)
                        query_lo(i + 4)
                        if todo[i + 4][0] == "swa":
                            pool.wait_ge(q_split, s0 + i + 5)
                    n = (i - NMEM) // 2
                    if layer == 0 and i < 4:
                        split_quarter(uw + 1, i)
                    elif layer == 1 and i < 4:
                        if i == 0:
                            pool.wait_ge(bank_done, H_FREE[H_Y1])
                        zs = slice(QB + i % 2 * 1024, QB + i % 2 * 1024 + 1024)
                        G.memset(raw32((Hh, Hl)[i // 2][:, zs]), 0.0).then_inc(zeros_made, 1)
                    elif layer == 1 and i > NMEM and i % 2 and n < 8:
                        split_quarter(uw + n // 4, n % 4)

            split_static(0, 2)
            memory_squares()
            done = 2
            for layer in range(2):
                u0, b0 = UNIT[layer, "w1", 0], BANK[layer, "w1", 0]
                uw = UNIT[layer, "wout", 0]
                split_static(done, uw - (1, 4)[layer == 0])
                attention(layer, "start")
                split_static(uw - (1, 4)[layer == 0], uw + (layer == 0))
                attention(layer, "steps")
                split_static(uw + 2, u0 + 8)
                with pool.Fori(1, GROUPS) as g:
                    for i in range(8):
                        used = 24 * g + b0 + ([-4, 0, 2, 4, 6, 8, 12, 16][i])
                        split(i % 2, 64 * g + 16 * ((u0 + i) // 2 + 1), 16 * g + 2 * (u0 + i + 1), used)
                done = u0 + 8 * GROUPS
            for h in range(2):
                pool.wait_ge(rstd_ready, h + 1)
                for k in range(FINAL_V, KT):
                    s = slice(h * HALF, h * HALF + HALF)
                    if h == 0:
                        pool.wait_ge(gain_applied, k - FINAL_V + 1)
                    G.tensor_tensor(X[:, k, s], X[:, k, s], rstd[:, s], ALU.mult).then_inc(final_ready[1], 1)

        @block.tensor
        def _(pe):
            def passes(out, lh, ll, rh, rl, first, last):
                T.matmul(out, lh, rh, start=first, stop=False)
                T.matmul(out, lh, rl, start=False, stop=False)
                return T.matmul(out, ll, rh, start=False, stop=last)

            def bank_free(b):
                if b >= 4:
                    a, n = EMPTIED[b - 4]
                    pe.wait_ge(emptied[a], n)

            def norm_sums(n):
                pe.wait_ge(sq_added, 16 * n + 16)
                for j in range(KT):
                    last = T.matmul(bank[4][:, j:j + 1], tmp[:, 2, j * P:(j + 1) * P], ones[:, 0:1], start=True, stop=True)
                last.then_inc(colsum_done, 1)

            def norm_spread(n):
                for h in range(2):
                    pe.wait_ge(diag_ready, 2 * n + h + 1)
                    T.matmul(bank[5 + h][:, :], ones[:, :], tmp[:, 2, h * HALF:h * HALF + HALF], start=True, stop=True).then_inc(bcast_done, 1)

            def memory_sums():
                pe.wait_ge(mem_ssq, 1)
                for j in range(2):
                    last = T.matmul(bank[7][:, j:j + 1], memsq[:, j * P:(j + 1) * P], ones[:, 0:1], start=True, stop=True)
                last.then_inc(mem_colsum, 1)

            def memory_spread():
                pe.wait_ge(mem_diag, 1)
                T.matmul(bank[7][:, 0:MEM], ones[:, :], memdiag[:, 0:MEM], start=True, stop=True).then_inc(mem_bcast, 1)

            def unit_from_h(slot, b, h_version, k_major, emptied_of, between=None, last_use=False, second_half=None):
                ks = Y_ORDER.get(h_version, range(KT))
                order = [(n, h) for n in range(KT) for h in range(2)] if k_major else [(n, h) for h in range(2) for n in range(KT)]
                if h_version in Y_ORDER:
                    pe.wait_ge(unit_split, second_half)
                    second_half = None
                for n, h in order:
                    k = ks[n]
                    if n == 0:
                        if h == 1 and between is not None:
                            between()
                        emptied_of(h)
                    if n == 4 and h == 0 and second_half is not None:
                        pe.wait_ge(unit_split, second_half)
                    if h_version is not None and h == 0:
                        pe.wait_ge(h_ready, 8 * h_version + n + 1)
                    ls = slice(k * P, k * P + P)
                    last = passes(bank[(b + h) % 4][:, :], wh[:, slot, ls], wl[:, slot, ls],
                                  Hh[:, hb(k, h * HALF, HALF)], Hl[:, hb(k, h * HALF, HALF)], n == 0, n == KT - 1)
                    if n == KT - 1:
                        last.then_inc(bank_done, 1)
                    elif last_use and h == 1:
                        last.then_inc(h_used, 1)

            def unit_static(layer, kind, i, h_version=None, between=None, last_use=False):
                u, b = UNIT[layer, kind, i], BANK[layer, kind, i]
                pe.wait_ge(unit_split, 2 * u + 1)
                unit_from_h(u % 2, b, h_version, h_version is not None or last_use, lambda h: bank_free(b + h), between, last_use,
                            second_half=2 * u + 2)

            def units_loop(layer, kind, i0, n):
                u, b = UNIT[layer, kind, i0], BANK[layer, kind, i0]
                e = EMPTIED[b - 4][1]
                assert not EMPTIED[b - 4][0] and b % 4 == 0 and u % 2 == 0
                with pe.Fori(0, n // 2) as i:
                    for s in range(2):
                        pe.wait_ge(unit_split, 4 * i + 2 * (u + s + 1))
                        unit_from_h(s, b + 2 * s, None, False, lambda h, s=s: pe.wait_ge(emptied[0], 4 * i + (e + 2 * s + h)))

            def memory_k(layer, i):
                pe.wait_ge(mem_ready, layer + 1)
                u, b = UNIT[layer, "mem", i], BANK[layer, "mem", i]
                pe.wait_ge(unit_split, 2 * u + 1)
                bank_free(b)
                for k in range(KT):
                    if k == 4:
                        pe.wait_ge(unit_split, 2 * u + 2)
                    ls, rs = slice(k * P, k * P + P), slice(MEMR[layer] + k * MEM, MEMR[layer] + k * MEM + MEM)
                    last = passes(bank[b % 4][:, 0:MEM], wh[:, u % 2, ls], wl[:, u % 2, ls], Rh[:, rs], Rl[:, rs], k == 0, k == KT - 1)
                last.then_inc(bank_done, 1)

            def memory_v(layer):
                u = UNIT[layer, "mem", 2]
                for m in range(2):
                    bank_free(BANK[layer, "mem", 2 + m])
                for k in range(KT):
                    if k % 2 == 0:
                        pe.wait_ge(unit_split, 2 * u + k // 2 + 1)
                    for m in range(2):
                        o = MEMR[layer] + k * MEM + m * P
                        ls, rs = slice(o, o + P), slice(k % 4 * 256, k % 4 * 256 + 256)
                        w = (u + k // 4) % 2
                        last = passes(bank[(BANK[layer, "mem", 2] + m) % 4][:, 0:256], Rh[:, ls], Rl[:, ls],
                                      wh[:, w, rs], wl[:, w, rs], k == 0, k == KT - 1)
                        if k == 3 and m == 1:
                            last.then_inc(mem_half, 1)
                        if k == KT - 1:
                            last.then_inc(bank_done, 1)

            def shared_v(layer):
                for t in range(KT):
                    b = BANK[layer, "V", 0] + t // 2
                    if t % 2 == 0:
                        bank_free(b)
                    for k in range(KT):
                        if t == 0 and k % 2 == 0:
                            pe.wait_ge(unit_split, 2 * UNIT[layer, "V", 0] + k // 2 + 1)
                        ls, rs = hb(k, t * P, P), slice(k % 4 * 256, k % 4 * 256 + 256)
                        last = passes(bank[b % 4][:, t % 2 * 256:t % 2 * 256 + 256], Hh[:, ls], Hl[:, ls],
                                      wh[:, k // 4, rs], wl[:, k // 4, rs], k == 0, k == KT - 1)
                    if t % 2:
                        last.then_inc(bank_done, 1)

            def gates(j):
                u, b, ks = UNIT[0, "G", j], BANK[0, "G", j], GATE_K[j % 3]
                pe.wait_ge(unit_split, 2 * u + 1)
                pe.wait_ge(conv_split, 2 * (j - j % 3 + ks[-1]) + 2)
                for h in range(2):
                    for which in range(2):
                        bb = b + 2 * h + which
                        bank_free(bb)
                        if h == 0 and which == 1:
                            pe.wait_ge(unit_split, 2 * u + 2)
                        for n, k in enumerate(ks):
                            ls, rs = slice((which * len(ks) + n) * P, (which * len(ks) + n + 1) * P), hb(k, h * HALF, HALF)
                            last = passes(bank[bb % 4][:, :], wh[:, u % 2, ls], wl[:, u % 2, ls], Rh[:, rs], Rl[:, rs],
                                          n == 0, n == len(ks) - 1)
                        last.then_inc(bank_done, 1)

            def attention(layer, part):
                todo, s0 = steps(layer), STEP0[layer]

                def scores(i):
                    kind, t, c = todo[i]
                    n = s0 + i
                    pe.wait_ge(q_split, n + 1)
                    if i >= 4:
                        pe.wait_ge(exp_done, n - 3)
                    if i == 2:
                        pe.wait_ge(emptied[0], EMPTIED[BANK[layer, "wout", 0] - 1][1])
                    if kind == "swa" and todo[i - 1][0] == "mem":
                        pe.wait_ge(v2_made, 4)
                        pe.wait_ge(bias_split, 1)
                    (qh, ql), out = query_at(kind, i), pS[i % 4]
                    if kind == "mem":
                        last = passes(out[:, :], qh, ql, mkh[:, t, :], mkl[:, t, :], True, True)
                    else:
                        bh, bl, ident_h = Hh[:, BS + t * P:BS + t * P + P], Hl[:, BS + t * P:BS + t * P + P], Hh[:, ID:ID + P]
                        j0 = 0
                        if c == 0:
                            j0 = 1
                            passes(out[:, 0:P], qh[:, 0:P], ql[:, 0:P], Rh[:, t // 3 * S:t // 3 * S + P], Rl[:, t // 3 * S:t // 3 * S + P], True, False)
                            T.matmul(out[:, 0:CHUNK], ident_h, bh[:, CHUNK:P], start=False, stop=False)
                            T.matmul(out[:, 0:CHUNK], ident_h, bl[:, CHUNK:P], start=False, stop=True)
                        dst = out[:, j0 * P:HALF].rearrange("p (j m) -> p j m", m=P)
                        T.matmul(dst, ident_h, bh.unsqueeze(1).to_broadcast([P, 4 - j0, P]), start=True, stop=False)
                        T.matmul(dst, ident_h, bl.unsqueeze(1).to_broadcast([P, 4 - j0, P]), start=False, stop=False)
                        for j in range(j0, 4):
                            first_key = (4 * c + j - 1) * CHUNK
                            rs = slice(t // 3 * S + first_key, t // 3 * S + first_key + P)
                            ls = slice(j * P, j * P + P)
                            last = passes(out[:, ls], qh[:, ls], ql[:, ls], Rh[:, rs], Rl[:, rs], False, j == 3)
                    last.then_inc(score_done, 1)

                def turn(i):
                    kind, t, c = todo[i]
                    n = s0 + i
                    pe.wait_ge(prob_ready, n + 1)
                    if i >= 2:
                        pe.wait_ge(turned_split, n - 1)
                    for j in range(4):
                        o = (j % 2 * 2 + j // 2 if kind == "mem" else j) * P
                        last = T.transpose(pT[i % 2][:, o:o + P], tmp[:, i % 3, j * P:j * P + P], ident[:, :])
                    last.then_inc(turned, 1)

                def values(i):
                    kind, t, c = todo[i]
                    n = s0 + i
                    pe.wait_ge(turned_split, n + 1)
                    if i >= 2:
                        pe.wait_ge(att_out, n - 1)
                    pt, out = PT + i % 3 * 512, pO[i % 2]
                    if kind == "mem":
                        for m in range(2):
                            ls, rs = slice(t * P, t * P + P), slice(pt + m * 256, pt + m * 256 + 256)
                            last = passes(out[:, 0:256], mvh[:, m, ls], mvl[:, m, ls], Hh[:, rs], Hl[:, rs], m == 0, m == 1)
                    else:
                        for j in range(4):
                            q, gp = 4 * c + j, t // 3
                            rs = slice(pt + j * P, pt + j * P + P)
                            if q % 2 or q == 0:
                                vs = slice(2 * S + q // 2 * 256 + gp * P, 2 * S + q // 2 * 256 + gp * P + P)
                                vh, vl = Rh[:, vs], Rl[:, vs]
                            else:
                                vs = slice(V2 + (q // 2 - 1) * 256 + gp * P, V2 + (q // 2 - 1) * 256 + gp * P + P)
                                vh, vl = Hh[:, vs], Hl[:, vs]
                            last = passes(out[:, j * P:j * P + P], vh, vl, Hh[:, rs], Hl[:, rs], True, True)
                    last.then_inc(pv_done, 1)

                if part == "start":
                    pe.wait_ge(emptied[0], EMPTIED[BANK[layer, "mem", 3]][1])
                    scores(0)
                    scores(1)
                    return
                for i in range(len(todo)):
                    if i == 0:
                        turn(i)
                        scores(2)
                        scores(3)
                    elif i + 3 < len(todo) and todo[i + 3][0] == "mem":
                        scores(i + 3)
                        turn(i)
                    else:
                        turn(i)
                        if i + 3 < len(todo):
                            scores(i + 3)
                    if i >= 1:
                        values(i - 1)
                values(len(todo) - 1)

            def mlp(layer):
                u0, b0 = UNIT[layer, "w1", 0], BANK[layer, "w1", 0]
                e0 = EMPTIED[b0 - 4][1]

                def group(g, first):
                    for f in range(GF):
                        pe.wait_ge(unit_split, 16 * g + 2 * (u0 + f + 1))
                        unit_from_h(f % 2, b0 + 2 * f, (H_MLP0, H_MLP1)[layer] if first and f == 0 else None, first and f == 0,
                                    lambda h, f=f: pe.wait_ge(emptied[0], 24 * g + (e0 + 2 * f + h)),
                                    (lambda: norm_spread((MLP0, MLP1)[layer])) if first and f == 1 else None)
                        if first and f == 0:
                            norm_sums((MLP0, MLP1)[layer])
                    for v in range(4):
                        pe.wait_ge(unit_split, 16 * g + 2 * (u0 + 4 + v + 1))
                        for n in range(2):
                            for h in range(2):
                                c = 8 + 4 * v + 2 * n + h
                                pe.wait_ge(emptied[0], 24 * g + (e0 + c))
                                for f in range(GF):
                                    if v == 0 and n == 0:
                                        pe.wait_ge(hid_split, 8 * g + (64 * layer + 2 * f + h + 1))
                                    ls, rs = slice((n * GF + f) * P, (n * GF + f + 1) * P), slice(f * S + h * HALF, f * S + h * HALF + HALF)
                                    last = passes(bank[(b0 + c) % 4][:, :], wh[:, v % 2, ls], wl[:, v % 2, ls],
                                                  Rh[:, rs], Rl[:, rs], f == 0, f == GF - 1)
                                last.then_inc(bank_done, 1)
                group(0, True)
                with pe.Fori(1, GROUPS) as g:
                    group(g, False)

            pe.wait_ge(consts_made, 7)
            unit_static(0, "xr", 0, H_MIX0)
            pe.wait_ge(consts_loaded, 16 * 3)
            T.matmul(bank[7][0:12, 0:REL], relsb[:, :], onesb, start=True, stop=True).then_inc(toep_done, 1)
            norm_sums(MIX0)
            pe.wait_ge(toep_copied, 1)
            memory_sums()

            def spreads():
                norm_spread(MIX0)
                memory_spread()

            def projections(layer, order, between):
                for n, (kind, i) in enumerate(order):
                    if kind == "G":
                        gates(i)
                    elif kind != "mem":
                        unit_static(layer, kind, i, between=between if n == 0 else None)
                    elif i < 2:
                        memory_k(layer, i)
                    elif i == 2:
                        memory_v(layer)
            projections(0, A_ORDER[1:-1], spreads)
            attention(0, "start")
            unit_static(0, "gate", 5)
            attention(0, "steps")
            unit_static(0, "wout", 0, H_Y0)
            unit_static(0, "wout", 1)
            units_loop(0, "wout", 2, 4)
            unit_static(0, "wout", 6)
            unit_static(0, "wout", 7, last_use=True)
            mlp(0)
            unit_static(1, "q", 0, H_MIX1)
            norm_sums(MIX1)
            projections(1, B_ORDER[1:11], lambda: norm_spread(MIX1))
            unit_static(1, "qm", 1, last_use=True)
            unit_static(1, "K", 0, H_KV)
            unit_static(1, "K", 1)
            attention(1, "start")
            shared_v(1)
            attention(1, "steps")
            unit_static(1, "wout", 0, H_Y1)
            unit_static(1, "wout", 1)
            units_loop(1, "wout", 2, 4)
            unit_static(1, "wout", 6)
            unit_static(1, "wout", 7, last_use=True)
            mlp(1)
            norm_sums(FINAL)
            norm_spread(FINAL)

        @block.scalar
        def _(act):
            own = [0]

            def link(ins):
                own[0] += 1
                ins.then_inc(act_own, 1)
                act.wait_ge(act_own, own[0])

            act.dma_start(col[:, :, :], cols).then_inc(col_loaded, 16)
            act.dma_start(gain[:, :, :], gains).then_inc(gain_loaded, 16)
            def norm_std(n):
                act.wait_ge(var_ready, n + 1)
                A.activation(nrm[:, 1, TOK], nrm[:, 0, TOK], ACT.Sqrt).then_inc(std_ready, 1)

            def memory_std():
                act.wait_ge(mem_var, 1)
                A.activation(nrm[:, 1, MEMC], nrm[:, 0, MEMC], ACT.Sqrt).then_inc(mem_std, 1)

            def memory_hi(layer):
                if layer:
                    act.wait_ge(mem_loaded, 32)
                else:
                    act.wait_ge(mem_normed, 1)
                A.activation(Rh[:, MEMR[layer]:MEMR[layer] + 2 * S], memraw[layer], ACT.Copy).then_inc(mem_hi, 1)

            def squares(version, which):
                for i in which:
                    n = 16 * version + i
                    if version != MIX0:
                        act.wait_ge(emptied[0], EMPTIED[UPDATES[version] + i][1])
                    if n >= 2:
                        act.wait_ge(sq_added, n - 1)
                    A.activation(tmp[:, 1, i % 2 * HALF:i % 2 * HALF + HALF], X[:, i // 2, i % 2 * HALF:i % 2 * HALF + HALF],
                                 ACT.Square).then_inc(x_squared, 1)

            def h_hi_tiles(v, ks):
                for k in ks:
                    A.activation(Hh[:, hb(k, 0, S)], X[:, k, :], ACT.Copy, scale=gain[:, GAIN_OF[v], k:k + 1]).then_inc(h_hi, 1)

            def h_version(v, norm):
                if v not in BEHIND:
                    if v in H_FREE:
                        act.wait_ge(bank_done, H_FREE[v])
                    for k in range(KT):
                        if norm == MIX0:
                            act.wait_ge(x_loaded[k], 16)
                        else:
                            squares(norm, (2 * k, 2 * k + 1))
                        h_hi_tiles(v, (k,))
                        if norm == MIX0:
                            squares(norm, (2 * k, 2 * k + 1))
                else:
                    for k in range(KT):
                        if k < KT - 1:
                            act.wait_ge(h_used, (KT - 1) * BEHIND.index(v) + k + 1)
                        else:
                            if norm is not None:
                                squares(norm, (14, 15))
                            act.wait_ge(bank_done, H_FREE[v])
                        h_hi_tiles(v, (k,))
                if norm is not None:
                    norm_std(norm)

            def y_version(v):
                if v == H_Y0:
                    act.wait_ge(y_done, 2 * LT)
                for n, k in enumerate(Y_ORDER[v]):
                    if v == H_Y1 and n == 1:
                        act.wait_ge(score_done, 2 * NMEM + NSWA)
                    if n == 3:
                        act.wait_ge(pv_done, (NMEM, 2 * NMEM + NSWA)[v == H_Y1])
                    if v == H_Y0:
                        need = NMEM // 2 * (k - 5) if k >= 6 else None
                    else:
                        need = NMEM + NMEM // 2 * (k - 5) if k >= 6 else 2 * NMEM + 4 * (k + 1)
                    if need is not None:
                        act.wait_ge(att_out, need)
                    A.activation(Hh[:, hb(k, 0, S)], Q[:, k, :], ACT.Copy).then_inc(h_hi, 1)

            def memory_kv_hi(layer, which=range(4)):
                for i in which:
                    b = BANK[layer, "mem", i]
                    act.wait_ge(bank_done, b + 1)
                    if i < 2:
                        for a in range(2):
                            ps = slice(64 * a, 64 * a + 64)
                            last = A.activation(mkh[ps, i, 256 * a:256 * a + 256], bank[b % 4][ps, 0:MEM], ACT.Copy)
                    else:
                        last = A.activation(mvh[:, i - 2, :], bank[b % 4][:, 0:256], ACT.Copy)
                    last.then_inc(mkv_hi, 1)

            def attention(layer, part):
                todo, s0 = steps(layer), STEP0[layer]

                def query_hi(i):
                    kind, t, c = todo[i]
                    if i >= 4:
                        act.wait_ge(score_done, s0 + i - 3)
                    if kind == "swa" and todo[i - 1][0] == "mem":
                        act.wait_ge(zeros_made, 4)
                    hi, _ = query_at(kind, i)
                    if kind == "mem":
                        last = A.activation(hi, Q[:, 6 + t, c * P:c * P + P], ACT.Copy)
                    else:
                        for a in range(2):
                            ps = slice(64 * a, 64 * a + 64)
                            last = A.activation(head_part(hi[ps], a), Q[ps, t, c * 256:c * 256 + 256].rearrange("p (j t) -> p j t", j=4), ACT.Copy)
                    last.then_inc(q_hi, 1)

                def exps(i):
                    kind, t, c = todo[i]
                    n = s0 + i
                    act.wait_ge(max_ready, n + 1)
                    if i >= 3:
                        act.wait_ge(turned, n - 2)
                    st = stat[:, i % 4]
                    if kind == "mem":
                        for j in range(2):
                            last = A.activation(tmp[:, i % 3, j * 256:j * 256 + 256], pS[i % 4][:, j * 256:j * 256 + 256], ACT.Exp,
                                                scale=SCALE, bias=st[:, 1, j:j + 1], accum_out=st[:, 2, j:j + 1])
                    else:
                        for j in range(4):
                            w = CHUNK if c == 0 and j == 0 else P
                            A.activation(tmp[:, i % 3, j * P:j * P + w], pS[i % 4][:, j * P:j * P + w], ACT.Exp,
                                         scale=SCALE, bias=st[:, 1, j:j + 1], accum_out=st[:, 2, j:j + 1])
                        if c == 0:
                            A.activation(tmp[:, i % 3, CHUNK:P], ones[:, 0:CHUNK], ACT.Copy, scale=0.0)
                        last = A.activation(st[:, 3, :], st[:, 1, :], ACT.Exp, bias=sink[:, t:t + 1])
                    last.then_inc(exp_done, 1)

                def turned_hi_part(i):
                    act.wait_ge(turned, s0 + i + 1)
                    if i >= 3:
                        act.wait_ge(pv_done, s0 + i - 2)
                    A.activation(Hh[:, PT + i % 3 * 512:PT + i % 3 * 512 + 512], pT[i % 2][:, :], ACT.Copy).then_inc(turned_hi, 1)

                if part == "start":
                    act.wait_ge(emptied[0], EMPTIED[BANK[layer, "qm", 1] + 1][1])
                    for i in range(2):
                        query_hi(i)
                    return
                if part == "exps":
                    if layer == 0:
                        act.wait_ge(lru_done, LT)
                    exps(0)
                    exps(1)
                    return
                act.wait_ge(bank_done, H_FREE[(H_Y0, H_Y1)[layer]])
                for i in range(2, 4):
                    query_hi(i)
                for i in range(len(todo)):
                    if i + 4 < len(todo):
                        query_hi(i + 4)
                    if 1 <= i < len(todo) - 1:
                        exps(i + 1)
                    turned_hi_part(i)
                    if layer and i == 2:
                        act.wait_ge(bias_loaded, 16 * 12)
                        A.activation(Hh[:, ID:ID + P], ident[:, :], ACT.Copy)
                        A.activation(Hh[:, BS:BS + 6 * P], XR[:, 0:6 * P], ACT.Copy, scale=1.0 / SCALE).then_inc(bias_hi, 1)
                    if layer and i in (4, 5):
                        a = i - 4
                        act.wait_ge(kv_split, 8)
                        src = slice(2 * S + a * 256, 2 * S + a * 256 + 7 * 256)
                        A.activation(Hh[64 * a:64 * a + 64, V2:V2 + 7 * 256], raw32(Rh[64 - 64 * a:128 - 64 * a, src]), ACT.Copy).then_inc(v2_made, 1)

            def mlp(layer):
                b0 = BANK[layer, "w1", 0]
                e0 = EMPTIED[b0 - 1][1]

                def group(g):
                    for i in range(2 * GF):
                        s = slice(i % 2 * HALF, i % 2 * HALF + HALF)
                        act.wait_ge(emptied[0], 24 * g + (e0 + i + 1))
                        if i < 2:
                            act.wait_ge(bank_done, 24 * g + b0)
                        else:
                            act.wait_ge(hid_split, 8 * g + (64 * layer + i - 1))
                        A.activation(tmp[:, 1, s], tmp[:, 0, s], ACT.Square).then_inc(relu_squared, 1)
                        act.wait_ge(relu_squared, 8 * g + (64 * layer + i + 1))
                        A.activation(Rh[:, (i // 2) * S + i % 2 * HALF:(i // 2) * S + i % 2 * HALF + HALF], tmp[:, 1, s],
                                     ACT.Copy).then_inc(hid_hi, 1)
                with act.Fori(0, GROUPS) as g:
                    group(g)

            act.wait_ge(col_loaded, 16)
            link(A.activation(sp[:, 0, :], col[:, 7, :], ACT.Abs))
            A.activation(sp[:, 1, :], sp[:, 0, :], ACT.Exp, scale=-1.0).then_inc(lam_exp, 1)
            for dst, src in ((relsb[:, :], relb), (onesb, onehot), (sink[:, :], sinkc)):
                act.dma_start(dst, src).then_inc(consts_loaded, 16)
            act.wait_ge(gain_loaded, 16)
            h_version(H_MIX0, MIX0)
            memory_std()
            act.wait_ge(toep_copied, 1)
            act.dma_start(rep.rearrange("(h i r) -> h i r", h=12, i=CHUNK), toep.unsqueeze(1).to_broadcast([12, CHUNK, REL])).then_inc(toep_written, 16)
            memory_hi(0)
            act.dma_start(memn, memraw[0]).then_inc(mem_written, 16)

            def decay_root(j):
                act.wait_ge(decay_half, j + 1)
                A.activation(tmp[:, 1, :], tmp[:, 1, :], ACT.Sqrt).then_inc(decay_sqrt, 1)

            for kind, j in A_ORDER:
                if kind == "mem":
                    memory_kv_hi(0, (j,))
                if kind == "xr":
                    for h in range(2):
                        s = slice(h * HALF, h * HALF + HALF)
                        act.wait_ge(emptied[0], EMPTIED[BANK[0, "xr", j] + h][1])
                        A.activation(Q[:, j, s], XR[:, 3 + h * HALF:3 + h * HALF + HALF], ACT.Identity,
                                     scale=col[:, 3, j:j + 1], bias=col[:, 4, j:j + 1]).then_inc(conv_seeded, 1)
                        act.wait_ge(conv_ready, 2 * j + h + 1)
                        if j == 2 and h == 0:
                            act.wait_ge(bank_done, LAST[UNIT[0, "mem", 3]])
                        if j >= 3 and h == 0:
                            act.wait_ge(bank_done, LAST[UNIT[0, "G", 2 if j > 3 else 1]])
                        A.activation(Rh[:, (j % 3) * S + h * HALF:(j % 3) * S + h * HALF + HALF], Q[:, j, s], ACT.Copy).then_inc(conv_hi, 1)
                elif kind == "gate":
                    if j == 0:
                        attention(0, "start")
                    if j == 5:
                        attention(0, "exps")
                    for h in range(2):
                        n, s = 2 * j + h, slice(h * HALF, h * HALF + HALF)
                        act.wait_ge(emptied[0], EMPTIED[BANK[0, "gate", j] + h][1])
                        A.activation(rx[:, 1, :], rx[:, 0, :], ACT.Square).then_inc(gate_squared, 1)
                        act.wait_ge(gate_inner, n + 1)
                        A.activation(rx[:, 1, :], rx[:, 1, :], ACT.Tanh, scale=GELU_C * GELU_A).then_inc(gate_tanh, 1)
                if kind == "G":
                    if j >= 1:
                        act.wait_ge(lru_done, j)
                    if j == 0:
                        act.wait_ge(sp_ready, 1)
                    for h in range(2):
                        for which in range(2):
                            b = BANK[0, "G", j] + 2 * h + which
                            act.wait_ge(bank_done, b + 1)
                            A.activation(tmp[:, 2 * which, h * HALF:h * HALF + HALF], bank[b % 4][:, :], ACT.Tanh, scale=0.5,
                                         bias=col[:, 5 + which, j:j + 1]).then_inc(emptied[1], 1)
                    act.wait_ge(emptied[1], EMPTIED[b][1])
                    A.activation(tmp[:, 1, :], tmp[:, 2, :], ACT.Tanh, scale=sp[:, 4, j:j + 1], bias=sp[:, 4, j:j + 1]).then_inc(decay_tanh, 1)
                    act.wait_ge(decay_tanh, 2 * j + 1)
                    A.activation(tmp[:, 2, :], tmp[:, 2, :], ACT.Exp, scale=sp[:, 5, j:j + 1], bias=sp[:, 5, j:j + 1]).then_inc(decay_tanh, 1)
                    decay_root(j)
            attention(0, "steps")
            y_version(H_Y0)
            squares(MLP0, range(14))
            h_version(H_MLP0, MLP0)
            mlp(0)
            h_version(H_MIX1, MIX1)
            act.wait_ge(mem_written, 16)
            act.dma_start(memraw[1], memn).then_inc(mem_loaded, 16)
            memory_hi(1)
            act.wait_ge(toep_written, 16)
            for p, pair in enumerate(PAIRS):
                for a, head in enumerate(pair):
                    o = head * CHUNK * REL + CHUNK - 1
                    act.dma_start(bias[64 * a:64 * a + 64, p, :], rep[o:o + CHUNK * (REL - 1)].rearrange(
                        "(i r) -> i r", r=REL - 1)[:, 0:2 * CHUNK]).then_inc(bias_loaded, 16)
            memory_kv_hi(1)
            h_version(H_KV, None)
            attention(1, "start")
            for i in range(8):
                if i == 5:
                    attention(1, "exps")
                s = slice(i * HALF, i * HALF + HALF)
                act.wait_ge(emptied[0], EMPTIED[BANK[1, "K", 0] + i][1])
                A.activation(Rh[:, s], tmp[:, 2, i % 2 * HALF:i % 2 * HALF + HALF], ACT.Copy).then_inc(kv_hi, 1)
            attention(1, "steps")
            y_version(H_Y1)
            squares(MLP1, range(14))
            h_version(H_MLP1, MLP1)
            mlp(1)
            squares(FINAL, range(16))
            norm_std(FINAL)
            for k in range(FINAL_V, KT):
                A.activation(X[:, k, :], X[:, k, :], ACT.Copy, scale=gain[:, 6, k:k + 1]).then_inc(gain_applied, 1)

        @block.vector
        def _(dve):
            own = [0]

            def link(ins):
                own[0] += 1
                ins.then_inc(dve_own, 1)
                dve.wait_ge(dve_own, own[0])

            def newton(c):
                link(V.reciprocal(nrm[:, 2, c], nrm[:, 1, c]))
                link(V.tensor_tensor(nrm[:, 3, c], nrm[:, 2, c], nrm[:, 2, c], ALU.mult))
                link(V.tensor_tensor(nrm[:, 3, c], nrm[:, 3, c], nrm[:, 0, c], ALU.mult))
                link(V.tensor_scalar(nrm[:, 3, c], nrm[:, 3, c], -0.5, 1.5, ALU.mult, ALU.add))
                link(V.tensor_tensor(nrm[:, 4, c], nrm[:, 2, c], nrm[:, 3, c], ALU.mult))

            def diagonal(dst, c):
                w = c.stop - c.start
                return V.tensor_tensor(dst.rearrange("p (j t) -> p j t", t=P), ident[:, :].unsqueeze(1).to_broadcast([P, w, P]),
                                       nrm[:, 4, c].unsqueeze(2).to_broadcast([P, w, P]), ALU.mult)

            def norm_finish(n, meanwhile=None):
                dve.wait_ge(colsum_done, n + 1)
                V.tensor_scalar(nrm[:, 0, TOK], bank[4][:, 0:8], 1.0 / D, EPS, ALU.mult, ALU.add).then_inc(var_ready, 1)
                dve.wait_ge(std_ready, n + 1)
                newton(TOK)
                for h in range(2):
                    diagonal(tmp[:, 2, h * HALF:h * HALF + HALF], slice(4 * h, 4 * h + 4)).then_inc(diag_ready, 1)
                if meanwhile is not None:
                    meanwhile()
                for h in range(2):
                    s = slice(h * HALF, h * HALF + HALF)
                    dve.wait_ge(bcast_done, 2 * n + h + 1)
                    if n != FINAL:
                        link(V.tensor_copy(rstd[:, s], bank[5 + h][:, :]))
                        continue
                    V.tensor_copy(rstd[:, s], bank[5 + h][:, :]).then_inc(rstd_ready, 1)
                    dve.wait_ge(rstd_ready, h + 1)
                    for k in range(FINAL_V):
                        V.scalar_tensor_tensor(X[:, k, s], X[:, k, s], gain[:, 6, k:k + 1], rstd[:, s], ALU.mult, ALU.mult).then_inc(final_ready[0], 1)

            def memory_stats():
                dve.wait_ge(mem_colsum, 1)
                V.tensor_scalar(nrm[:, 0, MEMC], bank[7][:, 0:2], 1.0 / D, EPS, ALU.mult, ALU.add).then_inc(mem_var, 1)
                dve.wait_ge(mem_std, 1)
                newton(MEMC)
                diagonal(memdiag[:, 0:MEM], MEMC).then_inc(mem_diag, 1)

            def memory_scale():
                mem = memraw[0]
                dve.wait_ge(mem_bcast, 1)
                for k in range(KT):
                    ks = slice(k * MEM, k * MEM + MEM)
                    last = V.scalar_tensor_tensor(mem[:, ks], mem[:, ks], gain[:, 0, k:k + 1], bank[7][:, 0:MEM], ALU.mult, ALU.mult)
                last.then_inc(mem_normed, 1)

            def memory_lo(layer):
                dve.wait_ge(mem_hi, layer + 1)
                rs = slice(MEMR[layer], MEMR[layer] + 2 * S)
                V.tensor_tensor(Rl[:, rs], memraw[layer], raw32(Rh[:, rs]), ALU.subtract).then_inc(mem_ready, 1)

            def add_square(version, i):
                n = 16 * version + i
                h = i % 2
                dst, sq = tmp[:, 2, h * HALF:h * HALF + HALF], tmp[:, 1, h * HALF:h * HALF + HALF]
                dve.wait_ge(x_squared, n + 1)
                if i < 2:
                    ins = V.tensor_copy(dst, sq)
                else:
                    dve.wait_ge(sq_added, n - 1)
                    ins = V.tensor_tensor(dst, dst, sq, ALU.add)
                ins.then_inc(sq_added, 1)

            def h_lo_tiles(v, ks):
                for k in ks:
                    dve.wait_ge(h_hi, 8 * v + k + 1)
                    V.scalar_tensor_tensor(Hl[:, hb(k, 0, S)], X[:, k, :], gain[:, GAIN_OF[v], k:k + 1], raw32(Hh[:, hb(k, 0, S)]),
                                           ALU.mult, ALU.subtract).then_inc(h_ready, 1)

            def h_version(v, norm):
                for k in range(KT):
                    h_lo_tiles(v, (k,))
                    add_square(norm, 2 * k)
                    add_square(norm, 2 * k + 1)

            def y_lo(v, places):
                for n in places:
                    k = Y_ORDER[v][n]
                    dve.wait_ge(h_hi, 8 * v + n + 1)
                    V.tensor_tensor(Hl[:, hb(k, 0, S)], Q[:, k, :], raw32(Hh[:, hb(k, 0, S)]), ALU.subtract).then_inc(h_ready, 1)

            def memory_kv_lo(layer, which):
                for i in which:
                    b = BANK[layer, "mem", i]
                    dve.wait_ge(mkv_hi, 4 * layer + i + 1)
                    if i < 2:
                        for a in range(2):
                            ps, cs = slice(64 * a, 64 * a + 64), slice(256 * a, 256 * a + 256)
                            last = V.tensor_tensor(mkl[ps, i, cs], bank[b % 4][ps, 0:MEM], raw32(mkh[ps, i, cs]), ALU.subtract)
                    else:
                        last = V.tensor_tensor(mvl[:, i - 2, :], bank[b % 4][:, 0:256], raw32(mvh[:, i - 2, :]), ALU.subtract)
                    last.then_inc(emptied[0], 1)

            def evict(layer, kind, i, h):
                b = BANK[layer, kind, i] + h
                dve.wait_ge(bank_done, b + 1)
                return bank[b % 4]

            def wout(layer):
                version, v = ((MLP0, H_MLP0), (MLP1, H_MLP1))[layer]
                for i in range(16):
                    n, h = i // 2, i % 2
                    s = slice(h * HALF, h * HALF + HALF)
                    if i == 14:
                        h_lo_tiles(v, range(KT - 1))
                    pb = evict(layer, "wout", n, h)
                    V.tensor_tensor(X[:, n, s], X[:, n, s], pb[:, :], ALU.add).then_inc(emptied[0], 1)
                    if 1 <= i < 15:
                        add_square(version, i - 1)
                add_square(version, 14)
                add_square(version, 15)
                h_lo_tiles(v, (KT - 1,))

            def mlp(layer):
                b0 = BANK[layer, "w1", 0]
                version = (MIX1, FINAL)[layer]

                def hidden_lo(g, i):
                    s = slice((i // 2) * S + i % 2 * HALF, (i // 2) * S + i % 2 * HALF + HALF)
                    dve.wait_ge(hid_hi, 8 * g + (64 * layer + i + 1))
                    V.tensor_tensor(Rl[:, s], tmp[:, 1, i % 2 * HALF:i % 2 * HALF + HALF], raw32(Rh[:, s]), ALU.subtract).then_inc(hid_split, 1)

                def group(g, last_group):
                    for i in range(2 * GF):
                        s = slice(i % 2 * HALF, i % 2 * HALF + HALF)
                        dve.wait_ge(bank_done, 24 * g + (b0 + i + 1))
                        if i >= 2:
                            dve.wait_ge(relu_squared, 8 * g + (64 * layer + i - 1))
                        V.scalar_tensor_tensor(tmp[:, 0, s], bank[(b0 + i) % 4][:, :], 0.0, rstd[:, s], ALU.max, ALU.mult).then_inc(emptied[0], 1)
                        if i >= 1:
                            hidden_lo(g, i - 1)
                    hidden_lo(g, 2 * GF - 1)
                    for i in range(16):
                        s = slice(i % 2 * HALF, i % 2 * HALF + HALF)
                        dve.wait_ge(bank_done, 24 * g + (b0 + 8 + i + 1))
                        V.tensor_tensor(X[:, i // 2, s], X[:, i // 2, s], bank[(b0 + i) % 4][:, :], ALU.add).then_inc(emptied[0], 1)
                        if last_group and i >= 1:
                            add_square(version, i - 1)
                            if version == MIX1 and i % 2 and i >= 3:
                                h_lo_tiles(H_MIX1, (i // 2 - 1,))
                with dve.Fori(0, GROUPS - 1) as g:
                    group(g, False)
                group(GROUPS - 1, True)
                add_square(version, 15)
                if version == MIX1:
                    h_lo_tiles(H_MIX1, (KT - 1,))

            def attention(layer, part):
                todo, s0 = steps(layer), STEP0[layer]

                def maxima(i):
                    kind, t, c = todo[i]
                    n = s0 + i
                    dve.wait_ge(score_done, n + 1)
                    st = stat[:, i % 4]
                    if kind == "mem":
                        link(V.tensor_reduce(st[:, 0, 0:2], pS[i % 4][:, :].rearrange("p (a m) -> p a m", a=2), AX.X, ALU.max))
                        V.tensor_scalar(st[:, 1, 0:2], st[:, 0, 0:2], -SCALE, None, ALU.mult).then_inc(max_ready, 1)
                    else:
                        j0, ps = int(c == 0), pS[i % 4]
                        if j0:
                            V.tensor_reduce(st[:, 0, 0:1], ps[:, 0:CHUNK].unsqueeze(1), AX.X, ALU.max)
                        link(V.tensor_reduce(st[:, 0, j0:4], ps[:, j0 * P:HALF].rearrange("p (j m) -> p j m", m=P), AX.X, ALU.max))
                        V.tensor_scalar(st[:, 1, :], st[:, 0, :], -SCALE, sp[:, 7, t:t + 1], ALU.mult, ALU.min).then_inc(max_ready, 1)

                def denominators(i):
                    kind, t, c = todo[i]
                    st, g = stat[:, i % 4], 2 if kind == "mem" else 4
                    dve.wait_ge(exp_done, s0 + i + 1)
                    if kind == "swa":
                        link(V.tensor_tensor(st[:, 2, :], st[:, 2, :], st[:, 3, :], ALU.add))
                    V.reciprocal(st[:, 4, 0:g], st[:, 2, 0:g]).then_inc(denom_ready, 1)

                def turned_lo_part(i):
                    dve.wait_ge(turned_hi, s0 + i + 1)
                    s = slice(PT + i % 3 * 512, PT + i % 3 * 512 + 512)
                    V.tensor_tensor(Hl[:, s], pT[i % 2][:, :], raw32(Hh[:, s]), ALU.subtract).then_inc(turned_split, 1)

                def take_out(i):
                    kind, t, c = todo[i]
                    dve.wait_ge(pv_done, s0 + i + 1)
                    for a in range(2):
                        ps = slice(64 * a, 64 * a + 64)
                        if kind == "mem":
                            last = V.tensor_copy(Q[ps, 6 + t, c * P:c * P + P], pO[i % 2][ps, a * P:a * P + P])
                        else:
                            last = V.tensor_copy(Q[ps, t, c * 256:c * 256 + 256].rearrange("p (j t) -> p j t", j=4),
                                                 head_part(pO[i % 2][ps, :], a))
                    last.then_inc(att_out, 1)

                if part == "start":
                    maxima(0)
                    maxima(1)
                    denominators(0)
                    return
                for i in range(len(todo)):
                    if i >= 1:
                        denominators(i)
                    if i + 2 < len(todo):
                        maxima(i + 2)
                    if i >= 1:
                        turned_lo_part(i - 1)
                    if i >= 2:
                        take_out(i - 2)
                    if layer and i == 3:
                        dve.wait_ge(bias_hi, 1)
                        V.scalar_tensor_tensor(Hl[:, BS:BS + 6 * P], XR[:, 0:6 * P], 1.0 / SCALE, raw32(Hh[:, BS:BS + 6 * P]),
                                               ALU.mult, ALU.subtract).then_inc(bias_split, 1)
                    if layer and i in (4, 5):
                        a = i - 4
                        dve.wait_ge(kv_split, 8)
                        src = slice(2 * S + a * 256, 2 * S + a * 256 + 7 * 256)
                        V.tensor_copy(Hl[64 * a:64 * a + 64, V2:V2 + 7 * 256], raw32(Rl[64 - 64 * a:128 - 64 * a, src])).then_inc(v2_made, 1)
                turned_lo_part(len(todo) - 1)
                take_out(len(todo) - 2)
                y_lo((H_Y0, H_Y1)[layer], range(2))
                take_out(len(todo) - 1)

            def decay_constants():
                dve.wait_ge(lam_exp, 1)
                link(V.tensor_scalar(sp[:, 0, :], sp[:, 1, :], 2.0, None, ALU.add))
                link(V.reciprocal(sp[:, 0, :], sp[:, 0, :]))
                link(V.tensor_tensor(sp[:, 2, :], sp[:, 1, :], sp[:, 0, :], ALU.mult))
                link(V.tensor_tensor(sp[:, 3, :], sp[:, 2, :], sp[:, 2, :], ALU.mult))
                link(V.memset(sp[:, 4, :], 1.0 / 17.0))
                for d in (15, 13, 11, 9, 7, 5, 3, 1):
                    link(V.tensor_tensor(sp[:, 4, :], sp[:, 4, :], sp[:, 3, :], ALU.mult))
                    link(V.tensor_scalar(sp[:, 4, :], sp[:, 4, :], 1.0 / d, None, ALU.add))
                link(V.tensor_tensor(sp[:, 4, :], sp[:, 4, :], sp[:, 2, :], ALU.mult))
                link(V.tensor_scalar(sp[:, 5, :], col[:, 7, :], -1.0, 0.0, ALU.mult, ALU.max))
                link(V.scalar_tensor_tensor(sp[:, 6, :], sp[:, 4, :], 2.0, sp[:, 5, :], ALU.mult, ALU.add))
                link(V.tensor_scalar(sp[:, 4, :], sp[:, 6, :], 2.0, None, ALU.mult))
                link(V.tensor_scalar(sp[:, 5, :], sp[:, 6, :], -4.0, None, ALU.mult))
                V.tensor_scalar(col[:, 5:7, :], col[:, 5:7, :], 0.5, None, ALU.mult).then_inc(sp_ready, 1)

            decay_constants()
            h_version(H_MIX0, MIX0)
            dve.wait_ge(toep_done, 1)
            link(V.tensor_scalar(sp[:, 7, :], sink[:, :], -1.0, None, ALU.mult))
            V.tensor_copy(toep, bank[7][0:12, 0:REL]).then_inc(toep_copied, 1)
            norm_finish(MIX0, memory_stats)
            memory_scale()
            dve.wait_ge(toep_written, 16)

            def decay_chain(j):
                th_x, root, a = tmp[:, 0, :], tmp[:, 1, :], tmp[:, 2, :]
                dve.wait_ge(decay_tanh, 2 * j + 2)
                link(V.scalar_tensor_tensor(a, a, 1.0, root, ALU.add, ALU.mult))
                V.tensor_scalar(a, a, -1.0, 1.0, ALU.mult, ALU.add).then_inc(decay_half, 1)
                link(V.scalar_tensor_tensor(th_x, th_x, 1.0, Q[:, j, :], ALU.add, ALU.mult))
                dve.wait_ge(decay_sqrt, j + 1)
                link(V.scalar_tensor_tensor(root, a, 1.0, root, ALU.add, ALU.mult))
                link(V.scalar_tensor_tensor(th_x, root, 0.5, th_x, ALU.mult, ALU.mult))
                V.tensor_tensor_scan(Q[:, j, :], a, th_x, 0.0, ALU.mult, ALU.add).then_inc(lru_done, 1)

            def conv_input(j, h):
                pb = evict(0, "xr", j, h)
                V.tensor_tensor(XR[:, 3 + h * HALF:3 + h * HALF + HALF], pb[:, :], rstd[:, h * HALF:h * HALF + HALF], ALU.mult).then_inc(emptied[0], 1)

            def conv_taps(j, h):
                s = slice(h * HALF, h * HALF + HALF)
                dve.wait_ge(conv_seeded, 2 * j + h + 1)
                for tap in range(3):
                    xs = XR[:, tap + h * HALF:tap + h * HALF + HALF]
                    ins = V.scalar_tensor_tensor(Q[:, j, s], xs, col[:, tap, j:j + 1], Q[:, j, s], ALU.mult, ALU.add)
                    if tap < 2:
                        link(ins)
                ins.then_inc(conv_ready, 1)

            def conv_lo(j, h):
                dve.wait_ge(conv_hi, 2 * j + h + 1)
                rs = slice((j % 3) * S + h * HALF, (j % 3) * S + h * HALF + HALF)
                V.tensor_tensor(Rl[:, rs], Q[:, j, h * HALF:h * HALF + HALF], raw32(Rh[:, rs]), ALU.subtract).then_inc(conv_split, 1)

            for kind, j in A_ORDER:
                if kind == "mem":
                    memory_kv_lo(0, (j,))
                if kind == "xr":
                    conv_input(j, 0)
                    if j == 0:
                        memory_lo(0)
                    conv_taps(j, 0)
                    conv_input(j, 1)
                    conv_lo(j, 0)
                    conv_taps(j, 1)
                    conv_lo(j, 1)
                if (kind, j) == ("gate", 5):
                    attention(0, "start")
                for h in range(2 if kind in ("qm", "gate") else 0):
                    s = slice(h * HALF, h * HALF + HALF)
                    pb = evict(0, kind, j, h)
                    if kind == "qm":
                        if j == 0 and h == 0:
                            dve.wait_ge(mem_written, 16)
                        V.tensor_tensor(Q[:, 6 + j, s], pb[:, :], rstd[:, s], ALU.mult).then_inc(emptied[0], 1)
                    else:
                        n = 2 * j + h
                        g, t = rx[:, 0, :], rx[:, 1, :]
                        V.tensor_tensor(g, pb[:, :], rstd[:, s], ALU.mult).then_inc(emptied[0], 1)
                        dve.wait_ge(gate_squared, n + 1)
                        V.scalar_tensor_tensor(t, t, 1.0 / GELU_A, g, ALU.add, ALU.mult).then_inc(gate_inner, 1)
                        dve.wait_ge(gate_tanh, n + 1)
                        link(V.scalar_tensor_tensor(t, t, 1.0, g, ALU.add, ALU.mult))
                        dve.wait_ge(lru_done, j + 1)
                        V.scalar_tensor_tensor(Q[:, j, s], t, 0.5, Q[:, j, s], ALU.mult, ALU.mult).then_inc(y_done, 1)
                        dve.wait_ge(y_done, n + 1)
                if kind == "G":
                    decay_chain(j)
            attention(0, "steps")
            y_lo(H_Y0, range(2, KT))
            wout(0)
            norm_finish(MLP0)
            mlp(0)
            norm_finish(MIX1)

            def queries(kind, i, tile):
                for h in range(2):
                    s = slice(h * HALF, h * HALF + HALF)
                    pb = evict(1, kind, i, h)
                    V.tensor_tensor(Q[:, tile, s], pb[:, :], rstd[:, s], ALU.mult).then_inc(emptied[0], 1)
            for kind, i in B_ORDER[:12]:
                if kind == "mem":
                    memory_kv_lo(1, (i,))
                else:
                    if (kind, i) == ("qm", 1):
                        h_lo_tiles(H_KV, range(KT - 1))
                    queries(kind, i, i if kind == "q" else 6 + i)
                if (kind, i) == ("q", 0):
                    memory_lo(1)
            h_lo_tiles(H_KV, (KT - 1,))
            for i in range(9):
                if i == 5:
                    attention(1, "start")
                if i < 8:
                    b = BANK[1, "K", 0] + i
                    t = tmp[:, 2, i % 2 * HALF:i % 2 * HALF + HALF]
                    dve.wait_ge(bank_done, b + 1)
                    if i >= 2:
                        dve.wait_ge(kv_split, i - 1)
                    if i < 4:
                        V.tensor_tensor(t, bank[b % 4][:, :], rstd[:, i % 2 * HALF:i % 2 * HALF + HALF], ALU.mult).then_inc(emptied[0], 1)
                    else:
                        V.tensor_tensor(t.rearrange("p (a d) -> p a d", a=2), bank[b % 4][:, :].rearrange("p (a d) -> p a d", a=2),
                                        nrm[:, 4, 2 * i - 8:2 * i - 6].unsqueeze(2).to_broadcast([P, 2, 256]), ALU.mult).then_inc(emptied[0], 1)
                if i >= 1:
                    s = slice((i - 1) * HALF, i * HALF)
                    dve.wait_ge(kv_hi, i)
                    V.tensor_tensor(Rl[:, s], tmp[:, 2, (i - 1) % 2 * HALF:(i - 1) % 2 * HALF + HALF], raw32(Rh[:, s]), ALU.subtract).then_inc(kv_split, 1)
            attention(1, "steps")
            y_lo(H_Y1, range(2, KT))
            wout(1)
            norm_finish(MLP1)
            mlp(1)
            norm_finish(FINAL)


def _buckets():
    n = -(np.arange(REL) - (2 * CHUNK - 1))
    half, exact = 16, 8
    out = (n < 0).astype(np.int32) * half
    n = np.abs(n)
    large = exact + (np.log(np.maximum(n, 1) / exact) / np.log(128 / exact) * (half - exact)).astype(np.int32)
    return out + np.where(n < exact, n, np.minimum(large, half - 1))


def _columns(w, tiles=None):
    k, n = w.shape
    return np.ascontiguousarray(w.reshape(k // P, P, n // P, P).transpose(2, 1, 0, 3)).reshape(n // P, P, k)


def _units(x):
    parts = {}
    heads = np.concatenate([np.arange(h * HEAD, h * HEAD + HEAD) for pair in PAIRS for h in pair])
    out_rows = np.concatenate([heads, np.arange(LRU, D)])
    a_in = _columns(x["a_w_in"][0])
    b_in = _columns(np.concatenate([x["b_w_in"][0][:, heads], x["b_w_in"][0][:, LRU:]], axis=1))

    def rows(w):
        return w.reshape(2, 4, P, 256).transpose(0, 2, 1, 3).reshape(2, P, 1024)
    for i in range(6):
        parts[0, "gate", i], parts[0, "xr", i], parts[1, "q", i] = a_in[i], a_in[6 + i], b_in[i]
        unit = np.zeros((P, 8, P), np.float32)
        ks = GATE_K[i % 3]
        for which, name in enumerate(("a_gx_w", "a_ga_w")):
            for n, k in enumerate(ks):
                r0, c0 = (i - i % 3 + k) * P, i * P
                for blk in range(8):
                    lo, hi = blk * GB, blk * GB + GB
                    ra, rb, ca, cb = max(lo, r0), min(hi, r0 + P), max(lo, c0), min(hi, c0 + P)
                    if ra < rb and ca < cb:
                        unit[ra - r0:rb - r0, which * len(ks) + n, ca - c0:cb - c0] = x[name][0, blk, ra - lo:rb - lo, ca - lo:cb - lo]
        parts[0, "G", i] = unit.reshape(P, 1024)
    for i in range(2):
        parts[0, "qm", i], parts[1, "qm", i] = a_in[12 + i], b_in[6 + i]
    kv = x["w_kv_shared"]
    k_units, v_units = _columns(kv[:, :256]), rows(kv[:, 256:])
    for i in range(2):
        parts[1, "K", i], parts[1, "V", i] = k_units[i], v_units[i]
    for layer in range(2):
        m = x["w_mem_kv"][layer]
        mk, mv = _columns(m[:, :256]), rows(m[:, 256:])
        wo = _columns(x["w_out"][layer][out_rows] if layer else x["w_out"][layer])
        w1 = _columns(x["w1"][layer])
        w2 = x["w2"][layer].reshape(GROUPS, GF, P, 4, 2, P).transpose(0, 3, 2, 4, 1, 5).reshape(4 * GROUPS, P, 1024)
        for i in range(2):
            parts[layer, "mem", i], parts[layer, "mem", 2 + i] = mk[i], mv[i]
        for i in range(8):
            parts[layer, "wout", i] = wo[i]
        for i in range(32):
            parts[layer, "w1", i], parts[layer, "w2", i] = w1[i], w2[i]
    return np.stack([parts[key] for key in ORDER])


def _tiles(v, n):
    return v.reshape(n, P).T


def kernel(**inputs):
    import concourse.bacc as bacc
    from concourse.bass_utils import run_bass_kernel_spmd

    x = {k: np.asarray(v) for k, v in inputs.items()}
    gains = [x["mem_norm_g"], x["mix_norm_g"][0], x["mix_norm_g"][1], x["mlp_norm_g"][0], x["mlp_norm_g"][1], x["kv_norm_g"], x["final_norm_g"]]
    cols = [*x["a_conv_w"][0], x["a_conv_b"][0], x["a_gx_b"][0], x["a_ga_b"][0], x["a_lambda"][0]]
    onehot = (_buckets()[None, :] == np.arange(32)[:, None]).astype(np.float32)
    arrays = {
        "xT": x["x"][0].T.reshape(KT, P, S).transpose(1, 0, 2),
        "memT": x["mem"][0].T.reshape(KT, P, MEM).transpose(1, 0, 2).reshape(P, KT * MEM),
        "gains": np.stack([_tiles(g, KT) for g in gains], axis=1),
        "cols": np.stack([_tiles(c, LT) for c in cols], axis=1),
        "sinkc": np.repeat(x["b_sinks"][0][np.array(PAIRS)].T, CHUNK, axis=0),
        "relb": x["rel_bias"],
        "onehot": onehot,
        "wst": _units(x),
    }
    nc = bacc.Bacc("TRN2", target_bir_lowering=False, num_devices=1, dynamic_dma_scratch_size=1024)
    f32 = mybir.dt.float32
    arrays = {k: np.ascontiguousarray(v) for k, v in arrays.items()}
    aps = {k: nc.dram_tensor(k, v.shape, f32, kind="ExternalInput").ap() for k, v in arrays.items()}
    memn = nc.dram_tensor("memn", (P, KT * MEM), f32).ap()
    rep = nc.dram_tensor("rep", (12 * CHUNK * REL,), f32).ap()
    outT = nc.dram_tensor("outT", (P, KT, S), f32, kind="ExternalOutput").ap()
    trunk(nc, rep=rep, memn=memn, outT=outT, **aps)
    r = run_bass_kernel_spmd(nc, [arrays], core_ids=[0])
    return np.ascontiguousarray(r.results[0]["outT"].transpose(1, 0, 2).reshape(D, S).T)[None]
```
